# Optimizing a Trainium2 kernel written in Bass

```python
import math
import jax, jax.numpy as jnp
from jax import lax
import numpy as np

D_MODEL = 1024
BATCH = 1
SEQ = 256
DEPTH = 1

PLE_DIM = 256
D_POOL = 512
POOL_WINDOWS = (2, 4, 8, 16)
N_POOL_GROUPS = len(POOL_WINDOWS)
POOL_GROUP = D_POOL // N_POOL_GROUPS
D_ATTN = D_MODEL - D_POOL
N_HEADS = 8
HEAD_DIM = D_ATTN // N_HEADS
MOBA_BLOCK = 256
MOBA_TOPK = 3
Q_CHUNK = 32
NUM_BUCKETS = 32
MAX_DISTANCE = 128
D_FF = 2816
CONV_WIDTH = 3
EPS = 1e-6
D_IN = D_POOL + 3 * D_ATTN


def rms_norm(x, g):
    xf = x.astype(jnp.float32)
    y = xf * lax.rsqrt(jnp.mean(xf * xf, axis=-1, keepdims=True) + EPS)
    return (y * g.astype(jnp.float32)).astype(x.dtype)

def pool_mixer(u, w_pool, pool_scale):
    B, S, _ = u.shape
    uf = u.astype(jnp.float32)
    cpad = jnp.pad(jnp.cumsum(uf, axis=1), ((0, 0), (1, 0), (0, 0)))
    pos = jnp.arange(S)
    outs = []
    for g, w in enumerate(POOL_WINDOWS):
        c_g = cpad[:, :, g * POOL_GROUP:(g + 1) * POOL_GROUP]
        lagged = jnp.pad(c_g[:, :S + 1 - w], ((0, 0), (w - 1, 0), (0, 0)))
        count = jnp.minimum(pos + 1, w).astype(jnp.float32)[None, :, None]
        mean = (c_g[:, 1:] - lagged) / count
        outs.append(mean - uf[:, :, g * POOL_GROUP:(g + 1) * POOL_GROUP])
    pooled = jnp.stack(outs, axis=2)
    mixed = jnp.einsum('bsgc,gcd->bsgd', pooled, w_pool.astype(jnp.float32))
    return (mixed.reshape(B, S, D_POOL) * pool_scale.astype(jnp.float32)).astype(u.dtype)

def rel_bucket(dist):
    n = jnp.maximum(dist, 0)
    max_exact = NUM_BUCKETS // 2
    nf = jnp.maximum(n, 1).astype(jnp.float32)
    large = max_exact + (jnp.log(nf / max_exact) / math.log(MAX_DISTANCE / max_exact)
                         * (NUM_BUCKETS - max_exact)).astype(jnp.int32)
    large = jnp.minimum(large, NUM_BUCKETS - 1)
    return jnp.where(n < max_exact, n, large)

def moba_attention(q, k, v, rel_bias):
    B, S = q.shape[0], q.shape[1]
    nb = -(-S // MOBA_BLOCK)
    s_pad = nb * MOBA_BLOCK
    pad = ((0, 0), (0, s_pad - S), (0, 0), (0, 0))
    q, k, v = [jnp.pad(t, pad).transpose(0, 2, 1, 3) for t in (q, k, v)]
    k_blk = k.reshape(B, N_HEADS, nb, MOBA_BLOCK, HEAD_DIM)
    v_blk = v.reshape(B, N_HEADS, nb, MOBA_BLOCK, HEAD_DIM)
    k_mean = jnp.mean(k_blk.astype(jnp.float32), axis=3)
    gate = jnp.einsum('bhsd,bhnd->bhsn', q.astype(jnp.float32), k_mean)
    q_blk_idx = jnp.arange(s_pad) // MOBA_BLOCK
    past = jnp.arange(nb)[None, :] < q_blk_idx[:, None]
    gate = jnp.where(past, gate, -jnp.inf)
    n_sel = min(MOBA_TOPK, nb)
    _, sel = lax.top_k(gate, n_sel)
    sel_valid = sel < q_blk_idx[:, None]

    scale = HEAD_DIM ** -0.5
    bias_t = rel_bias.astype(jnp.float32).T
    b_idx = jnp.arange(B)[:, None, None, None]
    h_idx = jnp.arange(N_HEADS)[None, :, None, None]
    key_off = jnp.arange(MOBA_BLOCK)
    n_sel_keys = n_sel * MOBA_BLOCK

    def chunk(ci):
        start = ci * Q_CHUNK
        qc = lax.dynamic_slice_in_dim(q, start, Q_CHUNK, axis=2)
        sc = lax.dynamic_slice_in_dim(sel, start, Q_CHUNK, axis=2)
        vc = lax.dynamic_slice_in_dim(sel_valid, start, Q_CHUNK, axis=2)
        t = start + jnp.arange(Q_CHUNK)
        j = start // MOBA_BLOCK
        k_sel = k_blk[b_idx, h_idx, sc]
        v_sel = v_blk[b_idx, h_idx, sc]
        key_pos = sc[..., None] * MOBA_BLOCK + key_off
        bias_sel = bias_t[h_idx[..., None], rel_bucket(t[:, None, None] - key_pos)]
        l_sel = jnp.einsum('bhqd,bhqnkd->bhqnk', qc, k_sel).astype(jnp.float32) * scale + bias_sel
        l_sel = jnp.where(vc[..., None], l_sel, -jnp.inf)
        k_own = lax.dynamic_index_in_dim(k_blk, j, axis=2, keepdims=False)
        v_own = lax.dynamic_index_in_dim(v_blk, j, axis=2, keepdims=False)
        d_own = t[:, None] - (j * MOBA_BLOCK + key_off)[None, :]
        bias_own = bias_t[:, rel_bucket(d_own)]
        l_own = jnp.einsum('bhqd,bhkd->bhqk', qc, k_own).astype(jnp.float32) * scale + bias_own
        l_own = jnp.where(d_own >= 0, l_own, -jnp.inf)
        logits = jnp.concatenate([l_sel.reshape(B, N_HEADS, Q_CHUNK, n_sel_keys), l_own], axis=-1)
        probs = jax.nn.softmax(logits, axis=-1).astype(v.dtype)
        p_sel = probs[..., :n_sel_keys].reshape(B, N_HEADS, Q_CHUNK, n_sel, MOBA_BLOCK)
        p_own = probs[..., n_sel_keys:]
        return (jnp.einsum('bhqnk,bhqnkd->bhqd', p_sel, v_sel)
                + jnp.einsum('bhqk,bhkd->bhqd', p_own, v_own))

    outs = lax.map(chunk, jnp.arange(s_pad // Q_CHUNK))
    out = outs.transpose(1, 0, 3, 2, 4).reshape(B, s_pad, N_HEADS, HEAD_DIM)[:, :S]
    return out.reshape(B, S, D_ATTN)

def conv_ffn(h, w_up, conv_w, conv_b, w_down):
    S = h.shape[1]
    gate, val = jnp.split(h @ w_up, 2, axis=-1)
    gp = jnp.pad(gate, ((0, 0), (CONV_WIDTH - 1, 0), (0, 0)))
    conv = conv_b + gp[:, 0:S] * conv_w[0]
    for kk in range(1, CONV_WIDTH):
        conv = conv + gp[:, kk:kk + S] * conv_w[kk]
    return (jax.nn.gelu(conv, approximate=True) * val) @ w_down

def first_inputs(seed: int = 0) -> dict:
    key = jax.random.key(seed)
    ks = jax.random.split(key, 20)
    f32 = jnp.float32
    nrm = lambda k, shape, s: jax.random.normal(k, shape, f32) * s
    gain = lambda k: 1.0 + nrm(k, (DEPTH, D_MODEL), 0.05)
    return {
        "x": nrm(ks[0], (BATCH, SEQ, D_MODEL), 1.0),
        "p": nrm(ks[1], (DEPTH, BATCH, SEQ, PLE_DIM), 1.0),
        "rel_bias": nrm(ks[2], (NUM_BUCKETS, N_HEADS), 0.5),
        "g_mix_pre": gain(ks[3]),
        "g_mix_post": gain(ks[4]),
        "g_ffn_pre": gain(ks[5]),
        "g_ffn_post": gain(ks[6]),
        "w_in": nrm(ks[7], (DEPTH, D_MODEL, D_IN), D_MODEL ** -0.5),
        "w_pool": nrm(ks[8], (DEPTH, N_POOL_GROUPS, POOL_GROUP, POOL_GROUP), POOL_GROUP ** -0.5),
        "pool_scale": 1.0 + nrm(ks[9], (DEPTH, D_POOL), 0.1),
        "w_out": nrm(ks[10], (DEPTH, D_MODEL, D_MODEL), D_MODEL ** -0.5),
        "w_up": nrm(ks[11], (DEPTH, D_MODEL, 2 * D_FF), D_MODEL ** -0.5),
        "conv_w": nrm(ks[12], (DEPTH, CONV_WIDTH, D_FF), CONV_WIDTH ** -0.5),
        "conv_b": nrm(ks[13], (DEPTH, D_FF), 0.02),
        "w_down": nrm(ks[14], (DEPTH, D_FF, D_MODEL), D_FF ** -0.5),
        "w_ple": nrm(ks[15], (DEPTH, PLE_DIM, D_MODEL), PLE_DIM ** -0.5),
        "w_ple_gate": nrm(ks[16], (DEPTH, D_MODEL, D_MODEL), D_MODEL ** -0.5),
    }

def first_block(x, p, rel_bias, g_mix_pre, g_mix_post, g_ffn_pre, g_ffn_post, w_in, w_pool,
              pool_scale, w_out, w_up, conv_w, conv_b, w_down, w_ple, w_ple_gate):
    B, S, _ = x.shape
    for i in range(DEPTH):
        h = rms_norm(x, g_mix_pre[i])
        proj = h @ w_in[i]
        u, q, k, v = jnp.split(proj, [D_POOL, D_POOL + D_ATTN, D_POOL + 2 * D_ATTN], axis=-1)
        y_pool = pool_mixer(u, w_pool[i], pool_scale[i])
        y_attn = moba_attention(q.reshape(B, S, N_HEADS, HEAD_DIM),
                                k.reshape(B, S, N_HEADS, HEAD_DIM),
                                v.reshape(B, S, N_HEADS, HEAD_DIM), rel_bias)
        y = jnp.concatenate([y_pool, y_attn], axis=-1) @ w_out[i]
        x = x + rms_norm(y, g_mix_post[i])
        h = rms_norm(x, g_ffn_pre[i])
        x = x + rms_norm(conv_ffn(h, w_up[i], conv_w[i], conv_b[i], w_down[i]), g_ffn_post[i])
        x = x + (p[i] @ w_ple[i]) * jax.nn.sigmoid(x @ w_ple_gate[i])
    return x


DEPTH_2 = 2

N_MEM = 256
N_MIXERS = 3
HEAD_DIM_2 = 64
MIX_HEADS = 12
MIX_WIDTH = MIX_HEADS * HEAD_DIM_2
XA_HEADS = 4
XA_WIDTH = XA_HEADS * HEAD_DIM_2
OUT_IN = MIX_WIDTH + XA_WIDTH
ROPE_THETA = 500000.0
ROT_DIM = HEAD_DIM_2 // 4
LN_EPS = 1e-5
RMS_EPS = 1e-6
DEEPNORM_ALPHA = (2.0 * DEPTH_2) ** 0.25
DEEPNORM_BETA = (8.0 * DEPTH_2) ** -0.25

NSA_KV_HEADS = 4
NSA_GROUP = MIX_HEADS // NSA_KV_HEADS
NSA_KV_WIDTH = NSA_KV_HEADS * HEAD_DIM_2
CMP_LEN = 32
CMP_STRIDE = 16
CMP_HIDDEN = 128
SEL_BLOCK = 64
SEL_TOPK = 16
WINDOW = 512
NSA_QBLOCK = 32
NSA_IN = MIX_WIDTH + 6 * NSA_KV_WIDTH + 3 * MIX_HEADS + XA_WIDTH

MLA_Q_RANK = 256
MLA_KV_RANK = 128
MLA_NOPE = 64
MLA_ROPE = 32
MLA_V = 64
MLA_THETA = 10000.0
MLA_QBLOCK = 128
MLA_IN = MLA_Q_RANK + MLA_KV_RANK + MLA_ROPE + XA_WIDTH

CONV_CH = MIX_WIDTH
CONV_WIDTH_2 = 31
CONV_IN = 2 * CONV_CH + XA_WIDTH

N_GROUPS = 4
EXPERTS_PER_GROUP = 4
N_EXPERTS = N_GROUPS * EXPERTS_PER_GROUP
EXPERT_FF = 512
TOPK_IN_GROUP = 2


def layer_norm(x, g, b):
    xf = x.astype(jnp.float32)
    mu = jnp.mean(xf, -1, keepdims=True)
    var = jnp.mean(jnp.square(xf - mu), -1, keepdims=True)
    y = (xf - mu) * lax.rsqrt(var + LN_EPS) * g.astype(jnp.float32) + b.astype(jnp.float32)
    return y.astype(x.dtype)

def rms_norm_2(x, g):
    xf = x.astype(jnp.float32)
    y = xf * lax.rsqrt(jnp.mean(xf * xf, -1, keepdims=True) + RMS_EPS) * g.astype(jnp.float32)
    return y.astype(x.dtype)

def rope_tables(positions, dim, theta):
    inv = theta ** (-jnp.arange(0, dim, 2, dtype=jnp.float32) / dim)
    ang = positions.astype(jnp.float32)[..., None] * inv
    return jnp.cos(ang), jnp.sin(ang)

def apply_rope(x, cos, sin):
    r = cos.shape[-1]
    x1, x2 = x[..., :r], x[..., r:]
    c, s = cos[:, :, None, :], sin[:, :, None, :]
    return jnp.concatenate([x1 * c - x2 * s, x1 * s + x2 * c], -1).astype(x.dtype)

def partial_rope(x, cos, sin):
    return jnp.concatenate([apply_rope(x[..., :ROT_DIM], cos, sin), x[..., ROT_DIM:]], -1)

def masked_softmax(s, mask):
    s = jnp.where(mask, s.astype(jnp.float32), -jnp.inf)
    m = jnp.max(s, -1, keepdims=True)
    m = jnp.where(jnp.isfinite(m), m, 0.0)
    e = jnp.where(mask, jnp.exp(s - m), 0.0)
    return e / jnp.maximum(jnp.sum(e, -1, keepdims=True), 1e-30)

def nsa_mixer(mix_cols, cmp_pe, cmp_w1, cmp_w2, cos_n, sin_n):
    B, S, _ = mix_cols.shape
    H, K, G, Dh = MIX_HEADS, NSA_KV_HEADS, NSA_GROUP, HEAD_DIM_2
    offs = np.cumsum([MIX_WIDTH] + [NSA_KV_WIDTH] * 6).tolist()
    q, kc, vc, ks, vs, kw, vw, gate_logits = jnp.split(mix_cols, offs, axis=-1)
    dt = mix_cols.dtype
    q = partial_rope(q.reshape(B, S, H, Dh), cos_n, sin_n)
    ks = partial_rope(ks.reshape(B, S, K, Dh), cos_n, sin_n)
    kw = partial_rope(kw.reshape(B, S, K, Dh), cos_n, sin_n)
    vs, vw = vs.reshape(B, S, K, Dh), vw.reshape(B, S, K, Dh)
    kc, vc = kc.reshape(B, S, K, Dh), vc.reshape(B, S, K, Dh)
    gates = jax.nn.sigmoid(gate_logits.astype(jnp.float32)).astype(dt).reshape(B, S, H, 3)

    n_cmp = (S - CMP_LEN) // CMP_STRIDE + 1
    starts = np.arange(n_cmp) * CMP_STRIDE
    tok_idx = starts[:, None] + np.arange(CMP_LEN)[None, :]
    end_idx = starts + CMP_LEN - 1

    def compress(t, pe, w1, w2):
        blk = t[:, tok_idx] + pe[None, None, :, None, :]
        blk = blk.transpose(0, 1, 3, 2, 4).reshape(B, n_cmp, K, CMP_LEN * Dh)
        return jax.nn.silu(blk @ w1) @ w2

    k_cmp = compress(kc, cmp_pe[0], cmp_w1[0], cmp_w2[0])
    v_cmp = compress(vc, cmp_pe[1], cmp_w1[1], cmp_w2[1])
    k_cmp = partial_rope(k_cmp, cos_n[:, end_idx], sin_n[:, end_idx])

    n_sel = S // SEL_BLOCK
    top_n = min(SEL_TOPK, n_sel)
    sel_start = np.arange(n_sel) * SEL_BLOCK
    overlap = ((starts[:, None] < sel_start[None, :] + SEL_BLOCK)
               & (starts[:, None] + CMP_LEN > sel_start[None, :])).astype(np.float32)
    overlap = jnp.asarray(overlap)
    ksb = ks.reshape(B, n_sel, SEL_BLOCK, K, Dh).transpose(0, 3, 1, 2, 4)
    vsb = vs.reshape(B, n_sel, SEL_BLOCK, K, Dh).transpose(0, 3, 1, 2, 4)
    kwp = jnp.pad(kw, ((0, 0), (WINDOW, 0), (0, 0), (0, 0)))
    vwp = jnp.pad(vw, ((0, 0), (WINDOW, 0), (0, 0), (0, 0)))
    qg = q.reshape(B, S, K, G, Dh)
    scale = 1.0 / math.sqrt(Dh)
    C = NSA_QBLOCK
    bi = jnp.arange(B)[:, None, None, None]
    ki = jnp.arange(K)[None, :, None, None]
    blk_id = jnp.arange(n_sel)

    def block(i):
        t0 = i * C
        qb = lax.dynamic_slice_in_dim(qg, t0, C, axis=1)
        t = t0 + jnp.arange(C)
        s_c = jnp.einsum('bckgd,bnkd->bkgcn', qb, k_cmp) * scale
        p_c = masked_softmax(s_c, end_idx[None, :] <= t[:, None])
        o_c = jnp.einsum('bkgcn,bnkd->bckgd', p_c.astype(dt), v_cmp)
        imp = jnp.einsum('bkgcn,nj->bkcj', p_c, overlap)
        cur = t // SEL_BLOCK
        valid = blk_id[None, :] <= cur[:, None]
        forced = (blk_id[None, :] == 0) | (blk_id[None, :] == cur[:, None]) | (blk_id[None, :] == cur[:, None] - 1)
        imp = jnp.where(valid & forced, jnp.inf, jnp.where(valid, imp, -jnp.inf))
        _, sel = lax.top_k(imp, top_n)
        k_sel = ksb[bi, ki, sel]
        v_sel = vsb[bi, ki, sel]
        s_s = jnp.einsum('bckgd,bkcnld->bkgcnl', qb, k_sel) * scale
        key_pos = sel[..., None] * SEL_BLOCK + jnp.arange(SEL_BLOCK)
        mask_s = (key_pos <= t[None, None, :, None, None]).reshape(B, K, 1, C, top_n * SEL_BLOCK)
        p_s = masked_softmax(s_s.reshape(B, K, G, C, top_n * SEL_BLOCK), mask_s)
        o_s = jnp.einsum('bkgcm,bkcmd->bckgd', p_s.astype(dt),
                         v_sel.reshape(B, K, C, top_n * SEL_BLOCK, Dh))
        kwb = lax.dynamic_slice_in_dim(kwp, t0, WINDOW + C, axis=1)
        vwb = lax.dynamic_slice_in_dim(vwp, t0, WINDOW + C, axis=1)
        s_w = jnp.einsum('bckgd,bjkd->bkgcj', qb, kwb) * scale
        kp = t0 - WINDOW + jnp.arange(WINDOW + C)
        diff = t[:, None] - kp[None, :]
        p_w = masked_softmax(s_w, (diff >= 0) & (diff < WINDOW) & (kp[None, :] >= 0))
        o_w = jnp.einsum('bkgcj,bjkd->bckgd', p_w.astype(dt), vwb)
        gb = lax.dynamic_slice_in_dim(gates, t0, C, axis=1).reshape(B, C, K, G, 3)
        o = gb[..., 0:1] * o_c + gb[..., 1:2] * o_s + gb[..., 2:3] * o_w
        return o.reshape(B, C, H * Dh)

    out = lax.map(block, jnp.arange(S // C))
    return out.transpose(1, 0, 2, 3).reshape(B, S, MIX_WIDTH)

def mla_mixer(mix_cols, q_norm, w_uq, kv_norm, w_ukv, cos_m, sin_m):
    B, S, _ = mix_cols.shape
    H = MIX_HEADS
    dt = mix_cols.dtype
    c_q = mix_cols[..., :MLA_Q_RANK]
    c_kv = mix_cols[..., MLA_Q_RANK:MLA_Q_RANK + MLA_KV_RANK]
    k_rope = mix_cols[..., MLA_Q_RANK + MLA_KV_RANK:]
    q = (rms_norm_2(c_q, q_norm) @ w_uq).reshape(B, S, H, MLA_NOPE + MLA_ROPE)
    q = jnp.concatenate([q[..., :MLA_NOPE], apply_rope(q[..., MLA_NOPE:], cos_m, sin_m)], -1)
    kv = (rms_norm_2(c_kv, kv_norm) @ w_ukv).reshape(B, S, H, MLA_NOPE + MLA_V)
    k_nope, v = kv[..., :MLA_NOPE], kv[..., MLA_NOPE:]
    k_rope = apply_rope(k_rope[:, :, None, :], cos_m, sin_m)
    k = jnp.concatenate([k_nope, jnp.broadcast_to(k_rope, (B, S, H, MLA_ROPE))], -1)
    scale = 1.0 / math.sqrt(MLA_NOPE + MLA_ROPE)
    key_idx = jnp.arange(S)

    def block(i):
        t0 = i * MLA_QBLOCK
        qb = lax.dynamic_slice_in_dim(q, t0, MLA_QBLOCK, axis=1)
        s = jnp.einsum('bqhd,bkhd->bhqk', qb, k) * scale
        mask = (t0 + jnp.arange(MLA_QBLOCK))[:, None] >= key_idx[None, :]
        p = masked_softmax(s, mask)
        return jnp.einsum('bhqk,bkhd->bqhd', p.astype(dt), v).reshape(B, MLA_QBLOCK, H * MLA_V)

    out = lax.map(block, jnp.arange(S // MLA_QBLOCK))
    return out.transpose(1, 0, 2, 3).reshape(B, S, H * MLA_V)

def conv_mixer(mix_cols, b_in, dw_w, dw_b, ln_g, ln_b):
    a = mix_cols + b_in
    u = a[..., :CONV_CH] * jax.nn.sigmoid(a[..., CONV_CH:])
    y = lax.conv_general_dilated(u, dw_w[:, None, :], window_strides=(1,),
                                 padding=[(CONV_WIDTH_2 - 1, 0)],
                                 dimension_numbers=('NWC', 'WIO', 'NWC'),
                                 feature_group_count=CONV_CH) + dw_b
    return jax.nn.silu(layer_norm(y, ln_g, ln_b))

def memory_cross_attention(q, mem_k, mem_v):
    s = jnp.einsum('bshd,bmhd->bhsm', q, mem_k) * (1.0 / math.sqrt(HEAD_DIM_2))
    p = jax.nn.softmax(s.astype(jnp.float32), -1).astype(q.dtype)
    return jnp.einsum('bhsm,bmhd->bshd', p, mem_v)

def hier_moe(x, w_grp, b_grp, w_exp, b_exp, w_gate, w_up, w_down):
    def per_seq(xs):
        S = xs.shape[0]
        pg = jax.nn.softmax((xs @ w_grp + b_grp).astype(jnp.float32), -1)
        g_sel = jnp.argmax(pg, -1)
        g_prob = jnp.max(pg, -1)
        le = (xs @ w_exp + b_exp).astype(jnp.float32).reshape(S, N_GROUPS, EXPERTS_PER_GROUP)
        le = le[jnp.arange(S), g_sel]
        pe = jax.nn.softmax(le, -1)
        top_p, top_i = lax.top_k(pe, TOPK_IN_GROUP)
        top_p = top_p / jnp.sum(top_p, -1, keepdims=True)
        eid = g_sel[:, None] * EXPERTS_PER_GROUP + top_i
        gate = jnp.sum(jax.nn.one_hot(eid, N_EXPERTS, dtype=jnp.float32)
                       * (g_prob[:, None] * top_p)[..., None], axis=1)
        hdn = jax.nn.silu(jnp.einsum('sd,edf->sef', xs, w_gate)) * jnp.einsum('sd,edf->sef', xs, w_up)
        hdn = hdn * gate[..., None].astype(hdn.dtype)
        return jnp.einsum('sef,efd->sd', hdn, w_down)
    return lax.map(per_seq, x)

def second_inputs(seed: int = 0) -> dict:
    key = jax.random.key(seed)
    ks = iter(jax.random.split(key, 40))
    nA = len(range(0, DEPTH_2, N_MIXERS))
    nB = len(range(1, DEPTH_2, N_MIXERS))
    nC = len(range(2, DEPTH_2, N_MIXERS))
    f32 = jnp.float32

    def nrm(shape, scale):
        return jax.random.normal(next(ks), shape, f32) * scale

    def gain(shape):
        return 1.0 + nrm(shape, 0.02)

    positions = (jax.random.randint(next(ks), (BATCH, 1), 0, 2048, dtype=jnp.int32)
                 + jnp.arange(SEQ, dtype=jnp.int32)[None, :])
    return {
        'x': nrm((BATCH, SEQ, D_MODEL), 1.0),
        'mem': nrm((BATCH, N_MEM, D_MODEL), 1.0),
        'positions': positions,
        'nsa_w_in': nrm((nA, D_MODEL, NSA_IN), D_MODEL ** -0.5),
        'nsa_cmp_pe': nrm((nA, 2, CMP_LEN, HEAD_DIM_2), 0.1),
        'nsa_cmp_w1': nrm((nA, 2, CMP_LEN * HEAD_DIM_2, CMP_HIDDEN), (CMP_LEN * HEAD_DIM_2) ** -0.5),
        'nsa_cmp_w2': nrm((nA, 2, CMP_HIDDEN, HEAD_DIM_2), CMP_HIDDEN ** -0.5),
        'mla_w_in': nrm((nB, D_MODEL, MLA_IN), D_MODEL ** -0.5),
        'mla_q_norm': gain((nB, MLA_Q_RANK)),
        'mla_w_uq': nrm((nB, MLA_Q_RANK, MIX_HEADS * (MLA_NOPE + MLA_ROPE)), MLA_Q_RANK ** -0.5),
        'mla_kv_norm': gain((nB, MLA_KV_RANK)),
        'mla_w_ukv': nrm((nB, MLA_KV_RANK, MIX_HEADS * (MLA_NOPE + MLA_V)), MLA_KV_RANK ** -0.5),
        'conv_w_in': nrm((nC, D_MODEL, CONV_IN), D_MODEL ** -0.5),
        'conv_b_in': nrm((nC, 2 * CONV_CH), 0.02),
        'conv_dw_w': nrm((nC, CONV_WIDTH_2, CONV_CH), CONV_WIDTH_2 ** -0.5),
        'conv_dw_b': nrm((nC, CONV_CH), 0.02),
        'conv_ln_g': gain((nC, CONV_CH)),
        'conv_ln_b': nrm((nC, CONV_CH), 0.02),
        'mem_w_kv': nrm((DEPTH_2, D_MODEL, 2 * XA_WIDTH), D_MODEL ** -0.5),
        'w_out': nrm((DEPTH_2, OUT_IN, D_MODEL), OUT_IN ** -0.5 * DEEPNORM_BETA),
        'ln_g': gain((DEPTH_2, 2, D_MODEL)),
        'ln_b': nrm((DEPTH_2, 2, D_MODEL), 0.02),
        'moe_w_grp': nrm((DEPTH_2, D_MODEL, N_GROUPS), D_MODEL ** -0.5),
        'moe_b_grp': nrm((DEPTH_2, N_GROUPS), 0.01),
        'moe_w_exp': nrm((DEPTH_2, D_MODEL, N_EXPERTS), D_MODEL ** -0.5),
        'moe_b_exp': nrm((DEPTH_2, N_EXPERTS), 0.01),
        'moe_w_gate': nrm((DEPTH_2, N_EXPERTS, D_MODEL, EXPERT_FF), D_MODEL ** -0.5),
        'moe_w_up': nrm((DEPTH_2, N_EXPERTS, D_MODEL, EXPERT_FF), D_MODEL ** -0.5),
        'moe_w_down': nrm((DEPTH_2, N_EXPERTS, EXPERT_FF, D_MODEL), EXPERT_FF ** -0.5 * DEEPNORM_BETA),
    }

def second_block(x, mem, positions, nsa_w_in, nsa_cmp_pe, nsa_cmp_w1, nsa_cmp_w2,
              mla_w_in, mla_q_norm, mla_w_uq, mla_kv_norm, mla_w_ukv,
              conv_w_in, conv_b_in, conv_dw_w, conv_dw_b, conv_ln_g, conv_ln_b,
              mem_w_kv, w_out, ln_g, ln_b,
              moe_w_grp, moe_b_grp, moe_w_exp, moe_b_exp, moe_w_gate, moe_w_up, moe_w_down):
    B, S, _ = x.shape
    cos_n, sin_n = rope_tables(positions, ROT_DIM, ROPE_THETA)
    cos_m, sin_m = rope_tables(positions, MLA_ROPE, MLA_THETA)
    for i in range(DEPTH_2):
        kind = i % N_MIXERS
        j = i // N_MIXERS
        if kind == 0:
            proj = x @ nsa_w_in[j]
            mix = nsa_mixer(proj[..., :-XA_WIDTH], nsa_cmp_pe[j], nsa_cmp_w1[j], nsa_cmp_w2[j], cos_n, sin_n)
        elif kind == 1:
            proj = x @ mla_w_in[j]
            mix = mla_mixer(proj[..., :-XA_WIDTH], mla_q_norm[j], mla_w_uq[j],
                            mla_kv_norm[j], mla_w_ukv[j], cos_m, sin_m)
        else:
            proj = x @ conv_w_in[j]
            mix = conv_mixer(proj[..., :-XA_WIDTH], conv_b_in[j], conv_dw_w[j], conv_dw_b[j],
                             conv_ln_g[j], conv_ln_b[j])
        xq = proj[..., -XA_WIDTH:].reshape(B, S, XA_HEADS, HEAD_DIM_2)
        mkv = mem @ mem_w_kv[i]
        mk = mkv[..., :XA_WIDTH].reshape(B, N_MEM, XA_HEADS, HEAD_DIM_2)
        mv = mkv[..., XA_WIDTH:].reshape(B, N_MEM, XA_HEADS, HEAD_DIM_2)
        xa = memory_cross_attention(xq, mk, mv).reshape(B, S, XA_WIDTH)
        y = jnp.concatenate([mix, xa], -1) @ w_out[i]
        x = layer_norm(DEEPNORM_ALPHA * x + y, ln_g[i, 0], ln_b[i, 0])
        f = hier_moe(x, moe_w_grp[i], moe_b_grp[i], moe_w_exp[i], moe_b_exp[i],
                     moe_w_gate[i], moe_w_up[i], moe_w_down[i])
        x = layer_norm(DEEPNORM_ALPHA * x + f, ln_g[i, 1], ln_b[i, 1])
    return x


def setup_inputs(seed=0):
    out = dict(first_inputs(seed))
    for name, value in second_inputs(seed + 1).items():
        if name != "x":
            out[name + "_2"] = value
    return out


def reference(
    x, p, rel_bias, g_mix_pre, g_mix_post, g_ffn_pre, g_ffn_post, w_in, w_pool, pool_scale,
    w_out, w_up, conv_w, conv_b, w_down, w_ple, w_ple_gate, mem_2, positions_2, nsa_w_in_2,
    nsa_cmp_pe_2, nsa_cmp_w1_2, nsa_cmp_w2_2, mla_w_in_2, mla_q_norm_2, mla_w_uq_2,
    mla_kv_norm_2, mla_w_ukv_2, conv_w_in_2, conv_b_in_2, conv_dw_w_2, conv_dw_b_2, conv_ln_g_2,
    conv_ln_b_2, mem_w_kv_2, w_out_2, ln_g_2, ln_b_2, moe_w_grp_2, moe_b_grp_2, moe_w_exp_2,
    moe_b_exp_2, moe_w_gate_2, moe_w_up_2, moe_w_down_2,
):
    x = first_block(
        x, p, rel_bias, g_mix_pre, g_mix_post, g_ffn_pre, g_ffn_post, w_in, w_pool, pool_scale,
        w_out, w_up, conv_w, conv_b, w_down, w_ple, w_ple_gate,
    )
    return second_block(
        x, mem_2, positions_2, nsa_w_in_2, nsa_cmp_pe_2, nsa_cmp_w1_2, nsa_cmp_w2_2, mla_w_in_2,
        mla_q_norm_2, mla_w_uq_2, mla_kv_norm_2, mla_w_ukv_2, conv_w_in_2, conv_b_in_2,
        conv_dw_w_2, conv_dw_b_2, conv_ln_g_2, conv_ln_b_2, mem_w_kv_2, w_out_2, ln_g_2, ln_b_2,
        moe_w_grp_2, moe_b_grp_2, moe_w_exp_2, moe_b_exp_2, moe_w_gate_2, moe_w_up_2,
        moe_w_down_2,
    )


_drawn_inputs = setup_inputs


def setup_inputs(seed=0):
    import zlib

    import numpy as np

    out = dict(_drawn_inputs(seed))
    spreads = {}
    factors = {'conv_b': 3.584,
     'nsa_cmp_pe_2': 6.227,
     'mla_q_norm_2': 8.0,
     'mla_kv_norm_2': 8.0,
     'moe_b_grp_2': 6.314,
     'moe_b_exp_2': 8.0}
    for name, (base, spread) in spreads.items():
        noise = np.random.default_rng([zlib.crc32(name.encode()), seed]).standard_normal(out[name].shape)
        drawn = base * np.exp(spread * noise) if base else spread * noise
        out[name] = __import__('jax').numpy.asarray(drawn.astype(out[name].dtype))
    for name, factor in factors.items():
        out[name] = (out[name] * factor).astype(out[name].dtype)
    return out
```

```python
from contextlib import ExitStack

import numpy as np

import concourse.bass as bass
from concourse import mybir

F32 = mybir.dt.float32
I32 = mybir.dt.int32
ALU = mybir.AluOpType
ACT = mybir.ActivationFunctionType
AX = mybir.AxisListType

T, D = 256, 1024
KC = 8
BIG = 1.0e30
DFF = 2816
NJ = DFF // 128
ALPHA = 4.0 ** 0.25
NCMP = 15
TWO_PI_INV = float(np.float32(1.0 / (2.0 * np.pi)))
MAGIC = float(1.5 * 2.0 ** 23)


def two_pi_parts():
    parts, rest = [], 2.0 * np.pi
    for _ in range(4):
        m, e = np.frexp(rest)
        p = np.ldexp(np.floor(m * 512.0) / 512.0, e)
        parts.append(float(p))
        rest -= p
    return parts


def constants():
    ident = np.eye(128, dtype=np.float32)
    p = np.arange(128)[:, None]
    s = np.arange(256)[None, :]
    causal = np.where(s - 128 <= p, 0.0, BIG).astype(np.float32)
    j = np.arange(384)
    dist = 255 - j
    n = np.maximum(dist, 0)
    nf = np.maximum(n, 1).astype(np.float32)
    large = 16 + (np.log(nf / np.float32(16)) / np.float32(np.log(8.0)) * np.float32(16)).astype(np.int32)
    bucket = np.where(n < 16, n, np.minimum(large, 31))
    onehot = np.zeros((33, 384), np.float32)
    ok = dist >= 0
    onehot[bucket[ok], j[ok]] = -1.0
    onehot[32, ~ok] = BIG
    cnt = np.zeros((4, 256), np.float32)
    for g, w in enumerate((2, 4, 8, 16)):
        cnt[g] = np.float32(1.0) / np.minimum(np.arange(256) + 1, w).astype(np.float32)
    inv = np.concatenate([
        np.float32(500000.0) ** (-np.arange(0, 16, 2, dtype=np.float32) / np.float32(16)),
        np.float32(10000.0) ** (-np.arange(0, 32, 2, dtype=np.float32) / np.float32(32)),
    ]).astype(np.float32)
    end = np.arange(NCMP) * 16 + 31
    t = np.arange(256)
    cok = (end[None, :] <= t[:, None]).astype(np.float32).reshape(2, 128, NCMP).transpose(1, 0, 2)
    rank = np.array([4.0, 3.0, 2.0, 1.0], np.float32)
    row = np.concatenate([inv, cnt.reshape(-1), rank])
    row = np.broadcast_to(row, (128, row.size))
    return np.ascontiguousarray(np.concatenate(
        [ident, causal, np.ascontiguousarray(cok).reshape(128, 30), row, ident[::-1]], axis=1), np.float32), onehot


C_ID, C_MASK, C_COK, C_INV, C_CNT, C_RANK, C_FLIP = 0, 128, 384, 414, 438, 1462, 1466
C_ALL = 1594


class Queue:

    def __init__(self, sem, serial=False):
        self.sem, self.count, self.ops, self.seen = sem, 0, [], {}
        self.serial = serial

    def wait(self, *toks):
        for tok in toks:
            if tok is None:
                continue
            if isinstance(tok, list):
                self.wait(*tok)
                continue
            sem, n = tok
            if self.seen.get(sem.name, 0) < n:
                self.seen[sem.name] = n
                self.ops.append(("wait", sem, n))

    def do(self, fn, *toks, inc=True):
        self.wait(*toks)
        if self.serial and self.count:
            self.wait((self.sem, self.count))
        if not inc:
            self.ops.append(("op", fn, None, 0))
            return None
        self.count += 1
        self.ops.append(("op", fn, self.sem, 1))
        return (self.sem, self.count)

    def dma(self, fn, sem, *toks):
        self.wait(*toks)
        self.ops.append(("op", fn, sem, 16))

    def emit(self, eng):
        for op in self.ops:
            if op[0] == "wait":
                eng.wait_ge(op[1], op[2])
            else:
                ins = op[1](eng)
                if op[2] is not None:
                    ins.then_inc(op[2], op[3])


class Place:

    def __init__(self, ap):
        self.ap, self.free = ap, []


class Ring:
    def __init__(self, places):
        self.places, self.at = places, 0

    def take(self):
        p = self.places[self.at % len(self.places)]
        self.at += 1
        return p


def build(nc, ins, out, const, onehot, scratch):
    ctx = ExitStack()
    with ctx:
        def sb(name, shape, dt=F32):
            return ctx.enter_context(nc.sbuf_tensor(name, shape, dt))

        def sem(name):
            return ctx.enter_context(nc.semaphore(name))

        PE, V, S, G, SP = (Queue(sem(n)) for n in ("s_pe", "s_dve", "s_act", "s_pool", "s_sp"))
        G.serial = V.serial = S.serial = True
        banks = [Place(ctx.enter_context(nc.psum_tensor(f"ps{i}", [128, 512], F32))) for i in range(8)]
        work = Ring(banks[0:4])
        acc = banks[4:8]

        NSLOT = 5
        slots = []
        for i in range(NSLOT):
            pl = Place(sb(f"w{i}", [128, 4096]))
            pl.sem, pl.n = sem(f"s_w{i}"), 0
            slots.append(pl)
        wring = Ring(slots)

        def stream(*parts):
            sl = wring.take()
            for dst, src in parts:
                SP.dma(lambda e, d=dst(sl.ap), s=src: e.dma_start(d, s), sl.sem, sl.free)
                sl.n += 16
            sl.free = []
            return sl, (sl.sem, sl.n)

        def cols(w, kc, n0, n):
            return (lambda a: a[:, 0:kc * n].rearrange("p (c n) -> p c n", c=kc),
                    w[:, n0:n0 + n].rearrange("(c p) n -> p c n", p=128))

        def wview(sl, kc, n):
            return sl.ap[:, 0:kc * n].rearrange("p (c n) -> p c n", c=kc)

        x = sb("x", [128, 2, D])
        hT = sb("hT", [128, KC, T])
        yT = sb("yT", [128, KC, T])
        z = sb("z", [128, 2, D])
        cst = sb("cst", [128, C_ALL])
        colv = sb("colv", [128, 112])
        gains = [Place(sb(f"gain{i}", [128, D])) for i in range(2)]
        for i, g in enumerate(gains):
            g.sem, g.n = sem(f"s_g{i}"), 0
        arena = sb("arena", [128, 12360])
        Lb = Ring([Place(sb(f"L{i}", [128, 512])) for i in range(2)])
        Pb = Ring([Place(sb(f"P{i}", [128, 512])) for i in range(3)])
        Tb = Ring([Place(sb(f"PT{i}", [128, 512])) for i in range(3)])
        small = sb("small", [128, 1480])
        mkT = sb("mkT", [128, 2, 2, T])
        mv = sb("mv", [128, 2, 2, T])
        wge = sb("wge", [128, 2, KC, 20])
        bge = sb("bge", [128, 2, 20])
        w2c = sb("w2c", [128, 2, 64])

        ident = cst[:, C_ID:C_ID + 128]
        mask = cst[:, C_MASK:C_MASK + 256]
        cok = cst[:, C_COK:C_COK + 30].rearrange("p (t n) -> p t n", t=2)

        sm_at = [0]

        def sm(n):
            a = small[:, sm_at[0]:sm_at[0] + n]
            sm_at[0] += n
            return a

        ar_at = [0]

        def ar(n):
            a = arena[:, ar_at[0]:ar_at[0] + n]
            ar_at[0] += n
            assert ar_at[0] <= 12360
            return a

        G_MIX, G_FFN, PSC, QN, KN, CW, CB = 0, 8, 16, 20, 22, 23, 89

        s_x, s_cst, s_mem, s_small = sem("s_x"), sem("s_cst"), sem("s_mem"), sem("s_small")
        s_early, s_bias, s_out = sem("s_early"), sem("s_bias"), sem("s_out")
        ar_at[0] = 0
        mem = ar(2 * D).rearrange("p (t d) -> p t d", t=2)
        memT = ar(KC * T).rearrange("p (c t) -> p c t", c=KC)
        rows = ar(128)
        relx = ar(8)
        oh = ar(384)
        rb = ar(384)
        pes = ar(128)
        btab = ar(8 * 256).rearrange("p (h s) -> p h s", h=8)
        posi = sm(3).bitcast(I32)

        SP.dma(lambda e: e.dma_start(x[:, :, :], ins["x"][0].rearrange("(t p) d -> p t d", p=128)), s_x)
        SP.dma(lambda e: e.dma_start(mem, ins["mem_2"][0].rearrange("(t p) d -> p t d", p=128)), s_mem)
        S.dma(lambda e: e.dma_start(cst[:, :], const), s_cst)
        early = 0
        at = 0
        for name, view in (("g_mix_pre", 8), ("g_ffn_pre", 8), ("pool_scale", 4), ("mla_q_norm_2", 2),
                           ("mla_kv_norm_2", 1), ("conv_w", 66), ("conv_b", 22)):
            src = ins[name]
            if name == "conv_w":
                src = src[0].rearrange("k (j p) -> (k j) p", p=128)
            else:
                src = src[0].rearrange("(j p) -> j p", p=128)
            S.dma(lambda e, a=at, v=view, s=src: e.dma_start(rows[a:a + v, :], s), s_early)
            at += view
            early += 16
        NROWS = at
        S.dma(lambda e: e.dma_start(relx[0:32, :], ins["rel_bias"]), s_early)
        S.dma(lambda e: e.dma_start(oh[0:33, :], onehot), s_early)
        for k in range(2):
            for h in range(2):
                S.dma(lambda e, k=k, h=h: e.dma_start(pes[32 * k:32 * k + 32, 64 * h:64 * h + 64],
                                                      ins["nsa_cmp_pe_2"][0, k]), s_early)
        early += 16 * 6
        pcol = ins["positions_2"].rearrange("a t -> t a")
        for t in range(2):
            S.dma(lambda e, t=t: e.dma_start(posi[:, t:t + 1], pcol[t * 128:t * 128 + 128, :]), s_early)
        S.dma(lambda e: e.dma_start(posi[0:NCMP, 2:3], pcol[31:256:16, :], allow_slow_non_contiguous=True), s_early)
        early += 16 * 3
        T_early = (s_early, early)
        T_cst, T_x, T_mem = (s_cst, 16), (s_x, 16), (s_mem, 16)

        ns = 0
        for i in range(2):
            S.dma(lambda e, i=i: e.dma_start(wge[:, i, :, 0:4],
                                             ins["moe_w_grp_2"][i].rearrange("(c p) n -> p c n", p=128)), s_small)
            S.dma(lambda e, i=i: e.dma_start(wge[:, i, :, 4:20],
                                             ins["moe_w_exp_2"][i].rearrange("(c p) n -> p c n", p=128)), s_small)
            S.dma(lambda e, i=i: e.dma_start(bge[:, i, 0:4], ins["moe_b_grp_2"][i].partition_broadcast(128)), s_small)
            S.dma(lambda e, i=i: e.dma_start(bge[:, i, 4:20], ins["moe_b_exp_2"][i].partition_broadcast(128)), s_small)
            S.dma(lambda e, i=i: e.dma_start(w2c[:, i, :], ins["nsa_cmp_w2_2"][0, i]), s_small)
            ns += 80
        wpool = ar(4 * 128).rearrange("p (g d) -> p g d", g=4)
        S.dma(lambda e: e.dma_start(wpool, ins["w_pool"][0].rearrange("g c d -> c g d")), s_small)
        ns += 16
        T_small = (s_small, ns)

        def gain(i, row):
            g = gains[i]
            SP.dma(lambda e, a=g.ap, r=row: e.dma_start(a[:, :], r.partition_broadcast(128)), g.sem, g.free)
            g.n += 16
            g.free = []
            return g, (g.sem, g.n)

        half_pow = sm(8)
        k_pow = G.do(lambda e: e.memset(half_pow, -0.5))

        def rsqrt(dst, src, eps, scale, tok):
            a = V.do(lambda e: e.tensor_scalar(dst, src, scale, eps, ALU.mult, ALU.add), tok)
            n = src.shape[-1]
            return G.do(lambda e: e.tensor_tensor(dst, dst, half_pow[:, 0:n], ALU.pow), a, k_pow)

        sq = sm(8)
        rstd = sm(4)
        mean = sm(4)

        flip = [0]

        def evac(dst, src, tok, scale=None, eng=None):
            if eng is None:
                flip[0] ^= 1
                eng = "S" if flip[0] else "V"
            if eng == "S":
                if scale is None:
                    return S.do(lambda e: e.copy(dst, src), tok)
                return S.do(lambda e: e.mul(dst, src, scale), tok)
            if scale is None:
                return V.do(lambda e: e.tensor_copy(dst, src), tok)
            return V.do(lambda e: e.tensor_scalar(dst, src, scale, None, ALU.mult), tok)

        def turn(src, dst, tok, gcol=None, dfree=()):
            toks = []
            for c in range(4):
                bk = work.take()
                PE.wait(tok, bk.free, T_cst)
                for q in range(4):
                    kc, t = 2 * c + q // 2, q % 2
                    d = PE.do(lambda e, b=bk.ap, q=q, kc=kc, t=t: e.transpose(
                        b[:, q * 128:q * 128 + 128], src[:, t, kc * 128:kc * 128 + 128], ident), inc=(q == 3))
                if gcol is None:
                    k = evac(dst[:, 2 * c:2 * c + 2, :], bk.ap[:, :].rearrange("p (c t) -> p c t", c=2), [d, *dfree])
                else:
                    for q in range(2):
                        kc = 2 * c + q
                        k = V.do(lambda e, b=bk.ap, q=q, kc=kc: e.tensor_scalar(
                            dst[:, kc, :], b[:, q * 256:q * 256 + 256], gcol[:, kc:kc + 1], None, ALU.mult),
                            d, T_col, *dfree)
                bk.free = [k]
                toks.append(k)
            return toks

        def rms_turn(src, tok, gcol, dst, dfree=()):
            for t in range(2):
                a = S.do(lambda e, t=t: e.activation(z[:, t, :], src[:, t, :], ACT.Square,
                                                     accum_out=sq[:, t:t + 1]), tok)
            r = rsqrt(rstd[:, 0:2], sq[:, 0:2], 1e-6, 1.0 / D, a)
            for t in range(2):
                k = V.do(lambda e, t=t: e.tensor_scalar(z[:, t, :], src[:, t, :], rstd[:, t:t + 1], None, ALU.mult), r)
            return turn(z, dst, k, gcol, dfree)

        def lin_tok(lT, ltok, kcs, w, n0, n, use):
            sl, wt = stream(cols(w, kcs, n0, n))
            wv = wview(sl, kcs, n)
            for t in range(2):
                bk = work.take()
                PE.wait(ltok, bk.free, wt)
                for k in range(kcs):
                    d = PE.do(lambda e, b=bk.ap, k=k, t=t: e.matmul(
                        b[:, 0:n], lT[:, k, t * 128:t * 128 + 128], wv[:, k, :],
                        start=(k == 0), stop=(k == kcs - 1)), inc=(k == kcs - 1))
                bk.free = [use(t, bk.ap, d)]
            sl.free = [d]
            return d

        def lin_feat(lT, ltok, kcs, w, n0, n, use):
            sl, wt = stream(cols(w, kcs, n0, n))
            wv = wview(sl, kcs, n)
            for c in range(n // 256):
                bk = work.take()
                PE.wait(ltok, bk.free, wt)
                for q in range(2):
                    for k in range(kcs):
                        d = PE.do(lambda e, b=bk.ap, k=k, q=q, c=c: e.matmul(
                            b[:, q * 256:q * 256 + 256], wv[:, k, (2 * c + q) * 128:(2 * c + q) * 128 + 128],
                            lT[:, k, :], start=(k == 0), stop=(k == kcs - 1)), inc=(q == 1 and k == kcs - 1))
                bk.free = [use(c, bk.ap, d)]
            sl.free = [d]
            return d

        def out_proj(lT, ltok, w, use):
            for hf in range(2):
                d = lin_tok(lT, ltok, KC, w, hf * 512, 512, lambda t, b, tok, hf=hf: use(t, hf, b, tok))
            return d

        def rms_add(g, gtok, ytoks, ss):
            a = V.do(lambda e: e.tensor_reduce(sq[:, 4:6], ss, AX.X, ALU.add), ytoks)
            r = rsqrt(rstd[:, 2:4], sq[:, 4:6], 1e-6, 1.0 / D, a)
            res = []
            for t in range(2):
                k = V.do(lambda e, t=t: e.scalar_tensor_tensor(
                    z[:, t, :], z[:, t, :], rstd[:, 2 + t:3 + t], g.ap[:, :], ALU.mult, ALU.mult), r, gtok)
                k2 = G.do(lambda e, t=t: e.tensor_tensor(x[:, t, :], x[:, t, :], z[:, t, :], ALU.add), k)
                res.append(k2)
            g.free = [k]
            return res

        ss4 = sm(4).rearrange("p (t h) -> p t h", t=2)
        def keep_sq(t, hf, b, tok):
            a = V.do(lambda e: e.tensor_copy(z[:, t, hf * 512:hf * 512 + 512], b[:, :]), tok)
            jk = Lb.take()
            k = S.do(lambda e: e.activation(jk.ap[:, :], z[:, t, hf * 512:hf * 512 + 512], ACT.Square,
                                            accum_out=ss4[:, t, hf:hf + 1]), a, jk.free)
            jk.free = [k]
            return k

        st = sm(24).rearrange("p (t h s) -> p t h s", t=2, h=2)
        mvv = sm(4).rearrange("p (t s) -> p t s", t=2)

        def add_stats(t, hf, b, tok):
            a = V.do(lambda e: e.scalar_tensor_tensor(
                z[:, t, hf * 512:hf * 512 + 512], x[:, t, hf * 512:hf * 512 + 512], ALPHA, b[:, :],
                ALU.mult, ALU.add), tok)
            V.do(lambda e: e.bn_stats(st[:, t, hf, :], z[:, t, hf * 512:hf * 512 + 512]), a)
            return a

        def layer_norm(i, jn):
            gg, gt = gain(0, ins["ln_g_2"][i, jn])
            gb, bt = gain(1, ins["ln_b_2"][i, jn])
            stats = (V.sem, V.count)
            res = []
            for t in range(2):
                a = V.do(lambda e, t=t: e.bn_aggr(mvv[:, t, :], st[:, t, :, :].rearrange("p h s -> p (h s)")), stats)
            r = rsqrt(rstd[:, 0:2], mvv[:, :, 1], 1e-5, 1.0, a)
            for t in range(2):
                k = V.do(lambda e, t=t: e.tensor_scalar(z[:, t, :], z[:, t, :], mvv[:, t, 0:1], rstd[:, t:t + 1],
                                                        ALU.subtract, ALU.mult), r)
                k = V.do(lambda e, t=t: e.tensor_tensor(z[:, t, :], z[:, t, :], gg.ap[:, :], ALU.mult), k, gt)
                k2 = G.do(lambda e, t=t: e.tensor_tensor(x[:, t, :], z[:, t, :], gb.ap[:, :], ALU.add), k, bt)
                res.append(k2)
            gg.free, gb.free = [k], [k2]
            return res

        sbank, tbank, obank = Ring(banks[0:3]), Ring(banks[3:6]), Ring(banks[6:8])
        mrs = Ring([Place(sm(6)) for _ in range(4)])

        def attention(jobs, ready, pair_out):
            n = len(jobs)
            for i in range(n + 3):
                if i < n:
                    j = jobs[i]
                    bk = sbank.take()
                    PE.wait(bk.free, ready)
                    for q, (lq, rk, w, mk, gt) in enumerate(j["S"]):
                        d = PE.do(lambda e, b=bk.ap, q=q, lq=lq, rk=rk, w=w: e.matmul(
                            b[:, q * 256:q * 256 + w], lq, rk, start=True, stop=True), inc=(q == len(j["S"]) - 1))
                    Lp, Pp, ms = Lb.take(), Pb.take(), mrs.take()
                    m, rs, rc = ms.ap[:, 0:2], ms.ap[:, 2:4], ms.ap[:, 4:6]
                    ex = []
                    for q, (lq, rk, w, mk, gt) in enumerate(j["S"]):
                        c = slice(q * 256, q * 256 + w)
                        if mk is not None:
                            a = V.do(lambda e, c=c, q=q, mk=mk, L=Lp.ap, b=bk.ap, m=m: e.tensor_tensor_reduce(
                                L[:, c], b[:, c], mk, 1.0, 3.0e38, ALU.add, ALU.min, m[:, q:q + 1]), d, Lp.free, ms.free)
                            src, fin = Lp.ap, a
                        else:
                            a = V.do(lambda e, c=c, q=q, b=bk.ap, m=m: e.tensor_reduce(
                                m[:, q:q + 1], b[:, c], AX.X, ALU.min), d, ms.free)
                            src = bk.ap
                        ex.append(S.do(lambda e, c=c, q=q, s=src, P=Pp.ap, m=m, rs=rs: e.activation(
                            P[:, c], s[:, c], ACT.Exp, bias=m[:, q:q + 1], scale=-1.0,
                            accum_out=rs[:, q:q + 1]), a, Pp.free))
                    bk.free = [a] if j["S"][0][3] is not None else [ex[-1]]
                    Lp.free = [ex[-1]]
                    nq = len(j["S"])
                    j["P"], j["ms"] = Pp, ms
                    j["ex"], j["nq"] = ex[-1], nq
                if 1 <= i <= n:
                    j = jobs[i - 1]
                    rc, rs, nq = j["ms"].ap[:, 4:6], j["ms"].ap[:, 2:4], j["nq"]
                    k = V.do(lambda e, rc=rc, rs=rs, nq=nq: e.reciprocal(rc[:, 0:nq], rs[:, 0:nq]), j["ex"])
                    for q, (lq, rk, w, mk, gt) in enumerate(j["S"]):
                        c = slice(q * 256, q * 256 + w)
                        if gt is None:
                            kk = V.do(lambda e, c=c, q=q, P=j["P"].ap, rc=rc: e.tensor_scalar(
                                P[:, c], P[:, c], rc[:, q:q + 1], None, ALU.mult), k)
                        else:
                            kk = V.do(lambda e, c=c, q=q, P=j["P"].ap, rc=rc, gt=gt: e.tensor_scalar(
                                P[:, c], P[:, c], rc[:, q:q + 1], gt, ALU.mult, ALU.mult), k)
                    j["ms"].free = [kk]
                    j["norm"] = kk
                if 2 <= i <= n + 1:
                    j = jobs[i - 2]
                    bk, Tp = tbank.take(), Tb.take()
                    PE.wait(bk.free, j["norm"])
                    todo = [(q, s) for q, sp in enumerate(j["S"]) for s in range(sp[2] // 128)]
                    for o, (q, s) in enumerate(todo):
                        d = PE.do(lambda e, o=o, q=q, s=s, b=bk.ap, P=j["P"].ap: e.transpose(
                            b[:, o * 128:o * 128 + 128], P[:, q * 256 + s * 128:q * 256 + s * 128 + 128], ident),
                            inc=(o == len(todo) - 1))
                    j["P"].free = [d]
                    w = 128 * len(todo)
                    k = evac(Tp.ap[:, 0:w], bk.ap[:, 0:w], [d, *Tp.free])
                    bk.free = [k]
                    j["T"], j["Tk"], j["todo"] = Tp, k, todo
                if i >= 3:
                    j = jobs[i - 3]
                    if j["first"]:
                        ob = obank.take()
                        PE.wait(ob.free)
                    PE.wait(j["Tk"])
                    hp, t = j["half"] * 64, j["t"]
                    mm = [(j["v"][q][s], j["T"].ap[:, o * 128:o * 128 + 128]) for o, (q, s) in enumerate(j["todo"])]
                    mm += j.get("extra", [])
                    for o, (l, r) in enumerate(mm):
                        d = PE.do(lambda e, o=o, l=l, r=r, b=ob.ap, hp=hp, t=t, n=len(mm): e.matmul(
                            b[hp:hp + 64, t * 128:t * 128 + 128], l, r, start=(o == 0), stop=(o == n - 1)),
                            inc=(o == len(mm) - 1))
                    j["T"].free = [d]
                    if j["last"]:
                        ob.free = [pair_out(j["pair"], ob.ap, d)]

        def pair_jobs(heads, make):
            jobs = []
            for h in range(heads):
                for t in range(2):
                    j = make(h, t)
                    j.update(t=t, half=h % 2, pair=h // 2, first=(h % 2 == 0 and t == 0), last=(h % 2 == 1 and t == 1))
                    jobs.append(j)
            return jobs

        def msk(t):
            return (mask[:, 128:256], 128) if t == 0 else (mask[:, 0:256], 256)

        bk = work.take()
        PE.wait(T_early, T_cst)
        d1 = PE.do(lambda e, b=bk.ap: e.transpose(b[:, 0:NROWS], rows[0:NROWS, :], ident[0:NROWS, 0:NROWS]))
        T_col = V.do(lambda e, b=bk.ap: e.tensor_copy(colv[:, 0:NROWS], b[:, 0:NROWS]), d1)
        bk.free = [T_col]

        ang = sm(72).rearrange("p (k n) -> p k n", k=3)
        trig = sm(144).rearrange("p (q k n) -> p q k n", q=2, k=3)
        kk_ = sm(72).rearrange("p (k n) -> p k n", k=3)
        posf = sm(3)
        inv = cst[:, C_INV:C_INV + 24]
        a0 = V.do(lambda e: e.memset(posf, 0.0))
        V.do(lambda e: e.tensor_copy(posf[:, 0:2], posi[:, 0:2]), T_early, a0)
        a0 = V.do(lambda e: e.tensor_copy(posf[0:NCMP, 2:3], posi[0:NCMP, 2:3]))
        for k in range(3):
            a1 = V.do(lambda e, k=k: e.tensor_scalar(ang[:, k, :], inv, posf[:, k:k + 1], None, ALU.mult), a0, T_cst)
        for q, shift in ((0, 0.25), (1, 0.0)):
            b1 = V.do(lambda e, s=shift: e.tensor_scalar(kk_, ang, TWO_PI_INV, s, ALU.mult, ALU.add), a1)
            b1 = V.do(lambda e: e.tensor_scalar(kk_, kk_, MAGIC, None, ALU.add), b1)
            b1 = V.do(lambda e: e.tensor_scalar(kk_, kk_, MAGIC, None, ALU.subtract), b1)
            cur = ang
            for part in two_pi_parts():
                b1 = V.do(lambda e, q=q, c=cur, p=part: e.scalar_tensor_tensor(
                    trig[:, q, :, :], kk_, -p, c, ALU.mult, ALU.add), b1)
                cur = trig[:, q, :, :]
            if q == 0:
                b1 = V.do(lambda e: e.tensor_scalar(trig[:, 0, :, :], trig[:, 0, :, :], float(np.pi / 2), None,
                                                    ALU.add), b1)
            b1 = V.do(lambda e, q=q: e.tensor_scalar(trig[:, q, :, :], trig[:, q, :, :], 3.14159, -3.14159,
                                                     ALU.min, ALU.max), b1)
        T_trig = S.do(lambda e: e.activation(trig, trig, ACT.Sin), b1)

        def rope(x1, x2, k, lo, hi, heads, tmp, tok, p=128):
            n = hi - lo
            c, s = trig[0:p, 0, k, lo:hi], trig[0:p, 1, k, lo:hi]
            for _ in heads:
                c, s = c.unsqueeze(1), s.unsqueeze(1)
            c, s = c.broadcast_to([p, *heads, n]), s.broadcast_to([p, *heads, n])
            V.wait(tok, T_trig)
            V.do(lambda e: e.tensor_tensor(tmp[0], x1, c, ALU.mult))
            V.do(lambda e: e.tensor_tensor(tmp[1], x2, s, ALU.mult))
            V.do(lambda e: e.tensor_tensor(tmp[2], x1, s, ALU.mult))
            a = V.do(lambda e: e.tensor_tensor(tmp[3], x2, c, ALU.mult))
            V.do(lambda e: e.tensor_tensor(x1, tmp[0], tmp[1], ALU.subtract), a)
            return V.do(lambda e: e.tensor_tensor(x2, tmp[2], tmp[3], ALU.add))

        a = G.do(lambda e: e.memset(relx[32:33, :], 1.0))
        bk = work.take()
        d = PE.do(lambda e, b=bk.ap: e.matmul(b[0:8, 0:384], relx[0:33, :], oh[0:33, :], start=True, stop=True),
                  T_early, a, bk.free)
        k = V.do(lambda e, b=bk.ap: e.tensor_copy(rb[0:8, :], b[0:8, 0:384]), d)
        bk.free = [k]
        S.dma(lambda e: e.dma_start(scratch, rb[0:8, :]), s_bias, k)
        for h in range(8):
            src = bass.AP(scratch.tensor, scratch.offset + h * 384, [[1, 128], [1, 256]])
            S.dma(lambda e, h=h, src=src: e.dma_start(yT[:, h, :], src), s_bias, (s_bias, 16))
        T_bias = []
        for c in range(4):
            bk = work.take()
            d = PE.do(lambda e, b=bk.ap, c=c: e.matmul(
                b[:, :], cst[:, C_FLIP:C_FLIP + 128], yT[:, 2 * c:2 * c + 2, :], start=True, stop=True),
                (s_bias, 16 * 9), T_cst, bk.free)
            k = V.do(lambda e, b=bk.ap, c=c: e.tensor_copy(
                btab[:, 2 * c:2 * c + 2, :], b[:, :].rearrange("p (h s) -> p h s", h=2)), d)
            bk.free = [k]
            T_bias.append(k)

        peT = sm(64)
        bk = work.take()
        d = PE.do(lambda e, b=bk.ap: e.transpose(b[:, 0:64], pes[0:64, :], ident[0:64, 0:64]), bk.free)
        T_peT = V.do(lambda e, b=bk.ap: e.tensor_copy(peT, b[:, 0:64]), d)
        bk.free = [T_peT]
        cbias = sm(30).rearrange("p (t n) -> p t n", t=2)
        T_cb = V.do(lambda e: e.tensor_scalar(cbias, cok, -1.0, BIG, ALU.add, ALU.mult))

        T_hT = rms_turn(x, T_x, colv[:, G_MIX:G_MIX + 8], hT)
        T_memT = turn(mem, memT, T_mem)
        T_mk = []
        for i in range(2):
            w = ins["mem_w_kv_2"][i]

            def keep_k(c, b, tok, i=i):
                k = evac(mkT[:, i, :, :], b[:, :].rearrange("p (c t) -> p c t", c=2), tok)
                T_mk.append(k)
                return k

            def keep_v(t, b, tok, i=i):
                k = evac(mv[:, i, t, :], b[:, 0:256], tok)
                T_mk.append(k)
                return k

            lin_feat(memT, T_memT, KC, w, 0, 256, keep_k)
            T_mem_done = lin_tok(memT, T_memT, KC, w, 256, 256, keep_v)

        w_in = ins["w_in"][0]
        uT = ar(4 * T).rearrange("p (g t) -> p g t", g=4)
        pA = ar(T)
        pB = ar(T)
        qT = ar(4 * T).rearrange("p (g t) -> p g t", g=4)
        kT = ar(4 * T).rearrange("p (g t) -> p g t", g=4)
        vt = ar(2 * 512).rearrange("p (t d) -> p t d", t=2)
        toks = {"u": [], "q": [], "k": [], "v": []}

        def keep(dst, key, scale=None):
            def use(c, b, tok):
                k = evac(dst[:, 2 * c:2 * c + 2, :], b[:, :].rearrange("p (c t) -> p c t", c=2), tok, scale)
                toks[key].append(k)
                return k
            return use

        lin_feat(hT, T_hT, KC, w_in, 512, 512, keep(qT, "q", -0.125))
        lin_feat(hT, T_hT, KC, w_in, 1024, 512, keep(kT, "k"))

        def keep_vt(t, b, tok):
            k = evac(vt[:, t, :], b[:, :], tok)
            toks["v"].append(k)
            return k

        lin_tok(hT, T_hT, KC, w_in, 1536, 512, keep_vt)
        lin_feat(hT, T_hT, KC, w_in, 0, 512, keep(uT, "u"))

        T_y = []

        def moba(h, t):
            w = 128 * (t + 1)
            r, c = 64 * (h % 2), h // 2
            bt = btab[:, h, 128:256] if t == 0 else btab[:, h, :]
            return dict(S=[(qT[r:r + 64, c, t * 128:t * 128 + 128], kT[r:r + 64, c, 0:w], w, bt, None)],
                        v=[[vt[:, s, h * 64:h * 64 + 64] for s in range(2)]])

        def moba_out(p, b, tok):
            k = evac(yT[:, 4 + p, :], b[:, 0:256], tok)
            T_y.append(k)
            return k

        V.wait(T_bias)
        attention(pair_jobs(8, moba), toks["q"] + toks["k"] + toks["v"], moba_out)

        for g in range(4):
            src, tok = uT[:, g, :], toks["u"]
            for s in range(g + 1):
                sh = 1 << s
                dst = (pA, pB)[s % 2]
                k1 = V.do(lambda e, d=dst, c=src, sh=sh: e.tensor_copy(d[:, 0:sh], c[:, 0:sh]), tok)
                k2 = V.do(lambda e, d=dst, c=src, sh=sh: e.tensor_tensor(
                    d[:, sh:T], c[:, sh:T], c[:, 0:T - sh], ALU.add))
                src, tok = dst, [k1, k2]
            cn = cst[:, C_CNT + g * 256:C_CNT + g * 256 + 256]
            k1 = V.do(lambda e, c=src, cn=cn: e.tensor_tensor(c, c, cn, ALU.mult), tok)
            k1 = V.do(lambda e, c=src, g=g: e.tensor_tensor(uT[:, g, :], c, uT[:, g, :], ALU.subtract), k1)
            bk = work.take()
            d = PE.do(lambda e, b=bk.ap, g=g: e.matmul(b[:, 0:256], wpool[:, g, :], uT[:, g, :], start=True, stop=True),
                      k1, T_small, bk.free)
            k = S.do(lambda e, b=bk.ap, g=g: e.mul(yT[:, g, :], b[:, 0:256], colv[:, PSC + g:PSC + g + 1]), d, T_col)
            bk.free = [k]
            T_y.append(k)

        g0, gt0 = gain(0, ins["g_mix_post"][0])
        yk = []

        def keep_y(t, hf, b, tok):
            k = keep_sq(t, hf, b, tok)
            yk.append(k)
            return k

        out_proj(yT, T_y, ins["w_out"][0], keep_y)
        T_x1 = rms_add(g0, gt0, yk, ss4)

        T_h2 = rms_turn(x, T_x1, colv[:, G_FFN:G_FFN + 8], hT)
        ar_at[0] = 0
        h2T = ar(NJ * T).rearrange("p (j t) -> p j t", j=NJ)
        cbs = Ring([Place(ar(T)) for _ in range(3)])
        gbs = Ring([Place(ar(T)) for _ in range(2)])
        pT = ar(2 * T).rearrange("p (c t) -> p c t", c=2)
        pin = ar(2 * 256).rearrange("p (t d) -> p t d", t=2)
        sgm = ar(2 * D).rearrange("p (t d) -> p t d", t=2)
        s_p = sem("s_p")
        SP.dma(lambda e: e.dma_start(pin, ins["p"][0, 0].rearrange("(t p) d -> p t d", p=128)), s_p, yk)
        w_up = ins["w_up"][0]
        T_f = []
        for u in range(NJ // 2):
            sl, wt = stream(
                (lambda a: a[:, 0:4096].rearrange("p (c n) -> p c n", c=8)[:, :, 0:256],
                 w_up[:, u * 256:u * 256 + 256].rearrange("(c p) n -> p c n", p=128)),
                (lambda a: a[:, 0:4096].rearrange("p (c n) -> p c n", c=8)[:, :, 256:512],
                 w_up[:, DFF + u * 256:DFF + u * 256 + 256].rearrange("(c p) n -> p c n", p=128)))
            wv = wview(sl, 8, 512)
            for q in range(2):
                j = 2 * u + q
                bk = work.take()
                PE.wait(bk.free, wt, T_h2)
                for gv in range(2):
                    for k in range(KC):
                        d = PE.do(lambda e, b=bk.ap, gv=gv, k=k, q=q, wv=wv: e.matmul(
                            b[:, gv * 256:gv * 256 + 256], wv[:, k, gv * 256 + q * 128:gv * 256 + q * 128 + 128],
                            hT[:, k, :], start=(k == 0), stop=(k == KC - 1)), inc=(gv == 1 and k == KC - 1))
                cb, gb = cbs.take(), gbs.take()
                w = [colv[:, CW + i * NJ + j:CW + i * NJ + j + 1] for i in range(3)]
                bias = colv[:, CB + j:CB + j + 1]
                a = S.do(lambda e, b=bk.ap, c=cb.ap, w=w, bias=bias: e.activation(
                    c, b[:, 0:256], ACT.Identity, bias=bias, scale=w[2]), d, cb.free, yk)
                a = V.do(lambda e, b=bk.ap, c=cb.ap, w=w: e.scalar_tensor_tensor(
                    c[:, 1:T], b[:, 0:T - 1], w[1], c[:, 1:T], ALU.mult, ALU.add), a)
                a = V.do(lambda e, b=bk.ap, c=cb.ap, w=w: e.scalar_tensor_tensor(
                    c[:, 2:T], b[:, 0:T - 2], w[0], c[:, 2:T], ALU.mult, ALU.add), a)
                a = S.do(lambda e, c=cb.ap, g=gb.ap: e.activation(g, c, ACT.Gelu_apprx_tanh), a, gb.free)
                cb.free = [a]
                a = V.do(lambda e, b=bk.ap, g=gb.ap, j=j: e.tensor_tensor(h2T[:, j, :], g, b[:, 256:512], ALU.mult), a)
                gb.free, bk.free = [a], [a]
                T_f.append(a)
            sl.free = [d]

        bk = work.take()
        PE.wait((s_p, 16), bk.free)
        for q in range(4):
            d = PE.do(lambda e, b=bk.ap, q=q: e.transpose(
                b[:, q * 128:q * 128 + 128], pin[:, q % 2, (q // 2) * 128:(q // 2) * 128 + 128], ident), inc=(q == 3))
        T_pT = evac(pT, bk.ap[:, :].rearrange("p (c t) -> p c t", c=2), d)
        bk.free = [T_pT]

        w_down = ins["w_down"][0]
        for u in range(6):
            n = min(4, NJ - 4 * u)
            sl, wt = stream((lambda a, n=n: a[:, 0:n * 1024].rearrange("p (c n) -> p c n", c=n),
                             w_down[u * 512:u * 512 + n * 128, :].rearrange("(c p) n -> p c n", p=128)))
            wv = wview(sl, n, 1024)
            for c in range(n):
                j = 4 * u + c
                PE.wait(wt, T_f[j])
                if j == 0:
                    PE.wait(*[b.free for b in acc])
                for o in range(4):
                    t, hf = o // 2, o % 2
                    d = PE.do(lambda e, o=o, t=t, hf=hf, j=j, c=c, wv=wv: e.matmul(
                        acc[o].ap[:, :], h2T[:, j, t * 128:t * 128 + 128], wv[:, c, hf * 512:hf * 512 + 512],
                        start=(j == 0), stop=(j == NJ - 1)), inc=(o == 3))
            sl.free = [d]
        g1, gt1 = gain(1, ins["g_ffn_post"][0])
        fk = []
        for o in range(4):
            k = keep_sq(o // 2, o % 2, acc[o].ap, d)
            acc[o].free = [k]
            fk.append(k)
        T_x2 = rms_add(g1, gt1, fk, ss4)

        T_x2T = turn(x, hT, T_x2)

        def keep_sg(t, hf, b, tok):
            k = S.do(lambda e: e.activation(sgm[:, t, hf * 512:hf * 512 + 512], b[:, :], ACT.Sigmoid), tok)
            return k

        out_proj(hT, T_x2T, ins["w_ple_gate"][0], keep_sg)
        T_sg = (S.sem, S.count)
        T_x3 = []
        sl, wt = stream((lambda a: a[:, 0:2048].rearrange("p (c n) -> p c n", c=2),
                         ins["w_ple"][0].rearrange("(c p) n -> p c n", p=128)))
        wv = wview(sl, 2, 1024)
        for o in range(4):
            t, hf = o // 2, o % 2
            bk = work.take()
            PE.wait(bk.free, wt, T_pT)
            for k in range(2):
                d = PE.do(lambda e, b=bk.ap, k=k, t=t, hf=hf, wv=wv: e.matmul(
                    b[:, :], pT[:, k, t * 128:t * 128 + 128], wv[:, k, hf * 512:hf * 512 + 512],
                    start=(k == 0), stop=(k == 1)), inc=(k == 1))
            hs = slice(hf * 512, hf * 512 + 512)
            a = V.do(lambda e, b=bk.ap, t=t, hs=hs: e.tensor_tensor(sgm[:, t, hs], sgm[:, t, hs], b[:, :], ALU.mult),
                     d, T_sg)
            bk.free = [a]
            T_x3.append(G.do(lambda e, t=t, hs=hs: e.tensor_tensor(x[:, t, hs], x[:, t, hs], sgm[:, t, hs], ALU.add),
                             a, T_x2T))
        sl.free = [d]

        def cross(i, xqT, tok):
            def make(h, t):
                r, c = 64 * (h % 2), h // 2
                return dict(S=[(xqT[r:r + 64, c, t * 128:t * 128 + 128], mkT[r:r + 64, i, c, :], 256, None, None)],
                            v=[[mv[:, i, s, h * 64:h * 64 + 64] for s in range(2)]])

            def fin(p, b, tok2):
                k = evac(yT[:, 6 + p, :], b[:, 0:256], tok2)
                T_y.append(k)
                return k

            attention(pair_jobs(4, make), [*tok, *T_mk], fin)

        def turn_cols(src, c0, chunks, dst, tok, scale=None, step=128):
            res = []
            for c in range(0, chunks, 2):
                bk = work.take()
                PE.wait(bk.free, tok)
                m = min(2, chunks - c)
                for q in range(2 * m):
                    cc, t = c + q // 2, q % 2
                    a = src[:, t, c0 + cc * step:c0 + cc * step + 128]
                    d = PE.do(lambda e, b=bk.ap, q=q, a=a: e.transpose(b[:, q * 128:q * 128 + 128], a, ident),
                              inc=(q == 2 * m - 1))
                k = evac(dst[:, c:c + m, :], bk.ap[:, 0:m * 256].rearrange("p (c t) -> p c t", c=m), d, scale)
                bk.free = [k]
                res.append(k)
            return res

        lg = sm(40).rearrange("p (t n) -> p t n", t=2)
        eg = sm(8).rearrange("p (t n) -> p t n", t=2)
        ohg = sm(8).rearrange("p (t n) -> p t n", t=2)
        oh1 = sm(8).rearrange("p (t n) -> p t n", t=2)
        oh2 = sm(8).rearrange("p (t n) -> p t n", t=2)
        le = sm(8).rearrange("p (t n) -> p t n", t=2)
        le2 = sm(8).rearrange("p (t n) -> p t n", t=2)
        w4 = sm(8).rearrange("p (t n) -> p t n", t=2)
        c4 = sm(8).rearrange("p (t n) -> p t n", t=2)
        r2 = [sm(2) for _ in range(5)]
        pick = sm(32).rearrange("p (t g j) -> p t g j", t=2, g=4)
        gate = sm(32).rearrange("p (t n) -> p t n", t=2)
        rank = cst[:, C_RANK:C_RANK + 4].unsqueeze(1).broadcast_to([128, 2, 4])

        def bc(a, n=4):
            return a.unsqueeze(2).broadcast_to([128, 2, n])

        def first_max(dst, src, mx, tok):
            a = V.do(lambda e: e.tensor_reduce(mx, src, AX.X, ALU.max), tok)
            a = V.do(lambda e: e.tensor_tensor(c4, src, bc(mx), ALU.is_equal), a)
            a = V.do(lambda e: e.tensor_tensor(c4, c4, rank, ALU.mult), a)
            a = V.do(lambda e: e.tensor_reduce(r2[4], c4, AX.X, ALU.max), a)
            return V.do(lambda e: e.tensor_tensor(dst, c4, bc(r2[4]), ALU.is_equal), a)

        def moe(i, tok):
            T_xT = turn(x, hT, tok)
            bk = work.take()
            PE.wait(bk.free, T_xT, T_small)
            for t in range(2):
                for k in range(KC):
                    d = PE.do(lambda e, b=bk.ap, t=t, k=k: e.matmul(
                        b[:, t * 20:t * 20 + 20], hT[:, k, t * 128:t * 128 + 128], wge[:, i, k, :],
                        start=(k == 0), stop=(k == KC - 1)), inc=(t == 1 and k == KC - 1))
            a = V.do(lambda e, b=bk.ap: e.tensor_tensor(
                lg, b[:, 0:40].rearrange("p (t n) -> p t n", t=2),
                bge[:, i, :].unsqueeze(1).broadcast_to([128, 2, 20]), ALU.add), d)
            bk.free = [a]
            gmax, gs, m1, m2 = r2[0], r2[1], r2[2], r2[3]
            a = first_max(ohg, lg[:, :, 0:4], gmax, a)
            b1 = V.do(lambda e: e.tensor_tensor(eg, lg[:, :, 0:4], bc(gmax), ALU.subtract))
            e1 = S.do(lambda e: e.activation(eg, eg, ACT.Exp), b1)
            a = V.do(lambda e: e.tensor_tensor(
                pick, lg[:, :, 4:20].rearrange("p t (g j) -> p t g j", g=4),
                ohg.unsqueeze(3).broadcast_to([128, 2, 4, 4]), ALU.mult), a)
            a = V.do(lambda e: e.tensor_reduce(le, pick.rearrange("p t g j -> p t j g"), AX.X, ALU.add), a)
            a = first_max(oh1, le, m1, a)
            b1 = V.do(lambda e: e.tensor_tensor(w4, le, bc(m1), ALU.subtract))
            e2 = S.do(lambda e: e.activation(w4, w4, ACT.Exp), b1)
            a = V.do(lambda e: e.scalar_tensor_tensor(le2, oh1, -BIG, le, ALU.mult, ALU.add), a)
            a = first_max(oh2, le2, m2, a)
            a = V.do(lambda e: e.tensor_tensor(oh1, oh1, oh2, ALU.add), a)
            a = V.do(lambda e: e.tensor_tensor(w4, w4, oh1, ALU.mult), a, e2)
            b1 = V.do(lambda e: e.tensor_reduce(gs, eg, AX.X, ALU.add), e1)
            a = V.do(lambda e: e.tensor_reduce(m1, w4, AX.X, ALU.add), a)
            a = V.do(lambda e: e.tensor_tensor(m1, m1, gs, ALU.mult), a, b1)
            a = V.do(lambda e: e.reciprocal(m2, m1), a)
            a = V.do(lambda e: e.tensor_tensor(w4, w4, bc(m2), ALU.mult), a)
            a = V.do(lambda e: e.tensor_tensor(
                gate.rearrange("p t (g j) -> p t g j", g=4), ohg.unsqueeze(3).broadcast_to([128, 2, 4, 4]),
                w4.unsqueeze(2).broadcast_to([128, 2, 4, 4]), ALU.mult), a)
            bk = work.take()
            PE.wait(bk.free, a)
            for t in range(2):
                d = PE.do(lambda e, b=bk.ap, t=t: e.transpose(b[0:16, t * 128:t * 128 + 128], gate[:, t, :], ident),
                          inc=(t == 1))
            T_gT = V.do(lambda e, b=bk.ap: e.tensor_copy(gT[0:16, :], b[0:16, 0:256]), d)
            bk.free = [T_gT]

            def down(ex, hd, toks_h):
                sl, wt = stream((lambda a: a[:, 0:4096].rearrange("p (c n) -> p c n", c=4),
                                 ins["moe_w_down_2"][i, ex].rearrange("(c p) n -> p c n", p=128)))
                wv = wview(sl, 4, 1024)
                PE.wait(wt, *toks_h)
                if ex == 0:
                    PE.wait(*[b.free for b in acc])
                for f in range(4):
                    for o in range(4):
                        t, hf = o // 2, o % 2
                        d = PE.do(lambda e, o=o, t=t, hf=hf, f=f, wv=wv, hd=hd.ap: e.matmul(
                            acc[o].ap[:, :], hd[:, f * 256 + t * 128:f * 256 + t * 128 + 128],
                            wv[:, f, hf * 512:hf * 512 + 512], start=(ex == 0 and f == 0),
                            stop=(ex == 15 and f == 3)), inc=(f == 3 and o == 3))
                sl.free = [d]
                hd.free = [d]
                return d

            prev = None
            for ex in range(16):
                hd = hds.take()
                sg, gt_ = stream(cols(ins["moe_w_gate_2"][i, ex], KC, 0, 512))
                su, ut_ = stream(cols(ins["moe_w_up_2"][i, ex], KC, 0, 512))
                wg, wu = wview(sg, KC, 512), wview(su, KC, 512)
                bk = work.take()
                d = PE.do(lambda e, b=bk.ap, ex=ex: e.matmul(
                    b[:, 0:256], ident[0:16, ex:ex + 1].broadcast_to([16, 128]), gT[0:16, :], start=True, stop=True),
                    bk.free, T_gT)
                gbc = gbcs.take()
                kb = S.do(lambda e, b=bk.ap, g=gbc.ap: e.copy(g, b[:, 0:256]), d, gbc.free)
                bk.free = [kb]
                toks_h = []
                for f in range(4):
                    bk = work.take()
                    PE.wait(bk.free, T_xT, gt_, ut_)
                    for gv, wv in ((0, wg), (1, wu)):
                        for k in range(KC):
                            d = PE.do(lambda e, b=bk.ap, gv=gv, wv=wv, k=k, f=f: e.matmul(
                                b[:, gv * 256:gv * 256 + 256], wv[:, k, f * 128:f * 128 + 128], hT[:, k, :],
                                start=(k == 0), stop=(k == KC - 1)), inc=(gv == 1 and k == KC - 1))
                    tm = tms.take()
                    a = S.do(lambda e, b=bk.ap, t=tm.ap: e.activation(t, b[:, 0:256], ACT.Silu), d, tm.free)
                    a = V.do(lambda e, b=bk.ap, t=tm.ap: e.tensor_tensor(t, t, b[:, 256:512], ALU.mult), a)
                    bk.free = [a]
                    k = G.do(lambda e, t=tm.ap, g=gbc.ap, h=hd.ap, f=f: e.tensor_tensor(
                        h[:, f * 256:f * 256 + 256], t, g, ALU.mult), a, kb, hd.free)
                    tm.free = [k]
                    toks_h.append(k)
                gbc.free = [k]
                sg.free = su.free = [d]
                if prev is not None:
                    down(*prev)
                prev = (ex, hd, toks_h)
            d = down(*prev)
            for o in range(4):
                a = add_stats(o // 2, o % 2, acc[o].ap, d)
                acc[o].free = [a]
            return layer_norm(i, 1)

        T_y.clear()
        T_xT = turn(x, hT, T_x3)
        ar_at[0] = 0
        NP = 2600
        pj = ar(2 * NP).rearrange("p (t n) -> p t n", t=2)
        qT2 = ar(6 * T).rearrange("p (c t) -> p c t", c=6)
        xqT = ar(2 * T).rearrange("p (c t) -> p c t", c=2)
        ksT = ar(5 * T).rearrange("p (c t) -> p c t", c=5)
        kwT = ar(5 * T).rearrange("p (c t) -> p c t", c=5)
        kvT = ar(6 * T).rearrange("p (k c t) -> p k c t", k=2, c=3)
        PcT = [z[:, h // 4, (h % 4) * T:(h % 4) * T + T] if h < 8 else hT[:, h - 8, :] for h in range(12)]
        PcT2 = [z[:, c // 2, (c % 2) * 512:(c % 2) * 512 + 512].rearrange("p (h t) -> p h t", h=2) if c < 4
                else hT[:, 2 * c - 8:2 * c - 6, :] for c in range(6)]
        tmp4 = [sm(96) for _ in range(4)]
        pv = []

        T_ar = [T_x3[-1]]
        w_n = ins["nsa_w_in_2"][0]
        for c in range(6):
            n = 512 if c < 5 else 36

            def keep_pj(t, b, tok, c=c, n=n):
                k = evac(pj[:, t, c * 512:c * 512 + n], b[:, 0:n], [tok, *T_ar])
                pv.append(k)
                return k

            lin_tok(hT, T_xT, KC, w_n, c * 512, n, keep_pj)
        for t in range(2):
            h12 = pj[:, t, 0:768].rearrange("p (h d) -> p h d", h=12)
            tq = [a.rearrange("p (h d) -> p h d", h=12) for a in tmp4]
            k = rope(h12[:, :, 0:8], h12[:, :, 8:16], t, 0, 8, [12], tq, pv)
            for b0 in (1280, 1792):
                h4 = pj[:, t, b0:b0 + 256].rearrange("p (h d) -> p h d", h=4)
                tk = [a[:, 0:32].rearrange("p (h d) -> p h d", h=4) for a in tmp4]
                k = rope(h4[:, :, 0:8], h4[:, :, 8:16], t, 0, 8, [4], tk, None)
        sgt = sm(72).rearrange("p (t n) -> p t n", t=2)
        T_gate = S.do(lambda e: e.activation(sgt, pj[:, :, 2304:2340], ACT.Sigmoid), pv)
        T_q = turn_cols(pj, 0, 6, qT2, k, -0.125)
        T_ks = turn_cols(pj, 1280 - 64, 5, ksT, k, None, 64)
        T_kw = turn_cols(pj, 1792 - 64, 5, kwT, k, None, 64)
        T_xq = turn_cols(pj, 2340, 2, xqT, pv, -0.125)
        T_pe = G.do(lambda e: e.memset(kvT[:, :, 2, :], 0.0), T_ar)
        T_kc = turn_cols(pj, 768, 2, kvT[:, 0, :, :], pv) + turn_cols(pj, 1024, 2, kvT[:, 1, :, :], pv)
        T_kc.append(V.do(lambda e: e.tensor_copy(kvT[:, :, 2, 0:32], peT.rearrange("p (k l) -> p k l", k=2)), T_pe, T_peT))

        hs = sm(90).rearrange("p (k n) -> p k n", k=2)
        hid = sm(120).rearrange("p (k f n) -> p k f n", k=2, f=2)
        kcp = ar(384)
        kcm = [kcp[:, 64:320].rearrange("p (h d) -> p h d", h=4), ar(256).rearrange("p (h d) -> p h d", h=4)]
        kcT = sm(75).rearrange("p (h n) -> p h n", h=5)
        T_pad = [G.do(lambda e, a=a: e.memset(kcp[:, a:a + 64], 0.0), T_ar) for a in (0, 320)]
        T_cm = []
        for kv in range(2):
            src = ins["nsa_cmp_w1_2"][0, kv].rearrange("(l d) h -> d l h", d=64)
            sl, wt = stream(*[(lambda a, hf=hf: a[hf * 64:hf * 64 + 64, :].rearrange("p (l h) -> p l h", l=32), src)
                              for hf in range(2)])
            wv = wview(sl, 32, 128)
            b2 = [work.take(), work.take()]
            PE.wait(wt, T_kc, b2[0].free, b2[1].free)
            for l in range(32):
                for hf in range(2):
                    d = PE.do(lambda e, b=b2[hf].ap, hf=hf, l=l, kv=kv, wv=wv: e.matmul(
                        b[:, 0:45].rearrange("p (c n) -> p c n", c=3), wv[hf * 64:hf * 64 + 64, l, :],
                        kvT[hf * 64:hf * 64 + 64, kv, :, l:l + 225:16], start=(l == 0), stop=(l == 31)),
                        inc=(l == 31))
            sl.free = [d]
            for hf in range(2):
                a = V.do(lambda e, b=b2[hf].ap, hf=hf: e.tensor_copy(hs[:, hf, :], b[:, 0:45]), d)
                b2[hf].free = [a]
                a = S.do(lambda e, hf=hf, kv=kv: e.activation(hid[:, kv, hf, :], hs[:, hf, 0:30], ACT.Silu,
                                                             bias=hs[:, hf, 30:31]), a)
            V.wait(a)
            bk = work.take()
            PE.wait(a, bk.free, T_small)
            for h in range(4):
                d = PE.do(lambda e, b=bk.ap, h=h, kv=kv: e.matmul(
                    b[0:NCMP, h * 64:h * 64 + 64], hid[:, kv, h % 2, (h // 2) * 15:(h // 2) * 15 + 15], w2c[:, kv, :],
                    start=True, stop=True), inc=(h == 3))
            a = V.do(lambda e, b=bk.ap, kv=kv: e.tensor_copy(
                kcm[kv][0:NCMP, :, :], b[0:NCMP, 0:256].rearrange("p (h d) -> p h d", h=4)), d)
            bk.free = [a]
            T_cm.append(a)
        tk = [a[0:NCMP, 0:32].rearrange("p (h d) -> p h d", h=4) for a in tmp4]
        a = rope(kcm[0][0:NCMP, :, 0:8], kcm[0][0:NCMP, :, 8:16], 2, 0, 8, [4], tk, T_cm, NCMP)
        bk = work.take()
        PE.wait(bk.free, a, T_pad)
        for h in range(5):
            d = PE.do(lambda e, b=bk.ap, h=h: e.transpose(
                b[:, h * 15:h * 15 + 15], kcp[0:NCMP, h * 64:h * 64 + 128], ident[0:NCMP, 0:NCMP]), inc=(h == 4))
        T_kcT = V.do(lambda e, b=bk.ap: e.tensor_copy(kcT, b[:, 0:75].rearrange("p (h n) -> p h n", h=5)), d)
        bk.free = [T_kcT]

        pc = [ar(180).rearrange("p (h n) -> p h n", h=12) for _ in range(2)]
        cm = sm(48).rearrange("p (q h) -> p q h", q=4)
        T_pc = []
        for t in range(2):
            b2 = [work.take(), work.take()]
            PE.wait(b2[0].free, b2[1].free, T_q, T_kcT)
            for h in range(12):
                r = 64 * (h % 2)
                d = PE.do(lambda e, b=b2[h % 2].ap, h=h, r=r, t=t: e.matmul(
                    b[:, (h // 2) * 15:(h // 2) * 15 + 15], qT2[r:r + 64, h // 2, t * 128:t * 128 + 128],
                    kcT[r:r + 64, h // 3 + 1 - h % 2, :], start=True, stop=True), inc=(h >= 10))
            ok = cok[:, t, :].unsqueeze(1)
            for q in range(2):
                pq = pc[t].rearrange("p (c q) n -> p c q n", q=2)[:, :, q, :]
                a = V.do(lambda e, b=b2[q].ap, pq=pq: e.tensor_scalar(
                    pq, b[:, 0:90].rearrange("p (c n) -> p c n", c=6), -1.0, None, ALU.mult), d)
                b2[q].free = [a]
            okb = ok.broadcast_to([128, 12, NCMP])
            p3 = pc[t]
            a = V.do(lambda e, p3=p3, t=t: e.tensor_tensor(
                p3, p3, cbias[:, t, :].unsqueeze(1).broadcast_to([128, 12, NCMP]), ALU.add), a, T_cb)
            a = V.do(lambda e, p3=p3: e.tensor_reduce(cm[:, 0, :], p3, AX.X, ALU.max), a)
            a = V.do(lambda e, p3=p3: e.tensor_tensor(
                p3, p3, cm[:, 0, :].unsqueeze(2).broadcast_to([128, 12, NCMP]), ALU.subtract), a)
            a = S.do(lambda e, p3=p3: e.activation(p3, p3, ACT.Exp), a)
            a = V.do(lambda e, p3=p3, okb=okb: e.tensor_tensor(p3, p3, okb, ALU.mult), a)
            a = V.do(lambda e, p3=p3: e.tensor_reduce(cm[:, 1, :], p3, AX.X, ALU.add), a)
            a = V.do(lambda e: e.tensor_scalar(cm[:, 1, :], cm[:, 1, :], 1e-30, None, ALU.max), a)
            a = V.do(lambda e: e.reciprocal(cm[:, 2, :], cm[:, 1, :]), a)
            g3 = sgt[:, t, :].rearrange("p (h b) -> p h b", b=3)
            a = V.do(lambda e, g3=g3: e.tensor_tensor(cm[:, 3, :], cm[:, 2, :], g3[:, :, 0], ALU.mult), a, T_gate)
            a = V.do(lambda e, p3=p3: e.tensor_tensor(
                p3, p3, cm[:, 3, :].unsqueeze(2).broadcast_to([128, 12, NCMP]), ALU.mult), a)
            T_pc.append(a)
        for c in range(6):
            bk = work.take()
            PE.wait(bk.free, T_pc)
            for q in range(4):
                h, t = 2 * c + q // 2, q % 2
                d = PE.do(lambda e, b=bk.ap, q=q, h=h, t=t: e.transpose(
                    b[0:NCMP, q * 128:q * 128 + 128], pc[t][:, h, :], ident), inc=(q == 3))
            T_PcT = evac(PcT2[c][0:NCMP, :, :],
                         bk.ap[0:NCMP, :].rearrange("p (h t) -> p h t", h=2), d)
            bk.free = [T_PcT]
            pv.append(T_PcT)

        def nsa(h, t):
            mk, w = msk(t)
            r, c, kv = 64 * (h % 2), h // 2, h // 3
            q = qT2[r:r + 64, c, t * 128:t * 128 + 128]
            return dict(
                S=[(q, ksT[r:r + 64, kv + 1 - h % 2, 0:w], w, mk, sgt[:, t, 3 * h + 1:3 * h + 2]),
                   (q, kwT[r:r + 64, kv + 1 - h % 2, 0:w], w, mk, sgt[:, t, 3 * h + 2:3 * h + 3])],
                v=[[pj[:, s, 1536 + kv * 64:1536 + kv * 64 + 64] for s in range(2)],
                   [pj[:, s, 2048 + kv * 64:2048 + kv * 64 + 64] for s in range(2)]],
                extra=[(kcm[1][0:NCMP, kv, :], PcT[h][0:NCMP, t * 128:t * 128 + 128])])

        def mix_out(p, b, tok):
            k = evac(yT[:, p, :], b[:, 0:256], tok)
            T_y.append(k)
            return k

        V.wait(T_gate)
        attention(pair_jobs(12, nsa), [*T_q, *T_ks, *T_kw, *pv, *T_cm, *T_kc], mix_out)
        cross(0, xqT, T_xq)

        def join(i):
            def use(t, hf, b, tok):
                return add_stats(t, hf, b, tok)
            out_proj(yT, list(T_y), ins["w_out_2"][i], use)
            return layer_norm(i, 0)

        T_xa = join(0)
        T_mixed = list(T_xa)

        ar_at[0] = 0
        hds = Ring([Place(ar(1024)) for _ in range(2)])
        gbcs = Ring([Place(ar(256)) for _ in range(2)])
        tms = Ring([Place(ar(256)) for _ in range(3)])
        gT = ar(256)
        T_xb = moe(0, T_xa)

        T_y.clear()
        T_xT = turn(x, hT, T_xb)
        ar_at[0] = 0
        pm = ar(2 * 672).rearrange("p (t n) -> p t n", t=2)
        cqT = ar(2 * T).rearrange("p (c t) -> p c t", c=2)
        ckT = ar(T).rearrange("p (c t) -> p c t", c=1)
        xqT2 = ar(2 * T).rearrange("p (c t) -> p c t", c=2)
        qks = [Place(ar(768).rearrange("p (t h d) -> p t h d", t=2, h=4)) for _ in range(2)]
        trq = [ar(64).rearrange("p (h d) -> p h d", h=4) for _ in range(4)]
        vm = ar(2 * 768).rearrange("p (t h d) -> p t h d", t=2, h=12)
        qT3 = ar(12 * T).rearrange("p (h t) -> p h t", h=12)
        kT3 = ar(12 * T).rearrange("p (h t) -> p h t", h=12)
        assert ar_at[0] <= 12360
        pv2 = []
        w_m = ins["mla_w_in_2"][0]
        for n0, n in ((0, 512), (512, 160)):
            def keep_pm(t, b, tok, n0=n0, n=n):
                k = evac(pm[:, t, n0:n0 + n], b[:, 0:n], [tok, *T_xb])
                pv2.append(k)
                return k
            lin_tok(hT, T_xT, KC, w_m, n0, n, keep_pm)
        sqm = sm(4).rearrange("p (n t) -> p n t", n=2)
        rsm = sm(4).rearrange("p (n t) -> p n t", n=2)
        jk = Lb.take()
        S.wait(jk.free)
        for t in range(2):
            for n, (c0, w) in enumerate(((0, 256), (256, 128))):
                a = S.do(lambda e, t=t, n=n, c0=c0, w=w: e.activation(
                    jk.ap[:, 0:w], pm[:, t, c0:c0 + w], ACT.Square, accum_out=sqm[:, n, t:t + 1]), pv2)
        jk.free = [a]
        r0 = rsqrt(rsm[:, 0, :], sqm[:, 0, :], 1e-6, 1.0 / 256, a)
        r1 = rsqrt(rsm[:, 1, :], sqm[:, 1, :], 1e-6, 1.0 / 128, a)
        for t in range(2):
            V.do(lambda e, t=t: e.tensor_scalar(pm[:, t, 0:256], pm[:, t, 0:256], rsm[:, 0, t:t + 1], None, ALU.mult), r0)
            kn = V.do(lambda e, t=t: e.tensor_scalar(pm[:, t, 256:384], pm[:, t, 256:384], rsm[:, 1, t:t + 1], None,
                                                     ALU.mult), r1)
        tr = [tmp4[i][:, 0:16] for i in range(4)]
        for t in range(2):
            kr = rope(pm[:, t, 384:400], pm[:, t, 400:416], t, 8, 24, [], tr, pv2)
        T_xq2 = turn_cols(pm, 416, 2, xqT2, pv2, -0.125)
        T_cq = []
        bk = work.take()
        PE.wait(bk.free, kn)
        for q in range(4):
            d = PE.do(lambda e, b=bk.ap, q=q: e.transpose(
                b[:, q * 128:q * 128 + 128], pm[:, q % 2, (q // 2) * 128:(q // 2) * 128 + 128], ident), inc=(q == 3))
        for c in range(2):
            k = V.do(lambda e, b=bk.ap, c=c: e.tensor_scalar(
                cqT[:, c, :], b[:, c * 256:c * 256 + 256], colv[:, QN + c:QN + c + 1], None, ALU.mult), d)
        bk.free = [k]
        T_cq.append(k)
        bk = work.take()
        PE.wait(bk.free)
        for q in range(2):
            d = PE.do(lambda e, b=bk.ap, q=q: e.transpose(
                b[:, q * 128:q * 128 + 128], pm[:, q, 256:384], ident), inc=(q == 1))
        k = V.do(lambda e, b=bk.ap: e.tensor_scalar(
            ckT[:, 0, :], b[:, 0:256], colv[:, KN:KN + 1], None, ALU.mult), d)
        bk.free = [k]
        T_ck = [k]

        slq, qt_ = stream((lambda a: a[:, 0:2304].rearrange("p (c n) -> p c n", c=2),
                           ins["mla_w_uq_2"][0].rearrange("(c p) n -> p c n", p=128)))
        slk, kt_ = stream((lambda a: a[:, 0:1536], ins["mla_w_ukv_2"][0]))
        wq_, wk_ = wview(slq, 2, 1152), slk.ap[:, 0:1536]
        T_q3 = []
        for piece in range(3):
            for kind in range(2):
                qk = qks[kind]
                kt2 = []
                for t in range(2):
                    bk = work.take()
                    if kind == 0:
                        PE.wait(bk.free, qt_, T_cq)
                        for k in range(2):
                            d = PE.do(lambda e, b=bk.ap, k=k, t=t, p=piece: e.matmul(
                                b[:, 0:384], cqT[:, k, t * 128:t * 128 + 128], wq_[:, k, p * 384:p * 384 + 384],
                                start=(k == 0), stop=(k == 1)), inc=(k == 1))
                        slq.free = [d]
                        a = evac(qk.ap[:, t, :, :], bk.ap[:, 0:384].rearrange("p (h d) -> p h d", h=4), [d, *qk.free])
                        bk.free = [a]
                        a = rope(qk.ap[:, t, :, 64:80], qk.ap[:, t, :, 80:96], t, 8, 24, [4],
                                 trq, a)
                        kt2.append(a)
                    else:
                        d = PE.do(lambda e, b=bk.ap, t=t, p=piece: e.matmul(
                            b[:, :], ckT[:, 0, t * 128:t * 128 + 128], wk_[:, p * 512:p * 512 + 512],
                            start=True, stop=True), bk.free, kt_, T_ck)
                        slk.free = [d]
                        b4 = bk.ap[:, :].rearrange("p (h d) -> p h d", h=4)
                        a1 = S.do(lambda e, b4=b4, t=t, qk=qk: e.copy(qk.ap[:, t, :, 0:64], b4[:, :, 0:64]), d, qk.free)
                        a2 = S.do(lambda e, b4=b4, t=t, p=piece: e.copy(vm[:, t, 4 * p:4 * p + 4, :], b4[:, :, 64:128]))
                        bk.free = [a2]
                        a3 = G.do(lambda e, t=t, qk=qk: e.tensor_copy(
                            qk.ap[:, t, :, 64:96], pm[:, t, 384:416].unsqueeze(1).broadcast_to([128, 4, 32])),
                            kr, qk.free)
                        kt2 += [a2, a3]
                        T_q3.append(a2)
                dst = qT3 if kind == 0 else kT3
                for hh in range(2):
                    bk = work.take()
                    PE.wait(bk.free, kt2)
                    for q in range(4):
                        h, t = 2 * hh + q // 2, q % 2
                        d = PE.do(lambda e, b=bk.ap, q=q, h=h, t=t, qk=qk: e.transpose(
                            b[0:96, q * 128:q * 128 + 128], qk.ap[:, t, h, :], ident), inc=(q == 3))
                    h0 = 4 * piece + 2 * hh
                    a = evac(dst[0:96, h0:h0 + 2, :], bk.ap[0:96, :].rearrange("p (h t) -> p h t", h=2), d,
                             -float(96.0 ** -0.5) if kind == 0 else None)
                    bk.free = [a]
                    T_q3.append(a)
                qk.free = [d]

        def mla(h, t):
            mk, w = msk(t)
            return dict(S=[(qT3[0:96, h, t * 128:t * 128 + 128], kT3[0:96, h, 0:w], w, mk, None)],
                        v=[[vm[:, s, h, :] for s in range(2)]])

        attention(pair_jobs(12, mla), T_q3, mix_out)
        cross(1, xqT2, T_xq2)
        T_xa = join(1)
        T_mixed = list(T_xa)
        T_fin = moe(1, T_xa)

        SP.dma(lambda e: e.dma_start(out[0].rearrange("(t p) d -> p t d", p=128), x[:, :, :]), s_out, T_fin)
        SP.wait((s_out, 16))

        block = ctx.enter_context(nc.Block())

        @block.sync
        def _(e):
            SP.emit(e)

        @block.tensor
        def _(e):
            PE.emit(e)

        @block.vector
        def _(e):
            V.emit(e)

        @block.scalar
        def _(e):
            S.emit(e)

        @block.gpsimd
        def _(e):
            G.emit(e)


_INS = ["x", "p", "rel_bias", "g_mix_pre", "g_mix_post", "g_ffn_pre", "g_ffn_post", "w_in", "w_pool", "pool_scale",
        "w_out", "w_up", "conv_w", "conv_b", "w_down", "w_ple", "w_ple_gate", "mem_2", "positions_2", "nsa_w_in_2",
        "nsa_cmp_pe_2", "nsa_cmp_w1_2", "nsa_cmp_w2_2", "mla_w_in_2", "mla_q_norm_2", "mla_w_uq_2",
        "mla_kv_norm_2", "mla_w_ukv_2", "mem_w_kv_2", "w_out_2", "ln_g_2", "ln_b_2", "moe_w_grp_2", "moe_b_grp_2",
        "moe_w_exp_2", "moe_b_exp_2", "moe_w_gate_2", "moe_w_up_2", "moe_w_down_2"]


def kernel(**inputs):
    import numpy as _np
    import concourse.bacc as _bacc
    from concourse import mybir as _mybir
    from concourse.bass_utils import run_bass_kernel_spmd as _run

    nc = _bacc.Bacc("TRN2", target_bir_lowering=False, num_devices=1)
    arrays, args = {}, {}

    def give(name, a):
        arrays[name] = a
        return nc.dram_tensor(name, a.shape, _mybir.dt.from_np(a.dtype), kind="ExternalInput").ap()

    for name in _INS:
        args[name] = give(f"in_{name}", _np.ascontiguousarray(inputs[name]))
    cst, onehot = constants()
    cst_d, oh_d = give("const_rows", cst), give("const_onehot", onehot)
    scratch = nc.dram_tensor("bias_rows", (8, 384), F32, kind="Internal").ap()
    out = nc.dram_tensor("out", (1, T, D), F32, kind="ExternalOutput").ap()
    build(nc, args, out, cst_d, oh_d, scratch)
    r = _run(nc, [arrays], core_ids=[0])
    return r.results[0]["out"]
```

```python
from contextlib import ExitStack

import numpy as np

import concourse.bass as bass
from concourse import mybir

F32 = mybir.dt.float32
F32R = mybir.dt.float32r
I32 = mybir.dt.int32
ALU = mybir.AluOpType
ACT = mybir.ActivationFunctionType
AX = mybir.AxisListType

T, D = 256, 1024
KC = 8
BIG = 1.0e30
DFF = 2816
NJ = DFF // 128
ALPHA = 4.0 ** 0.25
CAP = 64
NCMP = 15
TWO_PI_INV = float(np.float32(1.0 / (2.0 * np.pi)))
MAGIC = float(1.5 * 2.0 ** 23)


def two_pi_parts():
    parts, rest = [], 2.0 * np.pi
    for _ in range(4):
        m, e = np.frexp(rest)
        p = np.ldexp(np.floor(m * 512.0) / 512.0, e)
        parts.append(float(p))
        rest -= p
    return parts


def constants():
    ident = np.eye(128, dtype=np.float32)
    p = np.arange(128)[:, None]
    s = np.arange(256)[None, :]
    causal = np.where(s - 128 <= p, 0.0, BIG).astype(np.float32)
    j = np.arange(384)
    dist = 255 - j
    n = np.maximum(dist, 0)
    nf = np.maximum(n, 1).astype(np.float32)
    large = 16 + (np.log(nf / np.float32(16)) / np.float32(np.log(8.0)) * np.float32(16)).astype(np.int32)
    bucket = np.where(n < 16, n, np.minimum(large, 31))
    onehot = np.zeros((33, 384), np.float32)
    ok = dist >= 0
    onehot[bucket[ok], j[ok]] = -1.0
    onehot[32, ~ok] = BIG
    cnt = np.zeros((4, 16), np.float32)
    for g, w in enumerate((2, 4, 8, 16)):
        cnt[g] = np.float32(1.0) / np.minimum(np.arange(16) + 1, w).astype(np.float32)
    inv = np.concatenate([
        np.float32(500000.0) ** (-np.arange(0, 16, 2, dtype=np.float32) / np.float32(16)),
        np.float32(10000.0) ** (-np.arange(0, 32, 2, dtype=np.float32) / np.float32(32)),
    ]).astype(np.float32)
    end = np.arange(NCMP) * 16 + 31
    t = np.arange(256)
    cok = (end[None, :] <= t[:, None]).astype(np.float32).reshape(2, 128, NCMP).transpose(1, 0, 2)
    rank = np.array([4.0, 3.0, 2.0, 1.0], np.float32)
    row = np.concatenate([inv, cnt.reshape(-1), rank])
    row = np.broadcast_to(row, (128, row.size))
    return np.ascontiguousarray(np.concatenate(
        [ident, causal, np.ascontiguousarray(cok).reshape(128, 30), row, ident[::-1],
         (p < np.arange(128)[None, :]).astype(np.float32), np.ones((128, 128), np.float32),
         np.broadcast_to(np.arange(CAP, dtype=np.float32) - 1000.0, (128, CAP)),
         np.concatenate([np.eye(CAP)] * 2)], axis=1), np.float32), onehot


C_ID, C_MASK, C_COK, C_INV, C_CNT, C_RANK, C_FLIP, C_UP, C_ONE, C_IOTA = 0, 128, 384, 414, 438, 502, 506, 634, 762, 890
C_TWO = C_IOTA + CAP
C_ALL = C_TWO + CAP


class Queue:

    def __init__(self, sem, serial=False):
        self.sem, self.count, self.ops, self.seen = sem, 0, [], {}
        self.serial = serial

    def wait(self, *toks):
        for tok in toks:
            if tok is None:
                continue
            if isinstance(tok, list):
                self.wait(*tok)
                continue
            sem, n = tok
            if self.seen.get(sem.name, 0) < n:
                self.seen[sem.name] = n
                self.ops.append(("wait", sem, n))

    def do(self, fn, *toks, inc=True):
        self.wait(*toks)
        if self.serial and self.count:
            self.wait((self.sem, self.count))
        if not inc:
            self.ops.append(("op", fn, None, 0))
            return None
        self.count += 1
        self.ops.append(("op", fn, self.sem, 1))
        return (self.sem, self.count)

    def dma(self, fn, sem, *toks):
        self.wait(*toks)
        self.ops.append(("op", fn, sem, 16))

    def emit(self, eng, ops=None):
        for op in self.ops if ops is None else ops:
            if op[0] == "wait":
                eng.wait_ge(op[1], op[2])
            elif op[0] == "branch":
                n = eng.value_load(op[1], min_val=0, max_val=T)
                with eng.If(n <= CAP):
                    self.emit(eng, op[2])
                with eng.Else():
                    self.emit(eng, op[3])
            elif op[0] == "level":
                eng.drain()
                eng.sem_inc(self.sem, op[1])
            else:
                ins = op[1](eng)
                if op[2] is not None:
                    ins.then_inc(op[2], op[3])


class Place:

    made = []

    def __init__(self, ap):
        self.ap, self.free = ap, []
        Place.made.append(self)


class Slot:

    def __init__(self, ap, sems):
        self.ap, self.halves = ap, [Place(ap[:, 0:2048]), Place(ap[:, 2048:4096])]
        for h, s in zip(self.halves, sems):
            h.sem, h.n = s, 0

    def give(self, toks):
        for h in self.halves:
            h.free = list(toks)

    free = property(None, give)


class Ring:
    def __init__(self, places):
        self.places, self.at = places, 0

    def take(self):
        p = self.places[self.at % len(self.places)]
        self.at += 1
        return p


def build(nc, ins, out, const, onehot, scratch):
    ctx = ExitStack()
    Place.made.clear()
    with ctx:
        def sb(name, shape, dt=F32):
            return ctx.enter_context(nc.sbuf_tensor(name, shape, dt))

        def sem(name):
            return ctx.enter_context(nc.semaphore(name))

        PE, V, S, G, SP = (Queue(sem(n)) for n in ("s_pe", "s_dve", "s_act", "s_pool", "s_sp"))
        G.serial = V.serial = S.serial = True
        banks = [Place(ctx.enter_context(nc.psum_tensor(f"ps{i}", [128, 512], F32))) for i in range(8)]
        work = Ring(banks[0:4])
        acc = banks[4:8]

        NSLOT = 5
        slots = []
        for i in range(NSLOT):
            slots.append(Slot(sb(f"w{i}", [128, 4096]), (sem(f"s_wa{i}"), sem(f"s_wb{i}"))))
        wring = Ring(slots)

        ahead = []

        def fetch(units):
            got = [stream(*u, halves=h) for u, h in units]
            ahead.extend(got)

        def fork(count, tok, short, long):
            queues = (PE, V, S, G, SP)
            for q in queues:
                q.wait(tok)
            start = [(q.count, dict(q.seen), q.ops) for q in queues]
            rings = (wring, work, Lb, Pb, Tb)
            at = [r.at for r in rings]
            free = [list(p.free) for p in Place.made]
            n0, pre = [h.n for p in slots for h in p.halves], list(ahead)
            ends = []
            for path in (short, long):
                for q, (c, seen, _) in zip(queues, start):
                    q.count, q.seen, q.ops = c, dict(seen), []
                for r, a in zip(rings, at):
                    r.at = a
                for p, f in zip(Place.made, free):
                    p.free = list(f)
                for h, n in zip([h for p in slots for h in p.halves], n0):
                    h.n = n
                ahead[:] = pre
                path()
                ends.append(([(q.count, q.seen, q.ops) for q in queues], [h.n for p in slots for h in p.halves],
                             wring.at, list(ahead)))
            assert ends[0][1:] == ends[1][1:]
            join = []
            for k, q in enumerate(queues):
                two = [e[0][k] for e in ends]
                q.count = max(c for c, _, _ in two) + 1
                if q is SP:
                    q.count -= 1
                else:
                    for c, _, ops in two:
                        ops.append(("level", q.count - c))
                    join.append((q.sem, q.count))
                q.seen = {n: min(two[0][1][n], two[1][1][n]) for n in two[0][1] if n in two[1][1]}
                q.ops = start[k][2] + [("branch", count, two[0][2], two[1][2])]
            for p in Place.made:
                p.free = list(join)
            return join

        def stream(*parts, halves=False):
            if ahead:
                return ahead.pop(0)
            sl = wring.take()
            toks = []
            for h, (dst, src) in zip(sl.halves, parts):
                SP.dma(lambda e, d=dst(sl.ap), s=src: e.dma_start(d, s), h.sem,
                       h.free if halves else [o.free for o in sl.halves])
                h.n += 16
                toks.append((h.sem, h.n))
            sl.free = []
            return sl, toks

        def cols(w, kc, n0, n):
            return (lambda a: a[:, 0:kc * n].rearrange("p (c n) -> p c n", c=kc),
                    w[:, n0:n0 + n].rearrange("(c p) n -> p c n", p=128))

        def wview(sl, kc, n):
            return sl.ap[:, 0:kc * n].rearrange("p (c n) -> p c n", c=kc)

        x = sb("x", [128, 2, D])
        hT = sb("hT", [128, KC, T])
        yT = sb("yT", [128, KC, T])
        z = sb("z", [128, 2, D])
        cst = sb("cst", [128, C_ALL])
        colv = sb("colv", [128, 112])
        gains = [Place(sb(f"gain{i}", [128, D])) for i in range(2)]
        for i, g in enumerate(gains):
            g.sem, g.n = sem(f"s_g{i}"), 0
        with ExitStack() as same:
            xgr = [same.enter_context(nc.sbuf_tensor(f"xgr{i}", [128, 2048], F32R)) for i in range(2)]
            whr = [same.enter_context(nc.sbuf_tensor(f"whr{i}", [128, 2, 512], F32R)) for i in range(4)]
            wlr = [same.enter_context(nc.sbuf_tensor(f"wlr{i}", [128, 2, 512], F32R)) for i in range(4)]
        arena = sb("arena", [128, 12360])
        Lb = Ring([Place(sb(f"L{i}", [128, 512])) for i in range(2)])
        Pb = Ring([Place(sb(f"P{i}", [128, 512])) for i in range(3)])
        Tb = Ring([Place(sb(f"PT{i}", [128, 512])) for i in range(3)])
        small = sb("small", [128, 1600])
        mkT = sb("mkT", [128, 2, 2, T])
        mv = sb("mv", [128, 2, 2, T])
        wge = sb("wge", [128, 2, KC, 20])
        bge = sb("bge", [128, 2, 20])
        w2c = sb("w2c", [128, 2, 64])

        ident = cst[:, C_ID:C_ID + 128]
        mask = cst[:, C_MASK:C_MASK + 256]
        cok = cst[:, C_COK:C_COK + 30].rearrange("p (t n) -> p t n", t=2)

        sm_at = [0]

        def sm(n):
            a = small[:, sm_at[0]:sm_at[0] + n]
            sm_at[0] += n
            return a

        ar_at = [0]

        def ar(n):
            a = arena[:, ar_at[0]:ar_at[0] + n]
            ar_at[0] += n
            assert ar_at[0] <= 12360
            return a

        G_MIX, G_FFN, PSC, QN, KN, CW, CB = 0, 8, 16, 20, 22, 23, 89

        s_x, s_cst, s_mem, s_small = sem("s_x"), sem("s_cst"), sem("s_mem"), sem("s_small")
        s_early, s_bias, s_out = sem("s_early"), sem("s_bias"), sem("s_out")
        ar_at[0] = 0
        mem = ar(2 * D).rearrange("p (t d) -> p t d", t=2)
        memT = ar(KC * T).rearrange("p (c t) -> p c t", c=KC)
        rows = ar(128)
        relx = ar(8)
        oh = ar(384)
        rb = ar(384)
        pes = ar(128)
        btab = ar(8 * 256).rearrange("p (h s) -> p h s", h=8)
        posi = sm(3).bitcast(I32)

        SP.dma(lambda e: e.dma_start(x[:, :, :], ins["x"][0].rearrange("(t p) d -> p t d", p=128)), s_x)
        SP.dma(lambda e: e.dma_start(mem, ins["mem_2"][0].rearrange("(t p) d -> p t d", p=128)), s_mem)
        S.dma(lambda e: e.dma_start(cst[:, :], const), s_cst)
        early = 0
        at = 0
        for name, view in (("g_mix_pre", 8), ("g_ffn_pre", 8), ("pool_scale", 4), ("mla_q_norm_2", 2),
                           ("mla_kv_norm_2", 1), ("conv_w", 66), ("conv_b", 22)):
            src = ins[name]
            if name == "conv_w":
                src = src[0].rearrange("k (j p) -> (k j) p", p=128)
            else:
                src = src[0].rearrange("(j p) -> j p", p=128)
            S.dma(lambda e, a=at, v=view, s=src: e.dma_start(rows[a:a + v, :], s), s_early)
            at += view
            early += 16
        NROWS = at
        S.dma(lambda e: e.dma_start(relx[0:32, :], ins["rel_bias"]), s_early)
        S.dma(lambda e: e.dma_start(oh[0:33, :], onehot), s_early)
        for k in range(2):
            for h in range(2):
                S.dma(lambda e, k=k, h=h: e.dma_start(pes[32 * k:32 * k + 32, 64 * h:64 * h + 64],
                                                      ins["nsa_cmp_pe_2"][0, k]), s_early)
        early += 16 * 6
        pcol = ins["positions_2"].rearrange("a t -> t a")
        for t in range(2):
            S.dma(lambda e, t=t: e.dma_start(posi[:, t:t + 1], pcol[t * 128:t * 128 + 128, :]), s_early)
        S.dma(lambda e: e.dma_start(posi[0:NCMP, 2:3], pcol[31:256:16, :], allow_slow_non_contiguous=True), s_early)
        early += 16 * 3
        T_early = (s_early, early)
        T_cst, T_x, T_mem = (s_cst, 16), (s_x, 16), (s_mem, 16)

        ns = 0
        for i in range(2):
            S.dma(lambda e, i=i: e.dma_start(wge[:, i, :, 0:4],
                                             ins["moe_w_grp_2"][i].rearrange("(c p) n -> p c n", p=128)), s_small)
            S.dma(lambda e, i=i: e.dma_start(wge[:, i, :, 4:20],
                                             ins["moe_w_exp_2"][i].rearrange("(c p) n -> p c n", p=128)), s_small)
            S.dma(lambda e, i=i: e.dma_start(bge[:, i, 0:4], ins["moe_b_grp_2"][i].partition_broadcast(128)), s_small)
            S.dma(lambda e, i=i: e.dma_start(bge[:, i, 4:20], ins["moe_b_exp_2"][i].partition_broadcast(128)), s_small)
            S.dma(lambda e, i=i: e.dma_start(w2c[:, i, :], ins["nsa_cmp_w2_2"][0, i]), s_small)
            ns += 80
        wpool = ar(4 * 128).rearrange("p (g d) -> p g d", g=4)
        S.dma(lambda e: e.dma_start(wpool, ins["w_pool"][0].rearrange("g c d -> c g d")), s_small)
        ns += 16
        T_small = (s_small, ns)

        def gain(i, row):
            g = gains[i]
            SP.dma(lambda e, a=g.ap, r=row: e.dma_start(a[:, :], r.partition_broadcast(128)), g.sem, g.free)
            g.n += 16
            g.free = []
            return g, (g.sem, g.n)

        half_pow = sm(8)
        k_pow = G.do(lambda e: e.memset(half_pow, -0.5))

        def rsqrt(dst, src, eps, scale, tok):
            a = V.do(lambda e: e.tensor_scalar(dst, src, scale, eps, ALU.mult, ALU.add), tok)
            n = src.shape[-1]
            return G.do(lambda e: e.tensor_tensor(dst, dst, half_pow[:, 0:n], ALU.pow), a, k_pow)

        sq = sm(8)
        rstd = sm(4)
        mean = sm(4)

        flip = [0]

        def evac(dst, src, tok, scale=None, eng=None):
            if eng is None:
                flip[0] ^= 1
                eng = "S" if flip[0] else "V"
            if eng == "S":
                if scale is None:
                    return S.do(lambda e: e.copy(dst, src), tok)
                return S.do(lambda e: e.mul(dst, src, scale), tok)
            if scale is None:
                return V.do(lambda e: e.tensor_copy(dst, src), tok)
            return V.do(lambda e: e.tensor_scalar(dst, src, scale, None, ALU.mult), tok)

        def turn(src, dst, tok, gcol=None, dfree=()):
            toks = []
            for c in range(4):
                bk = work.take()
                PE.wait(tok, bk.free, T_cst)
                for q in range(4):
                    kc, t = 2 * c + q // 2, q % 2
                    d = PE.do(lambda e, b=bk.ap, q=q, kc=kc, t=t: e.transpose(
                        b[:, q * 128:q * 128 + 128], src[:, t, kc * 128:kc * 128 + 128], ident), inc=(q == 3))
                if gcol is None:
                    k = evac(dst[:, 2 * c:2 * c + 2, :], bk.ap[:, :].rearrange("p (c t) -> p c t", c=2), [d, *dfree])
                else:
                    for q in range(2):
                        kc = 2 * c + q
                        k = V.do(lambda e, b=bk.ap, q=q, kc=kc: e.tensor_scalar(
                            dst[:, kc, :], b[:, q * 256:q * 256 + 256], gcol[:, kc:kc + 1], None, ALU.mult),
                            d, T_col, *dfree)
                bk.free = [k]
                toks.append(k)
            return toks

        def rms_turn(src, tok, gcol, dst, dfree=()):
            for t in range(2):
                a = S.do(lambda e, t=t: e.activation(z[:, t, :], src[:, t, :], ACT.Square,
                                                     accum_out=sq[:, t:t + 1]), tok)
            r = rsqrt(rstd[:, 0:2], sq[:, 0:2], 1e-6, 1.0 / D, a)
            for t in range(2):
                k = V.do(lambda e, t=t: e.tensor_scalar(z[:, t, :], src[:, t, :], rstd[:, t:t + 1], None, ALU.mult), r)
            return turn(z, dst, k, gcol, dfree)

        def lin_tok(lT, ltok, kcs, w, n0, n, use):
            sl, wt = stream(cols(w, kcs, n0, n))
            wv = wview(sl, kcs, n)
            for t in range(2):
                bk = work.take()
                PE.wait(ltok, bk.free, wt)
                for k in range(kcs):
                    d = PE.do(lambda e, b=bk.ap, k=k, t=t: e.matmul(
                        b[:, 0:n], lT[:, k, t * 128:t * 128 + 128], wv[:, k, :],
                        start=(k == 0), stop=(k == kcs - 1)), inc=(k == kcs - 1))
                bk.free = [use(t, bk.ap, d)]
            sl.free = [d]
            return d

        def lin_feat(lT, ltok, kcs, w, n0, n, use):
            sl, wt = stream(cols(w, kcs, n0, n))
            wv = wview(sl, kcs, n)
            for c in range(n // 256):
                bk = work.take()
                PE.wait(ltok, bk.free, wt)
                for q in range(2):
                    for k in range(kcs):
                        d = PE.do(lambda e, b=bk.ap, k=k, q=q, c=c: e.matmul(
                            b[:, q * 256:q * 256 + 256], wv[:, k, (2 * c + q) * 128:(2 * c + q) * 128 + 128],
                            lT[:, k, :], start=(k == 0), stop=(k == kcs - 1)), inc=(q == 1 and k == kcs - 1))
                bk.free = [use(c, bk.ap, d)]
            sl.free = [d]
            return d

        def out_proj(lT, ltok, w, use):
            for hf in range(2):
                d = lin_tok(lT, ltok, KC, w, hf * 512, 512, lambda t, b, tok, hf=hf: use(t, hf, b, tok))
            return d

        def rms_add(g, gtok, ytoks, ss):
            a = V.do(lambda e: e.tensor_reduce(sq[:, 4:6], ss, AX.X, ALU.add), ytoks)
            r = rsqrt(rstd[:, 2:4], sq[:, 4:6], 1e-6, 1.0 / D, a)
            res = []
            for t in range(2):
                k = V.do(lambda e, t=t: e.scalar_tensor_tensor(
                    z[:, t, :], z[:, t, :], rstd[:, 2 + t:3 + t], g.ap[:, :], ALU.mult, ALU.mult), r, gtok)
                k2 = G.do(lambda e, t=t: e.tensor_tensor(x[:, t, :], x[:, t, :], z[:, t, :], ALU.add), k)
                res.append(k2)
            g.free = [k]
            return res

        ss4 = sm(4).rearrange("p (t h) -> p t h", t=2)
        def keep_sq(t, hf, b, tok):
            a = V.do(lambda e: e.tensor_copy(z[:, t, hf * 512:hf * 512 + 512], b[:, :]), tok)
            jk = Lb.take()
            k = S.do(lambda e: e.activation(jk.ap[:, :], z[:, t, hf * 512:hf * 512 + 512], ACT.Square,
                                            accum_out=ss4[:, t, hf:hf + 1]), a, jk.free)
            jk.free = [k]
            return k

        st = sm(24).rearrange("p (t h s) -> p t h s", t=2, h=2)
        mvv = sm(4).rearrange("p (t s) -> p t s", t=2)

        def add_stats(t, hf, b, tok):
            a = V.do(lambda e: e.scalar_tensor_tensor(
                z[:, t, hf * 512:hf * 512 + 512], x[:, t, hf * 512:hf * 512 + 512], ALPHA, b[:, :],
                ALU.mult, ALU.add), tok)
            V.do(lambda e: e.bn_stats(st[:, t, hf, :], z[:, t, hf * 512:hf * 512 + 512]), a)
            return a

        def layer_norm(i, jn):
            gg, gt = gain(0, ins["ln_g_2"][i, jn])
            gb, bt = gain(1, ins["ln_b_2"][i, jn])
            stats = (V.sem, V.count)
            res = []
            for t in range(2):
                a = V.do(lambda e, t=t: e.bn_aggr(mvv[:, t, :], st[:, t, :, :].rearrange("p h s -> p (h s)")), stats)
            r = rsqrt(rstd[:, 0:2], mvv[:, :, 1], 1e-5, 1.0, a)
            for t in range(2):
                k = V.do(lambda e, t=t: e.tensor_scalar(z[:, t, :], z[:, t, :], mvv[:, t, 0:1], rstd[:, t:t + 1],
                                                        ALU.subtract, ALU.mult), r)
                k = V.do(lambda e, t=t: e.tensor_tensor(z[:, t, :], z[:, t, :], gg.ap[:, :], ALU.mult), k, gt)
                k2 = G.do(lambda e, t=t: e.tensor_tensor(x[:, t, :], z[:, t, :], gb.ap[:, :], ALU.add), k, bt)
                res.append(k2)
            gg.free, gb.free = [k], [k2]
            return res

        sbank, tbank, obank = Ring(banks[0:3]), Ring(banks[3:6]), Ring(banks[6:8])
        mrs = Ring([Place(sm(6)) for _ in range(4)])

        def attention(jobs, ready, pair_out):
            n = len(jobs)
            for i in range(n + 3):
                if i < n:
                    j = jobs[i]
                    bk = sbank.take()
                    PE.wait(bk.free, ready)
                    for q, (lq, rk, w, mk, gt) in enumerate(j["S"]):
                        d = PE.do(lambda e, b=bk.ap, q=q, lq=lq, rk=rk, w=w: e.matmul(
                            b[:, q * 256:q * 256 + w], lq, rk, start=True, stop=True), inc=(q == len(j["S"]) - 1))
                    Lp, Pp, ms = Lb.take(), Pb.take(), mrs.take()
                    m, rs, rc = ms.ap[:, 0:2], ms.ap[:, 2:4], ms.ap[:, 4:6]
                    ex = []
                    for q, (lq, rk, w, mk, gt) in enumerate(j["S"]):
                        c = slice(q * 256, q * 256 + w)
                        if mk is not None:
                            a = V.do(lambda e, c=c, q=q, mk=mk, L=Lp.ap, b=bk.ap, m=m: e.tensor_tensor_reduce(
                                L[:, c], b[:, c], mk, 1.0, 3.0e38, ALU.add, ALU.min, m[:, q:q + 1]), d, Lp.free, ms.free)
                            src, fin = Lp.ap, a
                        else:
                            a = V.do(lambda e, c=c, q=q, b=bk.ap, m=m: e.tensor_reduce(
                                m[:, q:q + 1], b[:, c], AX.X, ALU.min), d, ms.free)
                            src = bk.ap
                        ex.append(S.do(lambda e, c=c, q=q, s=src, P=Pp.ap, m=m, rs=rs: e.activation(
                            P[:, c], s[:, c], ACT.Exp, bias=m[:, q:q + 1], scale=-1.0,
                            accum_out=rs[:, q:q + 1]), a, Pp.free))
                    bk.free = [a] if j["S"][0][3] is not None else [ex[-1]]
                    Lp.free = [ex[-1]]
                    nq = len(j["S"])
                    j["P"], j["ms"] = Pp, ms
                    j["ex"], j["nq"] = ex[-1], nq
                if 1 <= i <= n:
                    j = jobs[i - 1]
                    rc, rs, nq = j["ms"].ap[:, 4:6], j["ms"].ap[:, 2:4], j["nq"]
                    k = V.do(lambda e, rc=rc, rs=rs, nq=nq: e.reciprocal(rc[:, 0:nq], rs[:, 0:nq]), j["ex"])
                    for q, (lq, rk, w, mk, gt) in enumerate(j["S"]):
                        c = slice(q * 256, q * 256 + w)
                        if gt is None:
                            kk = V.do(lambda e, c=c, q=q, P=j["P"].ap, rc=rc: e.tensor_scalar(
                                P[:, c], P[:, c], rc[:, q:q + 1], None, ALU.mult), k)
                        else:
                            kk = V.do(lambda e, c=c, q=q, P=j["P"].ap, rc=rc, gt=gt: e.tensor_scalar(
                                P[:, c], P[:, c], rc[:, q:q + 1], gt, ALU.mult, ALU.mult), k)
                    j["ms"].free = [kk]
                    j["norm"] = kk
                if 2 <= i <= n + 1:
                    j = jobs[i - 2]
                    bk, Tp = tbank.take(), Tb.take()
                    PE.wait(bk.free, j["norm"])
                    todo = [(q, s) for q, sp in enumerate(j["S"]) for s in range(sp[2] // 128)]
                    for o, (q, s) in enumerate(todo):
                        d = PE.do(lambda e, o=o, q=q, s=s, b=bk.ap, P=j["P"].ap: e.transpose(
                            b[:, o * 128:o * 128 + 128], P[:, q * 256 + s * 128:q * 256 + s * 128 + 128], ident),
                            inc=(o == len(todo) - 1))
                    j["P"].free = [d]
                    w = 128 * len(todo)
                    k = evac(Tp.ap[:, 0:w], bk.ap[:, 0:w], [d, *Tp.free])
                    bk.free = [k]
                    j["T"], j["Tk"], j["todo"] = Tp, k, todo
                if i >= 3:
                    j = jobs[i - 3]
                    if j["first"]:
                        ob = obank.take()
                        PE.wait(ob.free)
                    PE.wait(j["Tk"])
                    hp, t = j["half"] * 64, j["t"]
                    mm = [(j["v"][q][s], j["T"].ap[:, o * 128:o * 128 + 128]) for o, (q, s) in enumerate(j["todo"])]
                    mm += j.get("extra", [])
                    for o, (l, r) in enumerate(mm):
                        d = PE.do(lambda e, o=o, l=l, r=r, b=ob.ap, hp=hp, t=t, n=len(mm): e.matmul(
                            b[hp:hp + 64, t * 128:t * 128 + 128], l, r, start=(o == 0), stop=(o == n - 1)),
                            inc=(o == len(mm) - 1))
                    j["T"].free = [d]
                    if j["last"]:
                        ob.free = [pair_out(j["pair"], ob.ap, d)]

        def pair_jobs(heads, make):
            jobs = []
            for h in range(heads):
                for t in range(2):
                    j = make(h, t)
                    j.update(t=t, half=h % 2, pair=h // 2, first=(h % 2 == 0 and t == 0), last=(h % 2 == 1 and t == 1))
                    jobs.append(j)
            return jobs

        def msk(t):
            return (mask[:, 128:256], 128) if t == 0 else (mask[:, 0:256], 256)

        bk = work.take()
        PE.wait(T_early, T_cst)
        d1 = PE.do(lambda e, b=bk.ap: e.transpose(b[:, 0:NROWS], rows[0:NROWS, :], ident[0:NROWS, 0:NROWS]))
        T_col = V.do(lambda e, b=bk.ap: e.tensor_copy(colv[:, 0:NROWS], b[:, 0:NROWS]), d1)
        bk.free = [T_col]

        ang = sm(72).rearrange("p (k n) -> p k n", k=3)
        trig = sm(144).rearrange("p (q k n) -> p q k n", q=2, k=3)
        kk_ = sm(72).rearrange("p (k n) -> p k n", k=3)
        posf = sm(3)
        inv = cst[:, C_INV:C_INV + 24]
        a0 = V.do(lambda e: e.memset(posf, 0.0))
        V.do(lambda e: e.tensor_copy(posf[:, 0:2], posi[:, 0:2]), T_early, a0)
        a0 = V.do(lambda e: e.tensor_copy(posf[0:NCMP, 2:3], posi[0:NCMP, 2:3]))
        for k in range(3):
            a1 = V.do(lambda e, k=k: e.tensor_scalar(ang[:, k, :], inv, posf[:, k:k + 1], None, ALU.mult), a0, T_cst)
        for q, shift in ((0, 0.25), (1, 0.0)):
            b1 = V.do(lambda e, s=shift: e.tensor_scalar(kk_, ang, TWO_PI_INV, s, ALU.mult, ALU.add), a1)
            b1 = V.do(lambda e: e.tensor_scalar(kk_, kk_, MAGIC, None, ALU.add), b1)
            b1 = V.do(lambda e: e.tensor_scalar(kk_, kk_, MAGIC, None, ALU.subtract), b1)
            cur = ang
            for part in two_pi_parts():
                b1 = V.do(lambda e, q=q, c=cur, p=part: e.scalar_tensor_tensor(
                    trig[:, q, :, :], kk_, -p, c, ALU.mult, ALU.add), b1)
                cur = trig[:, q, :, :]
            if q == 0:
                b1 = V.do(lambda e: e.tensor_scalar(trig[:, 0, :, :], trig[:, 0, :, :], float(np.pi / 2), None,
                                                    ALU.add), b1)
            b1 = V.do(lambda e, q=q: e.tensor_scalar(trig[:, q, :, :], trig[:, q, :, :], 3.14159, -3.14159,
                                                     ALU.min, ALU.max), b1)
        T_trig = S.do(lambda e: e.activation(trig, trig, ACT.Sin), b1)

        def rope(x1, x2, k, lo, hi, heads, tmp, tok, p=128):
            n = hi - lo
            c, s = trig[0:p, 0, k, lo:hi], trig[0:p, 1, k, lo:hi]
            for _ in heads:
                c, s = c.unsqueeze(1), s.unsqueeze(1)
            c, s = c.broadcast_to([p, *heads, n]), s.broadcast_to([p, *heads, n])
            V.wait(tok, T_trig)
            V.do(lambda e: e.tensor_tensor(tmp[0], x1, c, ALU.mult))
            V.do(lambda e: e.tensor_tensor(tmp[1], x2, s, ALU.mult))
            V.do(lambda e: e.tensor_tensor(tmp[2], x1, s, ALU.mult))
            a = V.do(lambda e: e.tensor_tensor(tmp[3], x2, c, ALU.mult))
            V.do(lambda e: e.tensor_tensor(x1, tmp[0], tmp[1], ALU.subtract), a)
            return V.do(lambda e: e.tensor_tensor(x2, tmp[2], tmp[3], ALU.add))

        a = G.do(lambda e: e.memset(relx[32:33, :], 1.0))
        bk = work.take()
        d = PE.do(lambda e, b=bk.ap: e.matmul(b[0:8, 0:384], relx[0:33, :], oh[0:33, :], start=True, stop=True),
                  T_early, a, bk.free)
        k = V.do(lambda e, b=bk.ap: e.tensor_copy(rb[0:8, :], b[0:8, 0:384]), d)
        bk.free = [k]
        S.dma(lambda e: e.dma_start(scratch, rb[0:8, :]), s_bias, k)
        for h in range(8):
            src = bass.AP(scratch.tensor, scratch.offset + h * 384, [[1, 128], [1, 256]])
            S.dma(lambda e, h=h, src=src: e.dma_start(yT[:, h, :], src), s_bias, (s_bias, 16))
        T_bias = []
        for c in range(4):
            bk = work.take()
            d = PE.do(lambda e, b=bk.ap, c=c: e.matmul(
                b[:, :], cst[:, C_FLIP:C_FLIP + 128], yT[:, 2 * c:2 * c + 2, :], start=True, stop=True),
                (s_bias, 16 * 9), T_cst, bk.free)
            k = V.do(lambda e, b=bk.ap, c=c: e.tensor_copy(
                btab[:, 2 * c:2 * c + 2, :], b[:, :].rearrange("p (h s) -> p h s", h=2)), d)
            bk.free = [k]
            T_bias.append(k)

        peT = sm(64)
        bk = work.take()
        d = PE.do(lambda e, b=bk.ap: e.transpose(b[:, 0:64], pes[0:64, :], ident[0:64, 0:64]), bk.free)
        T_peT = V.do(lambda e, b=bk.ap: e.tensor_copy(peT, b[:, 0:64]), d)
        bk.free = [T_peT]
        cbias = sm(30).rearrange("p (t n) -> p t n", t=2)
        T_cb = V.do(lambda e: e.tensor_scalar(cbias, cok, -1.0, BIG, ALU.add, ALU.mult))

        T_hT = rms_turn(x, T_x, colv[:, G_MIX:G_MIX + 8], hT)
        T_memT = turn(mem, memT, T_mem)
        T_mk = []
        for i in range(2):
            w = ins["mem_w_kv_2"][i]

            def keep_k(c, b, tok, i=i):
                k = evac(mkT[:, i, :, :], b[:, :].rearrange("p (c t) -> p c t", c=2), tok)
                T_mk.append(k)
                return k

            def keep_v(t, b, tok, i=i):
                k = evac(mv[:, i, t, :], b[:, 0:256], tok)
                T_mk.append(k)
                return k

            lin_feat(memT, T_memT, KC, w, 0, 256, keep_k)
            T_mem_done = lin_tok(memT, T_memT, KC, w, 256, 256, keep_v)

        w_in = ins["w_in"][0]
        uT = ar(4 * T).rearrange("p (g t) -> p g t", g=4)
        pA = ar(T)
        pB = ar(T)
        qT = ar(4 * T).rearrange("p (g t) -> p g t", g=4)
        kT = ar(4 * T).rearrange("p (g t) -> p g t", g=4)
        vt = ar(2 * 512).rearrange("p (t d) -> p t d", t=2)
        toks = {"u": [], "q": [], "k": [], "v": []}

        def keep(dst, key, scale=None):
            def use(c, b, tok):
                k = evac(dst[:, 2 * c:2 * c + 2, :], b[:, :].rearrange("p (c t) -> p c t", c=2), tok, scale)
                toks[key].append(k)
                return k
            return use

        lin_feat(hT, T_hT, KC, w_in, 512, 512, keep(qT, "q", -0.125))
        lin_feat(hT, T_hT, KC, w_in, 1024, 512, keep(kT, "k"))

        def keep_vt(t, b, tok):
            k = evac(vt[:, t, :], b[:, :], tok)
            toks["v"].append(k)
            return k

        lin_tok(hT, T_hT, KC, w_in, 1536, 512, keep_vt)
        lin_feat(hT, T_hT, KC, w_in, 0, 512, keep(uT, "u"))

        T_y = []

        def moba(h, t):
            w = 128 * (t + 1)
            r, c = 64 * (h % 2), h // 2
            bt = btab[:, h, 128:256] if t == 0 else btab[:, h, :]
            return dict(S=[(qT[r:r + 64, c, t * 128:t * 128 + 128], kT[r:r + 64, c, 0:w], w, bt, None)],
                        v=[[vt[:, s, h * 64:h * 64 + 64] for s in range(2)]])

        def moba_out(p, b, tok):
            k = evac(yT[:, 4 + p, :], b[:, 0:256], tok)
            T_y.append(k)
            return k

        V.wait(T_bias)
        attention(pair_jobs(8, moba), toks["q"] + toks["k"] + toks["v"], moba_out)

        for g in range(4):
            src, tok = uT[:, g, :], toks["u"]
            for s in range(g + 1):
                sh = 1 << s
                dst = (pA, pB)[s % 2]
                k1 = V.do(lambda e, d=dst, c=src, sh=sh: e.tensor_copy(d[:, 0:sh], c[:, 0:sh]), tok)
                k2 = V.do(lambda e, d=dst, c=src, sh=sh: e.tensor_tensor(
                    d[:, sh:T], c[:, sh:T], c[:, 0:T - sh], ALU.add))
                src, tok = dst, [k1, k2]
            cn = cst[:, C_CNT + g * 16:C_CNT + g * 16 + 16]
            V.do(lambda e, c=src, cn=cn: e.tensor_tensor(c[:, 0:16], c[:, 0:16], cn, ALU.mult), tok)
            k1 = V.do(lambda e, c=src, g=g: e.tensor_scalar(c[:, 16:T], c[:, 16:T], 0.5 ** (g + 1), None, ALU.mult))
            k1 = V.do(lambda e, c=src, g=g: e.tensor_tensor(uT[:, g, :], c, uT[:, g, :], ALU.subtract), k1)
            bk = work.take()
            d = PE.do(lambda e, b=bk.ap, g=g: e.matmul(b[:, 0:256], wpool[:, g, :], uT[:, g, :], start=True, stop=True),
                      k1, T_small, bk.free)
            k = S.do(lambda e, b=bk.ap, g=g: e.mul(yT[:, g, :], b[:, 0:256], colv[:, PSC + g:PSC + g + 1]), d, T_col)
            bk.free = [k]
            T_y.append(k)

        g0, gt0 = gain(0, ins["g_mix_post"][0])
        yk = []

        def keep_y(t, hf, b, tok):
            k = keep_sq(t, hf, b, tok)
            yk.append(k)
            return k

        out_proj(yT, T_y, ins["w_out"][0], keep_y)
        T_x1 = rms_add(g0, gt0, yk, ss4)

        T_h2 = rms_turn(x, T_x1, colv[:, G_FFN:G_FFN + 8], hT)
        ar_at[0] = 0
        h2T = ar(NJ * T).rearrange("p (j t) -> p j t", j=NJ)
        cbs = Ring([Place(ar(T)) for _ in range(3)])
        gbs = Ring([Place(ar(T)) for _ in range(2)])
        pT = ar(2 * T).rearrange("p (c t) -> p c t", c=2)
        pin = ar(2 * 256).rearrange("p (t d) -> p t d", t=2)
        sgm = ar(2 * D).rearrange("p (t d) -> p t d", t=2)
        s_p = sem("s_p")
        SP.dma(lambda e: e.dma_start(pin, ins["p"][0, 0].rearrange("(t p) d -> p t d", p=128)), s_p, yk)
        w_up = ins["w_up"][0]
        T_f = []
        for u in range(NJ // 2):
            sl, wt = stream(
                (lambda a: a[:, 0:4096].rearrange("p (c n) -> p c n", c=8)[:, :, 0:256],
                 w_up[:, u * 256:u * 256 + 256].rearrange("(c p) n -> p c n", p=128)),
                (lambda a: a[:, 0:4096].rearrange("p (c n) -> p c n", c=8)[:, :, 256:512],
                 w_up[:, DFF + u * 256:DFF + u * 256 + 256].rearrange("(c p) n -> p c n", p=128)))
            wv = wview(sl, 8, 512)
            for q in range(2):
                j = 2 * u + q
                bk = work.take()
                PE.wait(bk.free, wt, T_h2)
                for gv in range(2):
                    for k in range(KC):
                        d = PE.do(lambda e, b=bk.ap, gv=gv, k=k, q=q, wv=wv: e.matmul(
                            b[:, gv * 256:gv * 256 + 256], wv[:, k, gv * 256 + q * 128:gv * 256 + q * 128 + 128],
                            hT[:, k, :], start=(k == 0), stop=(k == KC - 1)), inc=(gv == 1 and k == KC - 1))
                cb, gb = cbs.take(), gbs.take()
                w = [colv[:, CW + i * NJ + j:CW + i * NJ + j + 1] for i in range(3)]
                bias = colv[:, CB + j:CB + j + 1]
                a = S.do(lambda e, b=bk.ap, c=cb.ap, w=w, bias=bias: e.activation(
                    c, b[:, 0:256], ACT.Identity, bias=bias, scale=w[2]), d, cb.free, yk)
                a = V.do(lambda e, b=bk.ap, c=cb.ap, w=w: e.scalar_tensor_tensor(
                    c[:, 1:T], b[:, 0:T - 1], w[1], c[:, 1:T], ALU.mult, ALU.add), a)
                a = V.do(lambda e, b=bk.ap, c=cb.ap, w=w: e.scalar_tensor_tensor(
                    c[:, 2:T], b[:, 0:T - 2], w[0], c[:, 2:T], ALU.mult, ALU.add), a)
                a = S.do(lambda e, c=cb.ap, g=gb.ap: e.activation(g, c, ACT.Gelu_apprx_tanh), a, gb.free)
                cb.free = [a]
                a = V.do(lambda e, b=bk.ap, g=gb.ap, j=j: e.tensor_tensor(h2T[:, j, :], g, b[:, 256:512], ALU.mult), a)
                gb.free, bk.free = [a], [a]
                T_f.append(a)
            sl.free = [d]

        bk = work.take()
        PE.wait((s_p, 16), bk.free)
        for q in range(4):
            d = PE.do(lambda e, b=bk.ap, q=q: e.transpose(
                b[:, q * 128:q * 128 + 128], pin[:, q % 2, (q // 2) * 128:(q // 2) * 128 + 128], ident), inc=(q == 3))
        T_pT = evac(pT, bk.ap[:, :].rearrange("p (c t) -> p c t", c=2), d)
        bk.free = [T_pT]

        w_down = ins["w_down"][0]
        for u in range(6):
            n = min(4, NJ - 4 * u)
            sl, wt = stream((lambda a, n=n: a[:, 0:n * 1024].rearrange("p (c n) -> p c n", c=n),
                             w_down[u * 512:u * 512 + n * 128, :].rearrange("(c p) n -> p c n", p=128)))
            wv = wview(sl, n, 1024)
            for c in range(n):
                j = 4 * u + c
                PE.wait(wt, T_f[j])
                if j == 0:
                    PE.wait(*[b.free for b in acc])
                for o in range(4):
                    t, hf = o // 2, o % 2
                    d = PE.do(lambda e, o=o, t=t, hf=hf, j=j, c=c, wv=wv: e.matmul(
                        acc[o].ap[:, :], h2T[:, j, t * 128:t * 128 + 128], wv[:, c, hf * 512:hf * 512 + 512],
                        start=(j == 0), stop=(j == NJ - 1)), inc=(o == 3))
            sl.free = [d]
        g1, gt1 = gain(1, ins["g_ffn_post"][0])
        fk = []
        for o in range(4):
            k = keep_sq(o // 2, o % 2, acc[o].ap, d)
            acc[o].free = [k]
            fk.append(k)
        T_x2 = rms_add(g1, gt1, fk, ss4)

        T_x2T = turn(x, hT, T_x2)

        def keep_sg(t, hf, b, tok):
            k = S.do(lambda e: e.activation(sgm[:, t, hf * 512:hf * 512 + 512], b[:, :], ACT.Sigmoid), tok)
            return k

        out_proj(hT, T_x2T, ins["w_ple_gate"][0], keep_sg)
        T_sg = (S.sem, S.count)
        T_x3 = []
        sl, wt = stream((lambda a: a[:, 0:2048].rearrange("p (c n) -> p c n", c=2),
                         ins["w_ple"][0].rearrange("(c p) n -> p c n", p=128)))
        wv = wview(sl, 2, 1024)
        for o in range(4):
            t, hf = o // 2, o % 2
            bk = work.take()
            PE.wait(bk.free, wt, T_pT)
            for k in range(2):
                d = PE.do(lambda e, b=bk.ap, k=k, t=t, hf=hf, wv=wv: e.matmul(
                    b[:, :], pT[:, k, t * 128:t * 128 + 128], wv[:, k, hf * 512:hf * 512 + 512],
                    start=(k == 0), stop=(k == 1)), inc=(k == 1))
            hs = slice(hf * 512, hf * 512 + 512)
            a = V.do(lambda e, b=bk.ap, t=t, hs=hs: e.tensor_tensor(sgm[:, t, hs], sgm[:, t, hs], b[:, :], ALU.mult),
                     d, T_sg)
            bk.free = [a]
            T_x3.append(G.do(lambda e, t=t, hs=hs: e.tensor_tensor(x[:, t, hs], x[:, t, hs], sgm[:, t, hs], ALU.add),
                             a, T_x2T))
        sl.free = [d]

        def cross(i, xqT, tok):
            def make(h, t):
                r, c = 64 * (h % 2), h // 2
                return dict(S=[(xqT[r:r + 64, c, t * 128:t * 128 + 128], mkT[r:r + 64, i, c, :], 256, None, None)],
                            v=[[mv[:, i, s, h * 64:h * 64 + 64] for s in range(2)]])

            def fin(p, b, tok2):
                k = evac(yT[:, 6 + p, :], b[:, 0:256], tok2)
                T_y.append(k)
                return k

            attention(pair_jobs(4, make), [*tok, *T_mk], fin)

        def turn_cols(src, c0, chunks, dst, tok, scale=None, step=128):
            res = []
            for c in range(0, chunks, 2):
                bk = work.take()
                PE.wait(bk.free, tok)
                m = min(2, chunks - c)
                for q in range(2 * m):
                    cc, t = c + q // 2, q % 2
                    a = src[:, t, c0 + cc * step:c0 + cc * step + 128]
                    d = PE.do(lambda e, b=bk.ap, q=q, a=a: e.transpose(b[:, q * 128:q * 128 + 128], a, ident),
                              inc=(q == 2 * m - 1))
                k = evac(dst[:, c:c + m, :], bk.ap[:, 0:m * 256].rearrange("p (c t) -> p c t", c=m), d, scale)
                bk.free = [k]
                res.append(k)
            return res

        lg = sm(40).rearrange("p (t n) -> p t n", t=2)
        eg = sm(8).rearrange("p (t n) -> p t n", t=2)
        ohg = sm(8).rearrange("p (t n) -> p t n", t=2)
        oh1 = sm(8).rearrange("p (t n) -> p t n", t=2)
        oh2 = sm(8).rearrange("p (t n) -> p t n", t=2)
        le = sm(8).rearrange("p (t n) -> p t n", t=2)
        le2 = sm(8).rearrange("p (t n) -> p t n", t=2)
        w4 = sm(8).rearrange("p (t n) -> p t n", t=2)
        c4 = sm(8).rearrange("p (t n) -> p t n", t=2)
        r2 = [sm(2) for _ in range(5)]
        pick = sm(32).rearrange("p (t g j) -> p t g j", t=2, g=4)
        gate = sm(32).rearrange("p (t n) -> p t n", t=2)
        rank = cst[:, C_RANK:C_RANK + 4].unsqueeze(1).broadcast_to([128, 2, 4])

        def bc(a, n=4):
            return a.unsqueeze(2).broadcast_to([128, 2, n])

        def first_max(dst, src, mx, tok):
            a = V.do(lambda e: e.tensor_reduce(mx, src, AX.X, ALU.max), tok)
            a = V.do(lambda e: e.tensor_tensor(c4, src, bc(mx), ALU.is_equal), a)
            a = V.do(lambda e: e.tensor_tensor(c4, c4, rank, ALU.mult), a)
            a = V.do(lambda e: e.tensor_reduce(r2[4], c4, AX.X, ALU.max), a)
            return V.do(lambda e: e.tensor_tensor(dst, c4, bc(r2[4]), ALU.is_equal), a)

        most = sm(1)[0:1, :]
        most_i = sm(1).bitcast(I32)[0:1, :]
        pos = sm(32)

        def moe(i, tok, after):
            T_xT = turn(x, hT, tok)
            bk = work.take()
            PE.wait(bk.free, T_xT, T_small)
            for t in range(2):
                for k in range(KC):
                    d = PE.do(lambda e, b=bk.ap, t=t, k=k: e.matmul(
                        b[:, t * 20:t * 20 + 20], hT[:, k, t * 128:t * 128 + 128], wge[:, i, k, :],
                        start=(k == 0), stop=(k == KC - 1)), inc=(t == 1 and k == KC - 1))
            a = V.do(lambda e, b=bk.ap: e.tensor_tensor(
                lg, b[:, 0:40].rearrange("p (t n) -> p t n", t=2),
                bge[:, i, :].unsqueeze(1).broadcast_to([128, 2, 20]), ALU.add), d)
            bk.free = [a]
            gmax, gs, m1, m2 = r2[0], r2[1], r2[2], r2[3]
            a = first_max(ohg, lg[:, :, 0:4], gmax, a)
            b1 = V.do(lambda e: e.tensor_tensor(eg, lg[:, :, 0:4], bc(gmax), ALU.subtract))
            e1 = S.do(lambda e: e.activation(eg, eg, ACT.Exp), b1)
            a = V.do(lambda e: e.tensor_tensor(
                pick, lg[:, :, 4:20].rearrange("p t (g j) -> p t g j", g=4),
                ohg.unsqueeze(3).broadcast_to([128, 2, 4, 4]), ALU.mult), a)
            a = V.do(lambda e: e.tensor_reduce(le, pick.rearrange("p t g j -> p t j g"), AX.X, ALU.add), a)
            a = first_max(oh1, le, m1, a)
            b1 = V.do(lambda e: e.tensor_tensor(w4, le, bc(m1), ALU.subtract))
            e2 = S.do(lambda e: e.activation(w4, w4, ACT.Exp), b1)
            a = V.do(lambda e: e.scalar_tensor_tensor(le2, oh1, -BIG, le, ALU.mult, ALU.add), a)
            a = first_max(oh2, le2, m2, a)
            a = V.do(lambda e: e.tensor_tensor(oh1, oh1, oh2, ALU.add), a)
            a = V.do(lambda e: e.tensor_tensor(w4, w4, oh1, ALU.mult), a, e2)
            b1 = V.do(lambda e: e.tensor_reduce(gs, eg, AX.X, ALU.add), e1)
            a = V.do(lambda e: e.tensor_reduce(m1, w4, AX.X, ALU.add), a)
            a = V.do(lambda e: e.tensor_tensor(m1, m1, gs, ALU.mult), a, b1)
            a = V.do(lambda e: e.reciprocal(m2, m1), a)
            a = V.do(lambda e: e.tensor_tensor(w4, w4, bc(m2), ALU.mult), a)
            a = V.do(lambda e: e.tensor_tensor(
                gate.rearrange("p t (g j) -> p t g j", g=4), ohg.unsqueeze(3).broadcast_to([128, 2, 4, 4]),
                w4.unsqueeze(2).broadcast_to([128, 2, 4, 4]), ALU.mult), a)
            sel = V.do(lambda e: e.tensor_tensor(
                pick, ohg.unsqueeze(3).broadcast_to([128, 2, 4, 4]), oh1.unsqueeze(2).broadcast_to([128, 2, 4, 4]),
                ALU.mult), a)
            bk = work.take()
            up, one = cst[:, C_UP:C_UP + 128], cst[:, C_ONE:C_ONE + 128]
            PE.wait(bk.free, sel)
            for col, rows_, l, t, first, last in ((0, 128, up, 0, True, True), (16, 128, one, 0, True, False),
                                                  (16, 128, up, 1, False, True), (32, 1, one[:, 0:1], 0, True, False),
                                                  (32, 1, one[:, 0:1], 1, False, True)):
                d = PE.do(lambda e, b=bk.ap, c=col, r=rows_, l=l, t=t, f=first, z_=last: e.matmul(
                    b[0:r, c:c + 16], l, pick[:, t, :, :].rearrange("p g j -> p (g j)"), start=f, stop=z_), inc=last)
            a = V.do(lambda e, b=bk.ap: e.tensor_reduce(most, b[0:1, 32:48], AX.X, ALU.max), d)
            T_most = V.do(lambda e: e.tensor_copy(most_i, most), a)
            T_pos = V.do(lambda e, b=bk.ap: e.scalar_tensor_tensor(
                pos, pick.rearrange("p t g j -> p (t g j)"), -1000.0, b[:, 0:32], ALU.mult, ALU.add), d)
            bk.free = [T_pos]

            order = [("g", 0), ("u", 0)]
            for ex in range(1, 16):
                order += [("g", ex), ("d", ex - 1), ("u", ex)]
            order.append(("d", 15))

            def unit(kind, ex):
                w = ins[{"g": "moe_w_gate_2", "u": "moe_w_up_2", "d": "moe_w_down_2"}[kind]][i, ex]
                n = w.shape[1]
                return [(lambda a, h=h: a[:, h * 2048:h * 2048 + 2048].rearrange("p (c n) -> p c n", n=n),
                         w[h * (w.shape[0] // 2):(h + 1) * (w.shape[0] // 2), :].rearrange("(c p) n -> p c n", p=128))
                        for h in range(2)]

            fetch([(unit(*u), True) for u in order[:NSLOT]])
            todo = list(order)

            def weights(kind, ex):
                assert todo.pop(0) == (kind, ex)
                sl, wt = stream(*unit(kind, ex), halves=True)
                return sl, wt, wview(sl, 4, 1024) if kind == "d" else wview(sl, KC, 512)

            def short():
                todo[:] = order
                ur, yb = Ring(banks[0:2]), banks[2:4]
                P4 = hT[:, :, :].rearrange("p c t -> p (c t)").rearrange("p (t e s) -> p t e s", t=2, e=16)
                Pg4 = z[:, :, :].rearrange("p t (e s) -> p t e s", e=16)
                kP = []
                for t in range(2):
                    io = cst[:, C_IOTA:C_IOTA + CAP].unsqueeze(1).broadcast_to([128, 16, CAP])
                    pt = pos[:, t * 16:t * 16 + 16].unsqueeze(2).broadcast_to([128, 16, CAP])
                    k = V.do(lambda e, t=t, io=io, pt=pt: e.tensor_tensor(P4[:, t], io, pt, ALU.is_equal), T_pos)
                    kP.append(k)
                for t in range(2):
                    gt = gate[:, t, :].unsqueeze(2).broadcast_to([128, 16, CAP])
                    kG = G.do(lambda e, t=t, gt=gt: e.tensor_tensor(Pg4[:, t], P4[:, t], gt, ALU.mult), kP)

                got, bts_of = {}, {}

                def gather(p, hf):
                    if hf == 0:
                        got[p] = (xgs.take(), [])
                    xg, ks = got[p]
                    bk = ur.take()
                    PE.wait(bk.free, kP)
                    for c in range(4):
                        for t in range(2):
                            d = PE.do(lambda e, b=bk.ap, c=c, t=t, kc=4 * hf + c: e.matmul(
                                b[:, c * 128:c * 128 + 128], x[:, t, kc * 128:kc * 128 + 128],
                                P4[:, t, 2 * p:2 * p + 2, :].rearrange("p e s -> p (e s)"),
                                start=(t == 0), stop=(t == 1)), inc=(c == 3 and t == 1))

                    def keep():
                        v = xg.ap.rearrange("p (e k h s) -> p h k e s", e=2, k=KC, h=2)
                        b4 = bk.ap[:, :].rearrange("p (c e s) -> p c e s", c=4, e=2)
                        part = [[v[:, h, 4 * hf:4 * hf + 4, ee, :] for h in range(2)] for ee in range(2)]
                        for ee, (hi, lo) in enumerate(part):
                            k = S.do(lambda e, hi=hi, ee=ee: e.copy(hi, b4[:, :, ee, :]), d, xg.free)
                        V.wait(k)
                        for ee, (hi, lo) in enumerate(part):
                            k = V.do(lambda e, hi=hi, lo=lo, ee=ee: e.tensor_tensor(
                                lo, b4[:, :, ee, :], hi.bitcast(F32), ALU.subtract))
                        bk.free = [k]
                        ks.append(k)

                    return keep

                def way_back(p):
                    bk, bt = ur.take(), bts.take()
                    PE.wait(bk.free, kG)
                    for t in range(2):
                        d = PE.do(lambda e, b=bk.ap, t=t: e.transpose(
                            b[:, t * 128:t * 128 + 128], Pg4[:, t, 2 * p:2 * p + 2, :].rearrange("p e s -> p (e s)"),
                            ident), inc=(t == 1))
                    kb = evac(bt.ap, bk.ap[:, 0:256], [d, *bt.free], eng="S")
                    bk.free = [kb]
                    bts_of[p] = (bt, kb)

                parts, dn, cut = [], {}, [0]

                def split():
                    ex, r = divmod(cut[0], 8)
                    if ex == 16:
                        return
                    kind, j = "gu"[r // 4], r % 4
                    cut[0] += 1
                    if j == 0:
                        if kind == "u" and ex:
                            dn[ex - 1] = weights("d", ex - 1)
                        now[:] = weights(kind, ex)
                    sl, wt, wv = now
                    wt = wt[j // 2]
                    pc = pieces.take()
                    hi, lo = pc.ap
                    src = wv[:, 2 * j:2 * j + 2, :]
                    a = S.do(lambda e: e.copy(hi[:, :, :], src), wt, pc.free)
                    k = V.do(lambda e: e.tensor_tensor(lo[:, :, :], src, hi[:, :, :].bitcast(F32), ALU.subtract), a, wt)
                    if j % 2:
                        sl.halves[j // 2].free = [k]
                    parts.append((pc, k))

                now = []

                def down(ex, hd, kh):
                    sl, wt, wv = dn.pop(ex) if ex in dn else weights("d", ex)
                    r = 64 * (ex % 2)
                    PE.wait(kh)
                    if ex % 2 == 0:
                        PE.wait(yb[0].free, yb[1].free)
                    for f in range(4):
                        PE.wait(wt[f // 2])
                        for hf in range(2):
                            d = PE.do(lambda e, hf=hf, f=f: e.matmul(
                                yb[hf].ap[r:r + 64, :], hd.ap[:, f * CAP:f * CAP + CAP], wv[:, f, hf * 512:hf * 512 + 512],
                                start=(f == 0), stop=(f == 3)), inc=(f % 2 == 1 and hf == 1))
                            if f < 3 or hf == 0:
                                yield
                        if f % 2:
                            sl.halves[f // 2].free = [d]
                    hd.free = [d]
                    if ex % 2:
                        ye = yes.take()
                        ks = []
                        for hf in range(2):
                            k = evac(ye.ap[:, hf * 512:hf * 512 + 512], yb[hf].ap[:, :], [d, *ye.free])
                            yb[hf].free = [k]
                            ks.append(k)
                        ready[ex // 2] = (ye, ks)
                    yield

                ready = {}

                def scatter(p, ye, ky, bt, kb):
                    PE.wait(ky, kb)
                    if p == 0:
                        PE.wait(*[b.free for b in acc])
                    for o in range(4):
                        t, hf = o // 2, o % 2
                        d = PE.do(lambda e, o=o, t=t, hf=hf: e.matmul(
                            acc[o].ap[:, :], bt.ap[:, t * 128:t * 128 + 128], ye.ap[:, hf * 512:hf * 512 + 512],
                            start=(p == 0), stop=(p == 7)), inc=(o == 3))
                    ye.free, bt.free = [d], [d]

                prev = None
                split()
                split()
                keep = gather(0, 0)
                keep2 = gather(0, 1)
                keep()
                keep2()
                split()
                split()
                for ex in range(16):
                    p = ex // 2
                    xg, kx = got[p]
                    raw = []
                    for gv in range(2):
                        bk = ur.take()
                        PE.wait(bk.free)
                        for j in range(4):
                            pc, kp = parts.pop(0)
                            PE.wait(kp, kx[j // 2])
                            for q in range(2):
                                c0 = (ex % 2) * 1024 + (2 * j + q) * 128
                                for w in pc.ap:
                                    d = PE.do(lambda e, b=bk.ap, xg=xg.ap, c0=c0, w=w, q=q, f=(j == 0 and q == 0
                                              and w is pc.ap[0]), z_=(j == 3 and q == 1 and w is pc.ap[1]): e.matmul(
                                        b[:, :], xg[:, c0:c0 + 128], w[:, q, :], start=f, stop=z_),
                                        inc=(q == 1 and w is pc.ap[1]))
                            pc.free = [d]
                            if gv == 0 or j < (3 if ex % 2 else 1):
                                split()
                            if prev is not None:
                                for _ in range((0, 1, 1, 2, 2, 1, 1, 0)[4 * gv + j]):
                                    next(prev)
                        r = (Lb, Pb)[gv].take()
                        k = evac(r.ap[:, :], bk.ap[:, :], [d, *r.free], eng="S")
                        bk.free = [k]
                        raw.append((r, k))
                    if ex % 2:
                        xg.free = [d]
                    more = ex % 2 and p + 1 < 8
                    if more:
                        keep = gather(p + 1, 0)
                        keep()
                    elif ex % 2 == 0:
                        way_back(p)
                        if p:
                            scatter(p - 1, *ready[p - 1], *bts_of[p - 1])
                        split()
                        split()
                    split()
                    bk, hd, tm = ur.take(), hds1.take(), tms1.take()
                    PE.wait(bk.free)
                    for gv, (r, k) in enumerate(raw):
                        PE.wait(k)
                        for f in range(4):
                            d = PE.do(lambda e, b=bk.ap, o=(gv * 4 + f) * CAP, r=r.ap, f=f: e.matmul(
                                b[:, o:o + CAP], r[:, f * 128:f * 128 + 128], cst[:, C_TWO:C_TWO + CAP],
                                start=True, stop=True), inc=(f == 3))
                        r.free = [d]
                    if more:
                        keep = gather(p + 1, 1)
                    a = S.do(lambda e, b=bk.ap, t=tm.ap: e.activation(t, b[:, 0:4 * CAP], ACT.Silu), d, tm.free)
                    a = V.do(lambda e, b=bk.ap, t=tm.ap, h=hd.ap: e.tensor_tensor(
                        h, t, b[:, 4 * CAP:8 * CAP], ALU.mult), a, hd.free)
                    tm.free, bk.free = [a], [a]
                    if more:
                        keep()
                    prev = down(ex, hd, a)
                for _ in prev:
                    pass
                scatter(7, *ready[7], *bts_of[7])
                fetch([(u, False) for u in after])

            def long():
                todo[:] = order
                bk = work.take()
                PE.wait(bk.free)
                for t in range(2):
                    d = PE.do(lambda e, b=bk.ap, t=t: e.transpose(
                        b[0:16, t * 128:t * 128 + 128], gate[:, t, :], ident), inc=(t == 1))
                T_gT = V.do(lambda e, b=bk.ap: e.tensor_copy(gT[0:16, :], b[0:16, 0:256]), d)
                bk.free = [T_gT]

                def down(ex, hd, toks_h, sl, wt, wv):
                    PE.wait(wt, *toks_h)
                    if ex == 0:
                        PE.wait(*[b.free for b in acc])
                    for f in range(4):
                        for o in range(4):
                            t, hf = o // 2, o % 2
                            d = PE.do(lambda e, o=o, t=t, hf=hf, f=f, wv=wv, hd=hd.ap: e.matmul(
                                acc[o].ap[:, :], hd[:, f * 256 + t * 128:f * 256 + t * 128 + 128],
                                wv[:, f, hf * 512:hf * 512 + 512], start=(ex == 0 and f == 0),
                                stop=(ex == 15 and f == 3)), inc=(f == 3 and o == 3))
                    sl.free = [d]
                    hd.free = [d]

                prev = None
                for ex in range(16):
                    hd = hds.take()
                    sg, gt_, wg = weights("g", ex)
                    dw = weights("d", ex - 1) if ex else None
                    su, ut_, wu = weights("u", ex)
                    bk = work.take()
                    d = PE.do(lambda e, b=bk.ap, ex=ex: e.matmul(
                        b[:, 0:256], ident[0:16, ex:ex + 1].broadcast_to([16, 128]), gT[0:16, :],
                        start=True, stop=True), bk.free, T_gT)
                    gbc = gbcs.take()
                    kb = S.do(lambda e, b=bk.ap, g=gbc.ap: e.copy(g, b[:, 0:256]), d, gbc.free)
                    bk.free = [kb]
                    toks_h = []
                    for f in range(4):
                        bk = work.take()
                        PE.wait(bk.free, gt_, ut_)
                        for gv, wv in ((0, wg), (1, wu)):
                            for k in range(KC):
                                d = PE.do(lambda e, b=bk.ap, gv=gv, wv=wv, k=k, f=f: e.matmul(
                                    b[:, gv * 256:gv * 256 + 256], wv[:, k, f * 128:f * 128 + 128], hT[:, k, :],
                                    start=(k == 0), stop=(k == KC - 1)), inc=(gv == 1 and k == KC - 1))
                        tm = tms.take()
                        a = S.do(lambda e, b=bk.ap, t=tm.ap: e.activation(t, b[:, 0:256], ACT.Silu), d, tm.free)
                        a = V.do(lambda e, b=bk.ap, t=tm.ap: e.tensor_tensor(t, t, b[:, 256:512], ALU.mult), a)
                        bk.free = [a]
                        k = G.do(lambda e, t=tm.ap, g=gbc.ap, h=hd.ap, f=f: e.tensor_tensor(
                            h[:, f * 256:f * 256 + 256], t, g, ALU.mult), a, kb, hd.free)
                        tm.free = [k]
                        toks_h.append(k)
                    gbc.free = [k]
                    sg.free = su.free = [d]
                    if prev is not None:
                        down(*prev, *dw)
                    prev = (ex, hd, toks_h)
                down(*prev, *weights("d", 15))
                fetch([(u, False) for u in after])

            ends = fork(most_i, T_most, short, long)
            fin = []
            for o in range(4):
                a = add_stats(o // 2, o % 2, acc[o].ap, ends)
                fin.append(a)
            for o in range(4):
                acc[o].free = [fin[o]]
            return layer_norm(i, 1)

        T_y.clear()
        T_xT = turn(x, hT, T_x3)
        ar_at[0] = 0
        NP = 2600
        pj = ar(2 * NP).rearrange("p (t n) -> p t n", t=2)
        qT2 = ar(6 * T).rearrange("p (c t) -> p c t", c=6)
        xqT = ar(2 * T).rearrange("p (c t) -> p c t", c=2)
        ksT = ar(5 * T).rearrange("p (c t) -> p c t", c=5)
        kwT = ar(5 * T).rearrange("p (c t) -> p c t", c=5)
        kvT = ar(6 * T).rearrange("p (k c t) -> p k c t", k=2, c=3)
        PcT = [z[:, h // 4, (h % 4) * T:(h % 4) * T + T] if h < 8 else hT[:, h - 8, :] for h in range(12)]
        PcT2 = [z[:, c // 2, (c % 2) * 512:(c % 2) * 512 + 512].rearrange("p (h t) -> p h t", h=2) if c < 4
                else hT[:, 2 * c - 8:2 * c - 6, :] for c in range(6)]
        tmp4 = [sm(96) for _ in range(4)]
        pv = []

        T_ar = [T_x3[-1]]
        w_n = ins["nsa_w_in_2"][0]
        for c in range(6):
            n = 512 if c < 5 else 36

            def keep_pj(t, b, tok, c=c, n=n):
                k = evac(pj[:, t, c * 512:c * 512 + n], b[:, 0:n], [tok, *T_ar])
                pv.append(k)
                return k

            lin_tok(hT, T_xT, KC, w_n, c * 512, n, keep_pj)
        for t in range(2):
            h12 = pj[:, t, 0:768].rearrange("p (h d) -> p h d", h=12)
            tq = [a.rearrange("p (h d) -> p h d", h=12) for a in tmp4]
            k = rope(h12[:, :, 0:8], h12[:, :, 8:16], t, 0, 8, [12], tq, pv)
            for b0 in (1280, 1792):
                h4 = pj[:, t, b0:b0 + 256].rearrange("p (h d) -> p h d", h=4)
                tk = [a[:, 0:32].rearrange("p (h d) -> p h d", h=4) for a in tmp4]
                k = rope(h4[:, :, 0:8], h4[:, :, 8:16], t, 0, 8, [4], tk, None)
        sgt = sm(72).rearrange("p (t n) -> p t n", t=2)
        T_gate = S.do(lambda e: e.activation(sgt, pj[:, :, 2304:2340], ACT.Sigmoid), pv)
        T_q = turn_cols(pj, 0, 6, qT2, k, -0.125)
        T_ks = turn_cols(pj, 1280 - 64, 5, ksT, k, None, 64)
        T_kw = turn_cols(pj, 1792 - 64, 5, kwT, k, None, 64)
        T_xq = turn_cols(pj, 2340, 2, xqT, pv, -0.125)
        T_pe = G.do(lambda e: e.memset(kvT[:, :, 2, :], 0.0), T_ar)
        T_kc = turn_cols(pj, 768, 2, kvT[:, 0, :, :], pv) + turn_cols(pj, 1024, 2, kvT[:, 1, :, :], pv)
        T_kc.append(V.do(lambda e: e.tensor_copy(kvT[:, :, 2, 0:32], peT.rearrange("p (k l) -> p k l", k=2)), T_pe, T_peT))

        hs = sm(90).rearrange("p (k n) -> p k n", k=2)
        hid = sm(120).rearrange("p (k f n) -> p k f n", k=2, f=2)
        kcp = ar(384)
        kcm = [kcp[:, 64:320].rearrange("p (h d) -> p h d", h=4), ar(256).rearrange("p (h d) -> p h d", h=4)]
        kcT = sm(75).rearrange("p (h n) -> p h n", h=5)
        T_pad = [G.do(lambda e, a=a: e.memset(kcp[:, a:a + 64], 0.0), T_ar) for a in (0, 320)]
        T_cm = []
        for kv in range(2):
            src = ins["nsa_cmp_w1_2"][0, kv].rearrange("(l d) h -> d l h", d=64)
            sl, wt = stream(*[(lambda a, hf=hf: a[hf * 64:hf * 64 + 64, :].rearrange("p (l h) -> p l h", l=32), src)
                              for hf in range(2)])
            wv = wview(sl, 32, 128)
            b2 = [work.take(), work.take()]
            PE.wait(wt, T_kc, b2[0].free, b2[1].free)
            for l in range(32):
                for hf in range(2):
                    d = PE.do(lambda e, b=b2[hf].ap, hf=hf, l=l, kv=kv, wv=wv: e.matmul(
                        b[:, 0:45].rearrange("p (c n) -> p c n", c=3), wv[hf * 64:hf * 64 + 64, l, :],
                        kvT[hf * 64:hf * 64 + 64, kv, :, l:l + 225:16], start=(l == 0), stop=(l == 31)),
                        inc=(l == 31))
            sl.free = [d]
            for hf in range(2):
                a = V.do(lambda e, b=b2[hf].ap, hf=hf: e.tensor_copy(hs[:, hf, :], b[:, 0:45]), d)
                b2[hf].free = [a]
                a = S.do(lambda e, hf=hf, kv=kv: e.activation(hid[:, kv, hf, :], hs[:, hf, 0:30], ACT.Silu,
                                                             bias=hs[:, hf, 30:31]), a)
            V.wait(a)
            bk = work.take()
            PE.wait(a, bk.free, T_small)
            for h in range(4):
                d = PE.do(lambda e, b=bk.ap, h=h, kv=kv: e.matmul(
                    b[0:NCMP, h * 64:h * 64 + 64], hid[:, kv, h % 2, (h // 2) * 15:(h // 2) * 15 + 15], w2c[:, kv, :],
                    start=True, stop=True), inc=(h == 3))
            a = V.do(lambda e, b=bk.ap, kv=kv: e.tensor_copy(
                kcm[kv][0:NCMP, :, :], b[0:NCMP, 0:256].rearrange("p (h d) -> p h d", h=4)), d)
            bk.free = [a]
            T_cm.append(a)
        tk = [a[0:NCMP, 0:32].rearrange("p (h d) -> p h d", h=4) for a in tmp4]
        a = rope(kcm[0][0:NCMP, :, 0:8], kcm[0][0:NCMP, :, 8:16], 2, 0, 8, [4], tk, T_cm, NCMP)
        bk = work.take()
        PE.wait(bk.free, a, T_pad)
        for h in range(5):
            d = PE.do(lambda e, b=bk.ap, h=h: e.transpose(
                b[:, h * 15:h * 15 + 15], kcp[0:NCMP, h * 64:h * 64 + 128], ident[0:NCMP, 0:NCMP]), inc=(h == 4))
        T_kcT = V.do(lambda e, b=bk.ap: e.tensor_copy(kcT, b[:, 0:75].rearrange("p (h n) -> p h n", h=5)), d)
        bk.free = [T_kcT]

        pc = [ar(180).rearrange("p (h n) -> p h n", h=12) for _ in range(2)]
        cm = sm(48).rearrange("p (q h) -> p q h", q=4)
        T_pc = []
        for t in range(2):
            b2 = [work.take(), work.take()]
            PE.wait(b2[0].free, b2[1].free, T_q, T_kcT)
            for h in range(12):
                r = 64 * (h % 2)
                d = PE.do(lambda e, b=b2[h % 2].ap, h=h, r=r, t=t: e.matmul(
                    b[:, (h // 2) * 15:(h // 2) * 15 + 15], qT2[r:r + 64, h // 2, t * 128:t * 128 + 128],
                    kcT[r:r + 64, h // 3 + 1 - h % 2, :], start=True, stop=True), inc=(h >= 10))
            ok = cok[:, t, :].unsqueeze(1)
            for q in range(2):
                pq = pc[t].rearrange("p (c q) n -> p c q n", q=2)[:, :, q, :]
                a = V.do(lambda e, b=b2[q].ap, pq=pq: e.tensor_scalar(
                    pq, b[:, 0:90].rearrange("p (c n) -> p c n", c=6), -1.0, None, ALU.mult), d)
                b2[q].free = [a]
            okb = ok.broadcast_to([128, 12, NCMP])
            p3 = pc[t]
            a = V.do(lambda e, p3=p3, t=t: e.tensor_tensor(
                p3, p3, cbias[:, t, :].unsqueeze(1).broadcast_to([128, 12, NCMP]), ALU.add), a, T_cb)
            a = V.do(lambda e, p3=p3: e.tensor_reduce(cm[:, 0, :], p3, AX.X, ALU.max), a)
            a = V.do(lambda e, p3=p3: e.tensor_tensor(
                p3, p3, cm[:, 0, :].unsqueeze(2).broadcast_to([128, 12, NCMP]), ALU.subtract), a)
            a = S.do(lambda e, p3=p3: e.activation(p3, p3, ACT.Exp), a)
            a = V.do(lambda e, p3=p3, okb=okb: e.tensor_tensor(p3, p3, okb, ALU.mult), a)
            a = V.do(lambda e, p3=p3: e.tensor_reduce(cm[:, 1, :], p3, AX.X, ALU.add), a)
            a = V.do(lambda e: e.tensor_scalar(cm[:, 1, :], cm[:, 1, :], 1e-30, None, ALU.max), a)
            a = V.do(lambda e: e.reciprocal(cm[:, 2, :], cm[:, 1, :]), a)
            g3 = sgt[:, t, :].rearrange("p (h b) -> p h b", b=3)
            a = V.do(lambda e, g3=g3: e.tensor_tensor(cm[:, 3, :], cm[:, 2, :], g3[:, :, 0], ALU.mult), a, T_gate)
            a = V.do(lambda e, p3=p3: e.tensor_tensor(
                p3, p3, cm[:, 3, :].unsqueeze(2).broadcast_to([128, 12, NCMP]), ALU.mult), a)
            T_pc.append(a)
        for c in range(6):
            bk = work.take()
            PE.wait(bk.free, T_pc)
            for q in range(4):
                h, t = 2 * c + q // 2, q % 2
                d = PE.do(lambda e, b=bk.ap, q=q, h=h, t=t: e.transpose(
                    b[0:NCMP, q * 128:q * 128 + 128], pc[t][:, h, :], ident), inc=(q == 3))
            T_PcT = evac(PcT2[c][0:NCMP, :, :],
                         bk.ap[0:NCMP, :].rearrange("p (h t) -> p h t", h=2), d)
            bk.free = [T_PcT]
            pv.append(T_PcT)

        def nsa(h, t):
            mk, w = msk(t)
            r, c, kv = 64 * (h % 2), h // 2, h // 3
            q = qT2[r:r + 64, c, t * 128:t * 128 + 128]
            return dict(
                S=[(q, ksT[r:r + 64, kv + 1 - h % 2, 0:w], w, mk, sgt[:, t, 3 * h + 1:3 * h + 2]),
                   (q, kwT[r:r + 64, kv + 1 - h % 2, 0:w], w, mk, sgt[:, t, 3 * h + 2:3 * h + 3])],
                v=[[pj[:, s, 1536 + kv * 64:1536 + kv * 64 + 64] for s in range(2)],
                   [pj[:, s, 2048 + kv * 64:2048 + kv * 64 + 64] for s in range(2)]],
                extra=[(kcm[1][0:NCMP, kv, :], PcT[h][0:NCMP, t * 128:t * 128 + 128])])

        def mix_out(p, b, tok):
            k = evac(yT[:, p, :], b[:, 0:256], tok)
            T_y.append(k)
            return k

        V.wait(T_gate)
        attention(pair_jobs(12, nsa), [*T_q, *T_ks, *T_kw, *pv, *T_cm, *T_kc], mix_out)
        cross(0, xqT, T_xq)

        def join(i):
            def use(t, hf, b, tok):
                return add_stats(t, hf, b, tok)
            out_proj(yT, list(T_y), ins["w_out_2"][i], use)
            return layer_norm(i, 0)

        T_xa = join(0)
        T_mixed = list(T_xa)

        ar_at[0] = 0
        hds = Ring([Place(ar(1024)) for _ in range(2)])
        gbcs = Ring([Place(ar(256)) for _ in range(2)])
        tms = Ring([Place(ar(256)) for _ in range(3)])
        gT = ar(256)
        xgs = Ring([Place(a[:, :]) for a in xgr])
        pieces = Ring([Place(a) for a in zip(whr, wlr)])
        yes = Ring([Place(yT[:, 4 * i:4 * i + 4, :].rearrange("p c t -> p (c t)")) for i in range(2)])
        six = [Place(t.ap[:, h:h + 256]) for t in Tb.places for h in (0, 256)]
        bts, hds1, tms1 = Ring(six[0:3]), Ring(six[3:5]), Ring(six[5:6])
        w_m = ins["mla_w_in_2"][0]
        u_uq = (lambda a: a[:, 0:2304].rearrange("p (c n) -> p c n", c=2),
                ins["mla_w_uq_2"][0].rearrange("(c p) n -> p c n", p=128))
        u_ukv = (lambda a: a[:, 0:1536], ins["mla_w_ukv_2"][0])
        T_xb = moe(0, T_xa, [[cols(w_m, KC, 0, 512)], [cols(w_m, KC, 512, 160)], [u_uq], [u_ukv],
                             [cols(ins["w_out_2"][1], KC, 0, 512)]])

        T_y.clear()
        T_xT = turn(x, hT, T_xb)
        ar_at[0] = 0
        pm = ar(2 * 672).rearrange("p (t n) -> p t n", t=2)
        cqT = ar(2 * T).rearrange("p (c t) -> p c t", c=2)
        ckT = ar(T).rearrange("p (c t) -> p c t", c=1)
        xqT2 = ar(2 * T).rearrange("p (c t) -> p c t", c=2)
        qks = [Place(ar(768).rearrange("p (t h d) -> p t h d", t=2, h=4)) for _ in range(2)]
        trq = [ar(64).rearrange("p (h d) -> p h d", h=4) for _ in range(4)]
        vm = ar(2 * 768).rearrange("p (t h d) -> p t h d", t=2, h=12)
        qT3 = ar(12 * T).rearrange("p (h t) -> p h t", h=12)
        kT3 = ar(12 * T).rearrange("p (h t) -> p h t", h=12)
        assert ar_at[0] <= 12360
        pv2 = []
        for n0, n in ((0, 512), (512, 160)):
            def keep_pm(t, b, tok, n0=n0, n=n):
                k = evac(pm[:, t, n0:n0 + n], b[:, 0:n], [tok, *T_xb])
                pv2.append(k)
                return k
            lin_tok(hT, T_xT, KC, w_m, n0, n, keep_pm)
        sqm = sm(4).rearrange("p (n t) -> p n t", n=2)
        rsm = sm(4).rearrange("p (n t) -> p n t", n=2)
        jk = Lb.take()
        S.wait(jk.free)
        for t in range(2):
            for n, (c0, w) in enumerate(((0, 256), (256, 128))):
                a = S.do(lambda e, t=t, n=n, c0=c0, w=w: e.activation(
                    jk.ap[:, 0:w], pm[:, t, c0:c0 + w], ACT.Square, accum_out=sqm[:, n, t:t + 1]), pv2)
        jk.free = [a]
        r0 = rsqrt(rsm[:, 0, :], sqm[:, 0, :], 1e-6, 1.0 / 256, a)
        r1 = rsqrt(rsm[:, 1, :], sqm[:, 1, :], 1e-6, 1.0 / 128, a)
        for t in range(2):
            V.do(lambda e, t=t: e.tensor_scalar(pm[:, t, 0:256], pm[:, t, 0:256], rsm[:, 0, t:t + 1], None, ALU.mult), r0)
            kn = V.do(lambda e, t=t: e.tensor_scalar(pm[:, t, 256:384], pm[:, t, 256:384], rsm[:, 1, t:t + 1], None,
                                                     ALU.mult), r1)
        tr = [tmp4[i][:, 0:16] for i in range(4)]
        for t in range(2):
            kr = rope(pm[:, t, 384:400], pm[:, t, 400:416], t, 8, 24, [], tr, pv2)
        T_xq2 = turn_cols(pm, 416, 2, xqT2, pv2, -0.125)
        T_cq = []
        bk = work.take()
        PE.wait(bk.free, kn)
        for q in range(4):
            d = PE.do(lambda e, b=bk.ap, q=q: e.transpose(
                b[:, q * 128:q * 128 + 128], pm[:, q % 2, (q // 2) * 128:(q // 2) * 128 + 128], ident), inc=(q == 3))
        for c in range(2):
            k = V.do(lambda e, b=bk.ap, c=c: e.tensor_scalar(
                cqT[:, c, :], b[:, c * 256:c * 256 + 256], colv[:, QN + c:QN + c + 1], None, ALU.mult), d)
        bk.free = [k]
        T_cq.append(k)
        bk = work.take()
        PE.wait(bk.free)
        for q in range(2):
            d = PE.do(lambda e, b=bk.ap, q=q: e.transpose(
                b[:, q * 128:q * 128 + 128], pm[:, q, 256:384], ident), inc=(q == 1))
        k = V.do(lambda e, b=bk.ap: e.tensor_scalar(
            ckT[:, 0, :], b[:, 0:256], colv[:, KN:KN + 1], None, ALU.mult), d)
        bk.free = [k]
        T_ck = [k]

        slq, qt_ = stream(u_uq)
        slk, kt_ = stream(u_ukv)
        wq_, wk_ = wview(slq, 2, 1152), slk.ap[:, 0:1536]
        T_q3 = []
        for piece in range(3):
            for kind in range(2):
                qk = qks[kind]
                kt2 = []
                for t in range(2):
                    bk = work.take()
                    if kind == 0:
                        PE.wait(bk.free, qt_, T_cq)
                        for k in range(2):
                            d = PE.do(lambda e, b=bk.ap, k=k, t=t, p=piece: e.matmul(
                                b[:, 0:384], cqT[:, k, t * 128:t * 128 + 128], wq_[:, k, p * 384:p * 384 + 384],
                                start=(k == 0), stop=(k == 1)), inc=(k == 1))
                        slq.free = [d]
                        a = evac(qk.ap[:, t, :, :], bk.ap[:, 0:384].rearrange("p (h d) -> p h d", h=4), [d, *qk.free])
                        bk.free = [a]
                        a = rope(qk.ap[:, t, :, 64:80], qk.ap[:, t, :, 80:96], t, 8, 24, [4],
                                 trq, a)
                        kt2.append(a)
                    else:
                        d = PE.do(lambda e, b=bk.ap, t=t, p=piece: e.matmul(
                            b[:, :], ckT[:, 0, t * 128:t * 128 + 128], wk_[:, p * 512:p * 512 + 512],
                            start=True, stop=True), bk.free, kt_, T_ck)
                        slk.free = [d]
                        b4 = bk.ap[:, :].rearrange("p (h d) -> p h d", h=4)
                        a1 = S.do(lambda e, b4=b4, t=t, qk=qk: e.copy(qk.ap[:, t, :, 0:64], b4[:, :, 0:64]), d, qk.free)
                        a2 = S.do(lambda e, b4=b4, t=t, p=piece: e.copy(vm[:, t, 4 * p:4 * p + 4, :], b4[:, :, 64:128]))
                        bk.free = [a2]
                        a3 = G.do(lambda e, t=t, qk=qk: e.tensor_copy(
                            qk.ap[:, t, :, 64:96], pm[:, t, 384:416].unsqueeze(1).broadcast_to([128, 4, 32])),
                            kr, qk.free)
                        kt2 += [a2, a3]
                        T_q3.append(a2)
                dst = qT3 if kind == 0 else kT3
                for hh in range(2):
                    bk = work.take()
                    PE.wait(bk.free, kt2)
                    for q in range(4):
                        h, t = 2 * hh + q // 2, q % 2
                        d = PE.do(lambda e, b=bk.ap, q=q, h=h, t=t, qk=qk: e.transpose(
                            b[0:96, q * 128:q * 128 + 128], qk.ap[:, t, h, :], ident), inc=(q == 3))
                    h0 = 4 * piece + 2 * hh
                    a = evac(dst[0:96, h0:h0 + 2, :], bk.ap[0:96, :].rearrange("p (h t) -> p h t", h=2), d,
                             -float(96.0 ** -0.5) if kind == 0 else None)
                    bk.free = [a]
                    T_q3.append(a)
                qk.free = [d]

        def mla(h, t):
            mk, w = msk(t)
            return dict(S=[(qT3[0:96, h, t * 128:t * 128 + 128], kT3[0:96, h, 0:w], w, mk, None)],
                        v=[[vm[:, s, h, :] for s in range(2)]])

        attention(pair_jobs(12, mla), T_q3, mix_out)
        cross(1, xqT2, T_xq2)
        T_xa = join(1)
        T_mixed = list(T_xa)
        T_fin = moe(1, T_xa, [])

        SP.dma(lambda e: e.dma_start(out[0].rearrange("(t p) d -> p t d", p=128), x[:, :, :]), s_out, T_fin)
        SP.wait((s_out, 16))

        block = ctx.enter_context(nc.Block())

        @block.sync
        def _(e):
            SP.emit(e)

        @block.tensor
        def _(e):
            PE.emit(e)

        @block.vector
        def _(e):
            V.emit(e)

        @block.scalar
        def _(e):
            S.emit(e)

        @block.gpsimd
        def _(e):
            G.emit(e)


_INS = ["x", "p", "rel_bias", "g_mix_pre", "g_mix_post", "g_ffn_pre", "g_ffn_post", "w_in", "w_pool", "pool_scale",
        "w_out", "w_up", "conv_w", "conv_b", "w_down", "w_ple", "w_ple_gate", "mem_2", "positions_2", "nsa_w_in_2",
        "nsa_cmp_pe_2", "nsa_cmp_w1_2", "nsa_cmp_w2_2", "mla_w_in_2", "mla_q_norm_2", "mla_w_uq_2",
        "mla_kv_norm_2", "mla_w_ukv_2", "mem_w_kv_2", "w_out_2", "ln_g_2", "ln_b_2", "moe_w_grp_2", "moe_b_grp_2",
        "moe_w_exp_2", "moe_b_exp_2", "moe_w_gate_2", "moe_w_up_2", "moe_w_down_2"]


def kernel(**inputs):
    import numpy as _np
    import concourse.bacc as _bacc
    from concourse import mybir as _mybir
    from concourse.bass_utils import run_bass_kernel_spmd as _run

    nc = _bacc.Bacc("TRN2", target_bir_lowering=False, num_devices=1)
    arrays, args = {}, {}

    def give(name, a):
        arrays[name] = a
        return nc.dram_tensor(name, a.shape, _mybir.dt.from_np(a.dtype), kind="ExternalInput").ap()

    for name in _INS:
        args[name] = give(f"in_{name}", _np.ascontiguousarray(inputs[name]))
    cst, onehot = constants()
    cst_d, oh_d = give("const_rows", cst), give("const_onehot", onehot)
    scratch = nc.dram_tensor("bias_rows", (8, 384), F32, kind="Internal").ap()
    out = nc.dram_tensor("out", (1, T, D), F32, kind="ExternalOutput").ap()
    build(nc, args, out, cst_d, oh_d, scratch)
    r = _run(nc, [arrays], core_ids=[0])
    return r.results[0]["out"]
```

```python
from contextlib import ExitStack

import numpy as np

import concourse.bass as bass
from concourse import mybir

F32 = mybir.dt.float32
F32R = mybir.dt.float32r
I32 = mybir.dt.int32
ALU = mybir.AluOpType
ACT = mybir.ActivationFunctionType
AX = mybir.AxisListType

T, D = 256, 1024
KC = 8
BIG = 1.0e30
DFF = 2816
NJ = DFF // 128
ALPHA = 4.0 ** 0.25
CAP = 64
NCMP = 15
TWO_PI_INV = float(np.float32(1.0 / (2.0 * np.pi)))
MAGIC = float(1.5 * 2.0 ** 23)


def two_pi_parts():
    parts, rest = [], 2.0 * np.pi
    for _ in range(4):
        m, e = np.frexp(rest)
        p = np.ldexp(np.floor(m * 512.0) / 512.0, e)
        parts.append(float(p))
        rest -= p
    return parts


def constants():
    ident = np.eye(128, dtype=np.float32)
    p = np.arange(128)[:, None]
    s = np.arange(256)[None, :]
    causal = np.where(s - 128 <= p, 0.0, BIG).astype(np.float32)
    j = np.arange(384)
    dist = 255 - j
    n = np.maximum(dist, 0)
    nf = np.maximum(n, 1).astype(np.float32)
    large = 16 + (np.log(nf / np.float32(16)) / np.float32(np.log(8.0)) * np.float32(16)).astype(np.int32)
    bucket = np.where(n < 16, n, np.minimum(large, 31))
    onehot = np.zeros((33, 384), np.float32)
    ok = dist >= 0
    onehot[bucket[ok], j[ok]] = -1.0
    onehot[32, ~ok] = BIG
    cnt = np.zeros((4, 16), np.float32)
    for g, w in enumerate((2, 4, 8, 16)):
        cnt[g] = np.float32(1.0) / np.minimum(np.arange(16) + 1, w).astype(np.float32)
    inv = np.concatenate([
        np.float32(500000.0) ** (-np.arange(0, 16, 2, dtype=np.float32) / np.float32(16)),
        np.float32(10000.0) ** (-np.arange(0, 32, 2, dtype=np.float32) / np.float32(32)),
    ]).astype(np.float32)
    end = np.arange(NCMP) * 16 + 31
    t = np.arange(256)
    cok = (end[None, :] <= t[:, None]).astype(np.float32).reshape(2, 128, NCMP).transpose(1, 0, 2)
    rank = np.array([4.0, 3.0, 2.0, 1.0], np.float32)
    row = np.concatenate([inv, cnt.reshape(-1), rank])
    row = np.broadcast_to(row, (128, row.size))
    return np.ascontiguousarray(np.concatenate(
        [ident, causal, np.ascontiguousarray(cok).reshape(128, 30), row, ident[::-1],
         (p < np.arange(128)[None, :]).astype(np.float32), np.ones((128, 128), np.float32),
         np.broadcast_to(np.arange(CAP, dtype=np.float32) - 1000.0, (128, CAP)),
         np.concatenate([np.eye(CAP)] * 2)], axis=1), np.float32), onehot


C_ID, C_MASK, C_COK, C_INV, C_CNT, C_RANK, C_FLIP, C_UP, C_ONE, C_IOTA = 0, 128, 384, 414, 438, 502, 506, 634, 762, 890
C_TWO = C_IOTA + CAP
C_ALL = C_TWO + CAP


class Queue:

    def __init__(self, sem, serial=False):
        self.sem, self.count, self.ops, self.seen = sem, 0, [], {}
        self.serial = serial

    def wait(self, *toks):
        for tok in toks:
            if tok is None:
                continue
            if isinstance(tok, list):
                self.wait(*tok)
                continue
            sem, n = tok
            if self.seen.get(sem.name, 0) < n:
                self.seen[sem.name] = n
                self.ops.append(("wait", sem, n))

    def do(self, fn, *toks, inc=True):
        self.wait(*toks)
        if self.serial and self.count:
            self.wait((self.sem, self.count))
        if not inc:
            self.ops.append(("op", fn, None, 0))
            return None
        self.count += 1
        self.ops.append(("op", fn, self.sem, 1))
        return (self.sem, self.count)

    def dma(self, fn, sem, *toks):
        self.wait(*toks)
        self.ops.append(("op", fn, sem, 16))

    def emit(self, eng, ops=None):
        for op in self.ops if ops is None else ops:
            if op[0] == "wait":
                eng.wait_ge(op[1], op[2])
            elif op[0] == "branch":
                n = eng.value_load(op[1], min_val=0, max_val=T)
                with eng.If(n <= CAP):
                    self.emit(eng, op[2])
                with eng.Else():
                    self.emit(eng, op[3])
            elif op[0] == "level":
                eng.drain()
                eng.sem_inc(self.sem, op[1])
            else:
                ins = op[1](eng)
                if op[2] is not None:
                    ins.then_inc(op[2], op[3])


class Place:

    made = []

    def __init__(self, ap):
        self.ap, self.free = ap, []
        Place.made.append(self)


class Slot:

    def __init__(self, ap, sems):
        self.ap, self.halves = ap, [Place(ap[:, 0:2048]), Place(ap[:, 2048:4096])]
        for h, s in zip(self.halves, sems):
            h.sem, h.n = s, 0

    def give(self, toks):
        for h in self.halves:
            h.free = list(toks)

    free = property(None, give)


class Ring:
    def __init__(self, places):
        self.places, self.at = places, 0

    def take(self):
        p = self.places[self.at % len(self.places)]
        self.at += 1
        return p


def build(nc, ins, out, const, onehot, scratch):
    ctx = ExitStack()
    Place.made.clear()
    with ctx:
        def sb(name, shape, dt=F32):
            return ctx.enter_context(nc.sbuf_tensor(name, shape, dt))

        def sem(name):
            return ctx.enter_context(nc.semaphore(name))

        PE, V, S, G, SP = (Queue(sem(n)) for n in ("s_pe", "s_dve", "s_act", "s_pool", "s_sp"))
        G.serial = V.serial = S.serial = True
        banks = [Place(ctx.enter_context(nc.psum_tensor(f"ps{i}", [128, 512], F32))) for i in range(8)]
        work = Ring(banks[0:4])
        acc = banks[4:8]

        NSLOT = 5
        slots = []
        for i in range(NSLOT):
            if i == NSLOT - 2:
                with ExitStack() as same:
                    cuts = Ring([Place([same.enter_context(nc.sbuf_tensor(f"{n}{j}", [128, 1024], F32R))
                                        for n in ("phi", "plo")]) for j in range(4)])
            slots.append(Slot(sb(f"w{i}", [128, 4096]), (sem(f"s_wa{i}"), sem(f"s_wb{i}"))))
        wring, mring = Ring(slots[:NSLOT - 2]), Ring(slots)

        ahead = []

        def fetch(units):
            got = [stream(*u, halves=h) for u, h in units]
            ahead.extend(got)

        def fork(count, tok, short, long):
            queues = (PE, V, S, G, SP)
            for q in queues:
                q.wait(tok)
            start = [(q.count, dict(q.seen), q.ops) for q in queues]
            rings = (wring, mring, cuts, work, Lb, Pb, Tb)
            at = [r.at for r in rings]
            free = [list(p.free) for p in Place.made]
            n0, pre = [h.n for p in slots for h in p.halves], list(ahead)
            ends = []
            for path in (short, long):
                for q, (c, seen, _) in zip(queues, start):
                    q.count, q.seen, q.ops = c, dict(seen), []
                for r, a in zip(rings, at):
                    r.at = a
                for p, f in zip(Place.made, free):
                    p.free = list(f)
                for h, n in zip([h for p in slots for h in p.halves], n0):
                    h.n = n
                ahead[:] = pre
                path()
                ends.append(([(q.count, q.seen, q.ops) for q in queues], [h.n for p in slots for h in p.halves],
                             wring.at, mring.at, list(ahead)))
            assert ends[0][1:] == ends[1][1:]
            join = []
            for k, q in enumerate(queues):
                two = [e[0][k] for e in ends]
                q.count = max(c for c, _, _ in two) + 1
                if q is SP:
                    q.count -= 1
                else:
                    for c, _, ops in two:
                        ops.append(("level", q.count - c))
                    join.append((q.sem, q.count))
                q.seen = {n: min(two[0][1][n], two[1][1][n]) for n in two[0][1] if n in two[1][1]}
                q.ops = start[k][2] + [("branch", count, two[0][2], two[1][2])]
            for p in Place.made:
                p.free = list(join)
            return join

        def stream(*parts, halves=False):
            if ahead:
                return ahead.pop(0)
            sl = (mring if halves else wring).take()
            toks = []
            for h, (dst, src) in zip(sl.halves, parts):
                SP.dma(lambda e, d=dst(sl.ap), s=src: e.dma_start(d, s), h.sem,
                       h.free if halves else [o.free for o in sl.halves])
                h.n += 16
                toks.append((h.sem, h.n))
            sl.free = []
            return sl, toks

        def cols(w, kc, n0, n):
            return (lambda a: a[:, 0:kc * n].rearrange("p (c n) -> p c n", c=kc),
                    w[:, n0:n0 + n].rearrange("(c p) n -> p c n", p=128))

        def wview(sl, kc, n):
            return sl.ap[:, 0:kc * n].rearrange("p (c n) -> p c n", c=kc)

        x = sb("x", [128, 2, D])
        with ExitStack() as same:
            hTr, yTr = (same.enter_context(nc.sbuf_tensor(n, [128, KC, T], F32R)) for n in ("hTr", "yTr"))
        hT = sb("hT", [128, KC, T])
        yT = sb("yT", [128, KC, T])
        z = sb("z", [128, 2, D])
        cst = sb("cst", [128, C_ALL])
        colv = sb("colv", [128, 112])
        gains = [Place(sb(f"gain{i}", [128, D])) for i in range(2)]
        for i, g in enumerate(gains):
            g.sem, g.n = sem(f"s_g{i}"), 0
        with ExitStack() as same:
            xgr = [same.enter_context(nc.sbuf_tensor(f"xgr{i}", [128, 2048], F32R)) for i in range(2)]
            whr = [same.enter_context(nc.sbuf_tensor(f"whr{i}", [128, 2, 512], F32R)) for i in range(4)]
            wlr = [same.enter_context(nc.sbuf_tensor(f"wlr{i}", [128, 2, 512], F32R)) for i in range(4)]
        with ExitStack() as same:
            h2h, h2l = (same.enter_context(nc.sbuf_tensor(n, [128, NJ, T], F32R)) for n in ("h2h", "h2l"))
        arena = sb("arena", [128, 12360])
        Lb = Ring([Place(sb(f"L{i}", [128, 512])) for i in range(2)])
        Pb = Ring([Place(sb(f"P{i}", [128, 512])) for i in range(3)])
        Tb = Ring([Place(sb(f"PT{i}", [128, 512])) for i in range(3)])
        small = sb("small", [128, 1600])
        mkT = sb("mkT", [128, 2, 2, T])
        mv = sb("mv", [128, 2, 2, T])
        wge = sb("wge", [128, 2, KC, 20])
        bge = sb("bge", [128, 2, 20])
        w2c = sb("w2c", [128, 2, 64])

        ident = cst[:, C_ID:C_ID + 128]
        mask = cst[:, C_MASK:C_MASK + 256]
        cok = cst[:, C_COK:C_COK + 30].rearrange("p (t n) -> p t n", t=2)

        sm_at = [0]

        def sm(n):
            a = small[:, sm_at[0]:sm_at[0] + n]
            sm_at[0] += n
            return a

        ar_at = [0]

        def ar(n):
            a = arena[:, ar_at[0]:ar_at[0] + n]
            ar_at[0] += n
            assert ar_at[0] <= 12360
            return a

        G_MIX, G_FFN, PSC, QN, KN, CW, CB = 0, 8, 16, 20, 22, 23, 89

        s_x, s_cst, s_mem, s_small = sem("s_x"), sem("s_cst"), sem("s_mem"), sem("s_small")
        s_early, s_bias, s_out = sem("s_early"), sem("s_bias"), sem("s_out")
        ar_at[0] = 0
        mem = ar(2 * D).rearrange("p (t d) -> p t d", t=2)
        memT = ar(KC * T).rearrange("p (c t) -> p c t", c=KC)
        qk1 = ar(8 * T).rearrange("p (g t) -> p g t", g=8)
        rows = ar(128)
        relx = ar(8)
        oh = ar(384)
        rb = ar(384)
        pes = ar(128)
        btab = ar(8 * 256).rearrange("p (h s) -> p h s", h=8)
        posi = sm(3).bitcast(I32)

        SP.dma(lambda e: e.dma_start(cst[:, :], const), s_cst)
        SP.dma(lambda e: e.dma_start(mem, ins["mem_2"][0].rearrange("(t p) d -> p t d", p=128)), s_mem)
        fetch([([cols(ins["mem_w_kv_2"][0], KC, 0, 256)], False)])
        SP.dma(lambda e: e.dma_start(x[:, :, :], ins["x"][0].rearrange("(t p) d -> p t d", p=128)), s_x)
        early = 0
        at = 0
        for name, view in (("g_mix_pre", 8), ("g_ffn_pre", 8), ("pool_scale", 4), ("mla_q_norm_2", 2),
                           ("mla_kv_norm_2", 1), ("conv_w", 66), ("conv_b", 22)):
            src = ins[name]
            if name == "conv_w":
                src = src[0].rearrange("k (j p) -> (k j) p", p=128)
            else:
                src = src[0].rearrange("(j p) -> j p", p=128)
            SP.dma(lambda e, a=at, v=view, s=src: e.dma_start(rows[a:a + v, :], s), s_early)
            at += view
            early += 16
        NROWS = at
        SP.dma(lambda e: e.dma_start(relx[0:32, :], ins["rel_bias"]), s_early)
        SP.dma(lambda e: e.dma_start(oh[0:33, :], onehot), s_early)
        for k in range(2):
            SP.dma(lambda e, k=k: e.dma_start(pes[16 * k:16 * k + 16, :],
                                             ins["nsa_cmp_pe_2"][0, k].rearrange("(c q) d -> c (q d)", q=2)), s_early)
        early += 16 * 4
        pcol = ins["positions_2"].rearrange("a t -> t a")
        for t in range(2):
            SP.dma(lambda e, t=t: e.dma_start(posi[:, t:t + 1], pcol[t * 128:t * 128 + 128, :]), s_early)
        SP.dma(lambda e: e.dma_start(posi[0:NCMP, 2:3], pcol[31:256:16, :], allow_slow_non_contiguous=True), s_early)
        early += 16 * 3
        T_early = (s_early, early)
        T_cst, T_x, T_mem = (s_cst, 16), (s_x, 16), (s_mem, 16)

        ns = 0
        for i in range(2):
            S.dma(lambda e, i=i: e.dma_start(wge[:, i, :, 0:4],
                                             ins["moe_w_grp_2"][i].rearrange("(c p) n -> p c n", p=128)), s_small)
            S.dma(lambda e, i=i: e.dma_start(wge[:, i, :, 4:20],
                                             ins["moe_w_exp_2"][i].rearrange("(c p) n -> p c n", p=128)), s_small)
            S.dma(lambda e, i=i: e.dma_start(bge[:, i, 0:4], ins["moe_b_grp_2"][i].partition_broadcast(128)), s_small)
            S.dma(lambda e, i=i: e.dma_start(bge[:, i, 4:20], ins["moe_b_exp_2"][i].partition_broadcast(128)), s_small)
            S.dma(lambda e, i=i: e.dma_start(w2c[:, i, :], ins["nsa_cmp_w2_2"][0, i]), s_small)
            ns += 80
        wpool = ar(4 * 128).rearrange("p (g d) -> p g d", g=4)
        S.dma(lambda e: e.dma_start(wpool, ins["w_pool"][0].rearrange("g c d -> c g d")), s_small)
        ns += 16
        T_small = (s_small, ns)

        def gain(i, row, after=None):
            g = gains[i]
            G.dma(lambda e, a=g.ap, r=row: e.dma_start(a[:, :], r.partition_broadcast(128)), g.sem, g.free, after)
            g.n += 16
            g.free = []
            return g, (g.sem, g.n)


        half_pow = sm(8)
        k_pow = G.do(lambda e: e.memset(half_pow, -0.5))

        def rsqrt(dst, src, eps, scale, tok):
            a = V.do(lambda e: e.tensor_scalar(dst, src, scale, eps, ALU.mult, ALU.add), tok)
            n = src.shape[-1]
            return G.do(lambda e: e.tensor_tensor(dst, dst, half_pow[:, 0:n], ALU.pow), a, k_pow)

        sq = sm(8)
        rstd = sm(4)
        mean = sm(4)

        flip = [0]

        def evac(dst, src, tok, scale=None, eng=None):
            if eng is None:
                flip[0] ^= 1
                eng = "S" if flip[0] else "V"
            if eng == "S":
                if scale is None:
                    return S.do(lambda e: e.copy(dst, src), tok)
                return S.do(lambda e: e.mul(dst, src, scale), tok)
            if scale is None:
                return V.do(lambda e: e.tensor_copy(dst, src), tok)
            return V.do(lambda e: e.tensor_scalar(dst, src, scale, None, ALU.mult), tok)

        def evac2(dst, src, tok, scale=None):
            hi, lo = dst
            if scale is None:
                a = S.do(lambda e: e.copy(hi, src), tok)
                return V.do(lambda e: e.tensor_tensor(lo, src, hi.bitcast(F32), ALU.subtract), a)
            a = S.do(lambda e: e.mul(hi, src, scale), tok)
            return V.do(lambda e: e.scalar_tensor_tensor(lo, src, scale, hi.bitcast(F32), ALU.mult, ALU.subtract), a)

        plan, cutq = [], []

        def split():
            if not plan:
                return
            u = plan[0]
            if u["at"] == 0:
                u["sl"], u["wt"] = stream(*u["parts"])
            j, m, sl, pc = u["at"], u["m"], u["sl"], cuts.take()
            hi, lo = (a[:, 0:m] for a in pc.ap)
            src = sl.ap[:, j * m:j * m + m]
            a = S.do(lambda e: e.copy(hi, src), u["wt"], pc.free)
            k = V.do(lambda e: e.tensor_tensor(lo, src, hi.bitcast(F32), ALU.subtract), a, u["wt"])
            u["at"] += 1
            if u["at"] == u["n"]:
                sl.free = [k]
                plan.pop(0)
            cutq.append((pc, k))

        def start(units, ahead=4):
            plan.extend(dict(parts=p, m=m, n=n, at=0) for p, m, n in units)
            for _ in range(ahead):
                split()

        def by_cols(w, n0, n):
            return [cols(w, KC, n0, n)], 2 * n, KC // 2

        def three(out, l, r, first, last, group=False, inc=False):
            for i, (a, b) in enumerate(((0, 0), (0, 1), (1, 0))):
                d = PE.do(lambda e, a=a, b=b, i=i: e.matmul(out, l[a], r[b], start=first and i == 0, stop=last and i == 2,
                                                            skip_group_check=group), inc=inc and i == 2)
            return d

        def tok3(pair, ltok, n, use):
            bks = [work.take() for _ in range(2)]
            PE.wait(ltok, *[b.free for b in bks])
            for j in range(KC // 2):
                pc, k = cutq.pop(0)
                PE.wait(k)
                ds = []
                for t in range(2):
                    for q in range(2):
                        d = three(bks[t].ap[:, 0:n], [a[:, 2 * j + q, t * 128:t * 128 + 128] for a in pair],
                                  [a[:, q * n:q * n + n] for a in pc.ap], j == 0 and q == 0, j == 3 and q == 1, inc=q == 1)
                    ds.append(d)
                pc.free = [d]
                split()
            for t in range(2):
                bks[t].free = [use(t, bks[t].ap, ds[t])]
            return d

        def feat3(pair, ltok, n, chunk, use):
            bks = [work.take() for _ in range(2)]
            PE.wait(ltok, *[b.free for b in bks])
            for j in range(KC // 2):
                pc, k = cutq.pop(0)
                PE.wait(k)
                ds = []
                for c in range(2):
                    for h in range(2):
                        for q in range(2):
                            o = q * n + chunk(c, h)
                            d = three(bks[c].ap[:, h * 256:h * 256 + 256], [a[:, o:o + 128] for a in pc.ap],
                                      [a[:, 2 * j + q, :] for a in pair], j == 0 and q == 0 and h == 0,
                                      j == 3 and q == 1 and h == 1, True, inc=h == 1 and q == 1)
                    ds.append(d)
                pc.free = [d]
                split()
            for c in range(2):
                bks[c].free = [use(c, bks[c].ap, ds[c])]
            return d

        def pairs(c, h):
            return (2 * c + h) * 128

        def turn_row(t, src, dst, tok, eng=None):
            res = []
            for c in range(2):
                bk = work.take()
                PE.wait(tok, bk.free, T_cst)
                for q in range(4):
                    d = PE.do(lambda e, b=bk.ap, q=q, kc=4 * c + q: e.transpose(
                        b[:, q * 128:q * 128 + 128], src[:, t, kc * 128:kc * 128 + 128], ident), inc=(q == 3))
                b3 = bk.ap[:, :].rearrange("p (c t) -> p c t", c=4)
                at = (slice(None), slice(4 * c, 4 * c + 4), slice(t * 128, t * 128 + 128))
                if isinstance(dst, tuple):
                    k = evac2([a[at] for a in dst], b3, d)
                else:
                    k = evac(dst[at], b3, d, eng=eng)
                bk.free = [k]
                res.append(k)
            return res

        def turn(src, dst, toks):
            return turn_row(0, src, dst, toks[0]) + turn_row(1, src, dst, toks[1])

        def rms_row(t, src, tok, g, gtok):
            a = S.do(lambda e: e.activation(z[:, t, :], src[:, t, :], ACT.Square, accum_out=sq[:, t:t + 1]), tok)
            r = rsqrt(rstd[:, t:t + 1], sq[:, t:t + 1], 1e-6, 1.0 / D, a)
            k = V.do(lambda e: e.scalar_tensor_tensor(
                z[:, t, :], src[:, t, :], rstd[:, t:t + 1], g.ap[:, :], ALU.mult, ALU.mult), r, gtok)
            g.free = [k]
            return k

        def lin_tok(lT, ltok, kcs, w, n0, n, use):
            sl, wt = stream(cols(w, kcs, n0, n))
            wv = wview(sl, kcs, n)
            for t in range(2):
                bk = work.take()
                PE.wait(ltok, bk.free, wt)
                for k in range(kcs):
                    d = PE.do(lambda e, b=bk.ap, k=k, t=t: e.matmul(
                        b[:, 0:n], lT[:, k, t * 128:t * 128 + 128], wv[:, k, :],
                        start=(k == 0), stop=(k == kcs - 1)), inc=(k == kcs - 1))
                bk.free = [use(t, bk.ap, d)]
            sl.free = [d]
            return d

        def lin_feat(lT, ltok, kcs, w, n0, n, use):
            sl, wt = stream(cols(w, kcs, n0, n))
            wv = wview(sl, kcs, n)
            for c in range(n // 256):
                bk = work.take()
                PE.wait(ltok, bk.free, wt)
                for q in range(2):
                    for k in range(kcs):
                        d = PE.do(lambda e, b=bk.ap, k=k, q=q, c=c: e.matmul(
                            b[:, q * 256:q * 256 + 256], wv[:, k, (2 * c + q) * 128:(2 * c + q) * 128 + 128],
                            lT[:, k, :], start=(k == 0), stop=(k == kcs - 1)), inc=(q == 1 and k == kcs - 1))
                bk.free = [use(c, bk.ap, d)]
            sl.free = [d]
            return d

        def refill():
            while plan and len(cutq) < 4:
                split()

        def out_proj(pair, ltok, use, row):
            tok3(pair, ltok, 512, lambda t, b, tok: use(t, 0, b, tok))
            bks = [work.take() for _ in range(2)]
            pcs = [cutq.pop(0) for _ in range(4)]
            PE.wait(ltok, *[b.free for b in bks])
            for t in range(2):
                for j, (pc, k) in enumerate(pcs):
                    PE.wait(k)
                    for q in range(2):
                        d = three(bks[t].ap[:, :], [a[:, 2 * j + q, t * 128:t * 128 + 128] for a in pair],
                                  [a[:, q * 512:q * 512 + 512] for a in pc.ap], j == 0 and q == 0, j == 3 and q == 1,
                                  inc=q == 1)
                bks[t].free = [use(t, 1, bks[t].ap, d)]
                row(t)
            for pc, _ in pcs:
                pc.free = [d]

        def rms_add_row(t, g, gtok, tok):
            a = V.do(lambda e: e.tensor_reduce(sq[:, 4 + t:5 + t], ss4[:, t, :], AX.X, ALU.add), tok)
            r = rsqrt(rstd[:, 2 + t:3 + t], sq[:, 4 + t:5 + t], 1e-6, 1.0 / D, a)
            k = V.do(lambda e: e.scalar_tensor_tensor(
                z[:, t, :], z[:, t, :], rstd[:, 2 + t:3 + t], g.ap[:, :], ALU.mult, ALU.mult), r, gtok)
            g.free = [k]
            return V.do(lambda e: e.tensor_tensor(x[:, t, :], x[:, t, :], z[:, t, :], ALU.add), k)

        ss4 = sm(4).rearrange("p (t h) -> p t h", t=2)
        def keep_sq(t, hf, b, tok):
            a = V.do(lambda e: e.tensor_copy(z[:, t, hf * 512:hf * 512 + 512], b[:, :]), tok)
            jk = Lb.take()
            k = S.do(lambda e: e.activation(jk.ap[:, :], z[:, t, hf * 512:hf * 512 + 512], ACT.Square,
                                            accum_out=ss4[:, t, hf:hf + 1]), a, jk.free)
            jk.free = [k]
            return k

        st = sm(24).rearrange("p (t h s) -> p t h s", t=2, h=2)
        mvv = sm(4).rearrange("p (t s) -> p t s", t=2)

        def add_stats(t, hf, b, tok):
            a = V.do(lambda e: e.scalar_tensor_tensor(
                z[:, t, hf * 512:hf * 512 + 512], x[:, t, hf * 512:hf * 512 + 512], ALPHA, b[:, :],
                ALU.mult, ALU.add), tok)
            V.do(lambda e: e.bn_stats(st[:, t, hf, :], z[:, t, hf * 512:hf * 512 + 512]), a)
            return a

        ln = {}

        def ln_load(i, jn):
            ln[i, jn] = gain(0, ins["ln_g_2"][i, jn]), gain(1, ins["ln_b_2"][i, jn])

        def ln_row(t, i, jn):
            (gg, gt), (gb, bt) = ln[i, jn]
            a = V.do(lambda e: e.bn_aggr(mvv[:, t, :], st[:, t, :, :].rearrange("p h s -> p (h s)")))
            r = rsqrt(rstd[:, t:t + 1], mvv[:, t, 1:2], 1e-5, 1.0, a)
            k = V.do(lambda e: e.tensor_scalar(z[:, t, :], z[:, t, :], mvv[:, t, 0:1], rstd[:, t:t + 1],
                                               ALU.subtract, ALU.mult), r)
            k = V.do(lambda e: e.tensor_tensor(z[:, t, :], z[:, t, :], gg.ap[:, :], ALU.mult), k, gt)
            q = V if t else G
            k2 = q.do(lambda e: e.tensor_tensor(x[:, t, :], z[:, t, :], gb.ap[:, :], ALU.add), k, bt)
            gg.free, gb.free = [k], [*gb.free, k2]
            return k2

        sbank, tbank, obank = Ring(banks[0:3]), Ring(banks[3:6]), Ring(banks[6:8])
        mrs = Ring([Place(sm(6)) for _ in range(4)])

        def attention(jobs, ready, pair_out):
            n = len(jobs)
            for i in range(n + 3):
                if i < n:
                    j = jobs[i]
                    bk = sbank.take()
                    PE.wait(bk.free, ready)
                    for q, (lq, rk, w, mk, gt) in enumerate(j["S"]):
                        d = PE.do(lambda e, b=bk.ap, q=q, lq=lq, rk=rk, w=w: e.matmul(
                            b[:, q * 256:q * 256 + w], lq, rk, start=True, stop=True), inc=(q == len(j["S"]) - 1))
                    Lp, Pp, ms = Lb.take(), Pb.take(), mrs.take()
                    m, rs, rc = ms.ap[:, 0:2], ms.ap[:, 2:4], ms.ap[:, 4:6]
                    ex = []
                    for q, (lq, rk, w, mk, gt) in enumerate(j["S"]):
                        c = slice(q * 256, q * 256 + w)
                        if mk is not None:
                            a = V.do(lambda e, c=c, q=q, mk=mk, L=Lp.ap, b=bk.ap, m=m: e.tensor_tensor_reduce(
                                L[:, c], b[:, c], mk, 1.0, 3.0e38, ALU.add, ALU.min, m[:, q:q + 1]), d, Lp.free, ms.free)
                            src, fin = Lp.ap, a
                        else:
                            a = V.do(lambda e, c=c, q=q, b=bk.ap, m=m: e.tensor_reduce(
                                m[:, q:q + 1], b[:, c], AX.X, ALU.min), d, ms.free)
                            src = bk.ap
                        ex.append(S.do(lambda e, c=c, q=q, s=src, P=Pp.ap, m=m, rs=rs: e.activation(
                            P[:, c], s[:, c], ACT.Exp, bias=m[:, q:q + 1], scale=-1.0,
                            accum_out=rs[:, q:q + 1]), a, Pp.free))
                    bk.free = [a] if j["S"][0][3] is not None else [ex[-1]]
                    Lp.free = [ex[-1]]
                    nq = len(j["S"])
                    j["P"], j["ms"] = Pp, ms
                    j["ex"], j["nq"] = ex[-1], nq
                if 1 <= i <= n:
                    j = jobs[i - 1]
                    rc, rs, nq = j["ms"].ap[:, 4:6], j["ms"].ap[:, 2:4], j["nq"]
                    k = V.do(lambda e, rc=rc, rs=rs, nq=nq: e.reciprocal(rc[:, 0:nq], rs[:, 0:nq]), j["ex"])
                    for q, (lq, rk, w, mk, gt) in enumerate(j["S"]):
                        c = slice(q * 256, q * 256 + w)
                        if gt is None:
                            kk = V.do(lambda e, c=c, q=q, P=j["P"].ap, rc=rc: e.tensor_scalar(
                                P[:, c], P[:, c], rc[:, q:q + 1], None, ALU.mult), k)
                        else:
                            kk = V.do(lambda e, c=c, q=q, P=j["P"].ap, rc=rc, gt=gt: e.tensor_scalar(
                                P[:, c], P[:, c], rc[:, q:q + 1], gt, ALU.mult, ALU.mult), k)
                    j["ms"].free = [kk]
                    j["norm"] = kk
                if 2 <= i <= n + 1:
                    j = jobs[i - 2]
                    bk, Tp = tbank.take(), Tb.take()
                    PE.wait(bk.free, j["norm"])
                    todo = [(q, s) for q, sp in enumerate(j["S"]) for s in range(sp[2] // 128)]
                    for o, (q, s) in enumerate(todo):
                        d = PE.do(lambda e, o=o, q=q, s=s, b=bk.ap, P=j["P"].ap: e.transpose(
                            b[:, o * 128:o * 128 + 128], P[:, q * 256 + s * 128:q * 256 + s * 128 + 128], ident),
                            inc=(o == len(todo) - 1))
                    j["P"].free = [d]
                    w = 128 * len(todo)
                    k = evac(Tp.ap[:, 0:w], bk.ap[:, 0:w], [d, *Tp.free])
                    bk.free = [k]
                    j["T"], j["Tk"], j["todo"] = Tp, k, todo
                if i >= 3:
                    j = jobs[i - 3]
                    if j["first"]:
                        ob = obank.take()
                        PE.wait(ob.free)
                    PE.wait(j["Tk"])
                    hp, t = j["half"] * 64, j["t"]
                    mm = [(j["v"][q][s], j["T"].ap[:, o * 128:o * 128 + 128]) for o, (q, s) in enumerate(j["todo"])]
                    mm += j.get("extra", [])
                    for o, (l, r) in enumerate(mm):
                        d = PE.do(lambda e, o=o, l=l, r=r, b=ob.ap, hp=hp, t=t, n=len(mm): e.matmul(
                            b[hp:hp + 64, t * 128:t * 128 + 128], l, r, start=(o == 0), stop=(o == n - 1)),
                            inc=(o == len(mm) - 1))
                    j["T"].free = [d]
                    if j["last"]:
                        ob.free = [pair_out(j["pair"], ob.ap, d)]

        def pair_jobs(heads, make):
            jobs = []
            for h in range(heads):
                for t in range(2):
                    j = make(h, t)
                    j.update(t=t, half=h % 2, pair=h // 2, first=(h % 2 == 0 and t == 0), last=(h % 2 == 1 and t == 1))
                    jobs.append(j)
            return jobs

        def msk(t):
            return (mask[:, 128:256], 128) if t == 0 else (mask[:, 0:256], 256)

        T_memT = turn(mem, memT, [T_mem, T_mem])
        T_mk = []
        def mem_kv(i, part):
            w = ins["mem_w_kv_2"][i]

            def keep_k(c, b, tok, i=i):
                k = evac(mkT[:, i, :, :], b[:, :].rearrange("p (c t) -> p c t", c=2), tok)
                T_mk.append(k)
                return k

            def keep_v(t, b, tok, i=i):
                k = evac(mv[:, i, t, :], b[:, 0:256], tok)
                T_mk.append(k)
                return k

            if part == 0:
                lin_feat(memT, T_memT, KC, w, 0, 256, keep_k)
            else:
                lin_tok(memT, T_memT, KC, w, 256, 256, keep_v)
        gp = gain(0, ins["g_mix_pre"][0], T_mem)
        T_z = [rms_row(t, x, T_x, *gp) for t in range(2)]
        mem_kv(0, 0)
        mem_kv(0, 1)
        T_hT = turn(z, (hTr, yTr), T_z)
        w_in, w_up, w_down, w_n = ins["w_in"][0], ins["w_up"][0], ins["w_down"][0], ins["nsa_w_in_2"][0]
        start([by_cols(w_in, n0, 512) for n0 in (0, 512, 1024, 1536)]
              + [by_cols(ins["w_out"][0], n0, 512) for n0 in (0, 512)]
              + [([(lambda a, gv=gv: a[:, 0:4096].rearrange("p (c n) -> p c n", c=8)[:, :, gv * 256:gv * 256 + 256],
                    w_up[:, gv * DFF + u * 256:gv * DFF + u * 256 + 256].rearrange("(c p) n -> p c n", p=128))
                   for gv in range(2)], 1024, 4) for u in range(NJ // 2)]
              + [([(lambda a, n=n: a[:, 0:n * 1024].rearrange("p (c n) -> p c n", c=n),
                    w_down[u * 512:u * 512 + n * 128, :].rearrange("(c p) n -> p c n", p=128))], 1024, n)
                 for u, n in ((u, min(4, NJ - 4 * u)) for u in range(6))]
              + [by_cols(ins["w_ple_gate"][0], n0, 512) for n0 in (0, 512)]
              + [by_cols(w_n, c * 512, 512 if c < 5 else 36) for c in range(6)]
              + [by_cols(ins["w_out_2"][0], n0, 512) for n0 in (0, 512)])
        bk = work.take()
        PE.wait(T_early, T_cst, bk.free)
        d1 = PE.do(lambda e, b=bk.ap: e.transpose(b[:, 0:NROWS], rows[0:NROWS, :], ident[0:NROWS, 0:NROWS]))
        T_col = V.do(lambda e, b=bk.ap: e.tensor_copy(colv[:, 0:NROWS], b[:, 0:NROWS]), d1)
        bk.free = [T_col]

        ang = sm(72).rearrange("p (k n) -> p k n", k=3)
        trig = sm(144).rearrange("p (q k n) -> p q k n", q=2, k=3)
        kk_ = sm(72).rearrange("p (k n) -> p k n", k=3)
        posf = sm(3)
        inv = cst[:, C_INV:C_INV + 24]
        a0 = V.do(lambda e: e.memset(posf, 0.0))
        V.do(lambda e: e.tensor_copy(posf[:, 0:2], posi[:, 0:2]), T_early, a0)
        a0 = V.do(lambda e: e.tensor_copy(posf[0:NCMP, 2:3], posi[0:NCMP, 2:3]))
        for k in range(3):
            a1 = V.do(lambda e, k=k: e.tensor_scalar(ang[:, k, :], inv, posf[:, k:k + 1], None, ALU.mult), a0, T_cst)
        for q, shift in ((0, 0.25), (1, 0.0)):
            b1 = V.do(lambda e, s=shift: e.tensor_scalar(kk_, ang, TWO_PI_INV, s, ALU.mult, ALU.add), a1)
            b1 = V.do(lambda e: e.tensor_scalar(kk_, kk_, MAGIC, None, ALU.add), b1)
            b1 = V.do(lambda e: e.tensor_scalar(kk_, kk_, MAGIC, None, ALU.subtract), b1)
            cur = ang
            for part in two_pi_parts():
                b1 = V.do(lambda e, q=q, c=cur, p=part: e.scalar_tensor_tensor(
                    trig[:, q, :, :], kk_, -p, c, ALU.mult, ALU.add), b1)
                cur = trig[:, q, :, :]
            if q == 0:
                b1 = V.do(lambda e: e.tensor_scalar(trig[:, 0, :, :], trig[:, 0, :, :], float(np.pi / 2), None,
                                                    ALU.add), b1)
            b1 = V.do(lambda e, q=q: e.tensor_scalar(trig[:, q, :, :], trig[:, q, :, :], 3.14159, -3.14159,
                                                     ALU.min, ALU.max), b1)
        T_trig = S.do(lambda e: e.activation(trig, trig, ACT.Sin), b1)

        def rope(x1, x2, k, lo, hi, heads, tmp, tok, p=128):
            n = hi - lo
            c, s = trig[0:p, 0, k, lo:hi], trig[0:p, 1, k, lo:hi]
            for _ in heads:
                c, s = c.unsqueeze(1), s.unsqueeze(1)
            c, s = c.broadcast_to([p, *heads, n]), s.broadcast_to([p, *heads, n])
            V.wait(tok, T_trig)
            V.do(lambda e: e.tensor_tensor(tmp[0], x1, c, ALU.mult))
            V.do(lambda e: e.tensor_tensor(tmp[1], x2, s, ALU.mult))
            V.do(lambda e: e.tensor_tensor(tmp[2], x1, s, ALU.mult))
            a = V.do(lambda e: e.tensor_tensor(tmp[3], x2, c, ALU.mult))
            V.do(lambda e: e.tensor_tensor(x1, tmp[0], tmp[1], ALU.subtract), a)
            return V.do(lambda e: e.tensor_tensor(x2, tmp[2], tmp[3], ALU.add))

        a = G.do(lambda e: e.memset(relx[32:33, :], 1.0))
        bk = work.take()
        d = PE.do(lambda e, b=bk.ap: e.matmul(b[0:8, 0:384], relx[0:33, :], oh[0:33, :], start=True, stop=True),
                  T_early, a, bk.free)
        k = V.do(lambda e, b=bk.ap: e.tensor_copy(rb[0:8, :], b[0:8, 0:384]), d)
        bk.free = [k]
        G.dma(lambda e: e.dma_start(scratch, rb[0:8, :]), s_bias, k)
        zb = z[:, :, :].rearrange("p t d -> p (t d)").rearrange("p (h s) -> p h s", h=8)
        for h in range(8):
            src = bass.AP(scratch.tensor, scratch.offset + h * 384, [[1, 128], [1, 256]])
            G.dma(lambda e, h=h, src=src: e.dma_start(zb[:, h, :], src), s_bias, (s_bias, 16), T_hT)
        g0, gf = gain(1, ins["g_mix_post"][0]), gain(0, ins["g_ffn_pre"][0])
        peT = sm(32)
        bk = work.take()
        d = PE.do(lambda e, b=bk.ap: e.transpose(b[:, 0:32], pes[0:32, :], ident[0:32, 0:32]), bk.free)
        T_peT = V.do(lambda e, b=bk.ap: e.tensor_copy(peT, b[:, 0:32]), d)
        bk.free = [T_peT]
        cbias = sm(30).rearrange("p (t n) -> p t n", t=2)
        T_cb = V.do(lambda e: e.tensor_scalar(cbias, cok, -1.0, BIG, ALU.add, ALU.mult))

        uT = ar(4 * T).rearrange("p (g t) -> p g t", g=4)
        pA = ar(T)
        pB = ar(T)
        qT, kT = qk1[:, 0:4, :], qk1[:, 4:8, :]
        vt = ar(2 * 512).rearrange("p (t d) -> p t d", t=2)
        toks = {"u": [], "q": [], "k": [], "v": []}

        def keep(dst, key, scale=None):
            def use(c, b, tok):
                k = evac(dst[:, 2 * c:2 * c + 2, :], b[:, :].rearrange("p (c t) -> p c t", c=2),
                         tok, scale)
                toks[key].append(k)
                return k
            return use

        feat3((hTr, yTr), T_hT, 512, pairs, keep(uT, "u"))
        feat3((hTr, yTr), T_hT, 512, pairs, keep(qT, "q", -0.125))
        feat3((hTr, yTr), T_hT, 512, pairs, keep(kT, "k"))

        def keep_vt(t, b, tok):
            k = evac(vt[:, t, :], b[:, :], tok)
            toks["v"].append(k)
            return k

        tok3((hTr, yTr), T_hT, 512, keep_vt)

        T_y = []

        def moba(h, t):
            w = 128 * (t + 1)
            r, c = 64 * (h % 2), h // 2
            bt = btab[:, h, 128:256] if t == 0 else btab[:, h, :]
            return dict(S=[(qT[r:r + 64, c, t * 128:t * 128 + 128], kT[r:r + 64, c, 0:w], w, bt, None)],
                        v=[[vt[:, s, h * 64:h * 64 + 64] for s in range(2)]])

        def moba_out(p, b, tok):
            k = evac2([yTr[:, 4 + p, :], hTr[:, 4 + p, :]], b[:, 0:256], tok)
            T_y.append(k)
            return k

        T_bias = []
        for c in range(4):
            bk = work.take()
            d = PE.do(lambda e, b=bk.ap, c=c: e.matmul(
                b[:, :], cst[:, C_FLIP:C_FLIP + 128], zb[:, 2 * c:2 * c + 2, :], start=True, stop=True),
                (s_bias, 16 * 9), T_cst, bk.free)
            k = V.do(lambda e, b=bk.ap, c=c: e.tensor_copy(
                btab[:, 2 * c:2 * c + 2, :], b[:, :].rearrange("p (h s) -> p h s", h=2)), d)
            bk.free = [k]
            T_bias.append(k)

        T_pool = []
        for g in range(4):
            src, tok = uT[:, g, :], toks["u"]
            for s in range(g + 1):
                sh = 1 << s
                dst = (pA, pB)[s % 2]
                G.do(lambda e, d=dst, c=src, sh=sh: e.tensor_copy(d[:, 0:sh], c[:, 0:sh]), tok)
                G.do(lambda e, d=dst, c=src, sh=sh: e.tensor_tensor(d[:, sh:T], c[:, sh:T], c[:, 0:T - sh], ALU.add))
                src = dst
            cn = cst[:, C_CNT + g * 16:C_CNT + g * 16 + 16]
            G.do(lambda e, c=src, cn=cn: e.tensor_tensor(c[:, 0:16], c[:, 0:16], cn, ALU.mult))
            G.do(lambda e, c=src, g=g: e.tensor_scalar(c[:, 16:T], c[:, 16:T], 0.5 ** (g + 1), None, ALU.mult))
            T_pool.append(G.do(lambda e, c=src, g=g: e.tensor_tensor(uT[:, g, :], c, uT[:, g, :], ALU.subtract)))

        V.wait(T_bias)
        attention(pair_jobs(8, moba), toks["q"] + toks["k"] + toks["v"], moba_out)

        for g in range(4):
            bk = work.take()
            d = PE.do(lambda e, b=bk.ap, g=g: e.matmul(b[:, 0:256], wpool[:, g, :], uT[:, g, :], start=True, stop=True),
                      T_pool[g], T_small, bk.free)
            k = evac2([yTr[:, g, :], hTr[:, g, :]], bk.ap[:, 0:256], [d, T_col], colv[:, PSC + g:PSC + g + 1])
            bk.free = [k]
            T_y.append(k)

        yk, T_h2 = [], []

        def keep_y(t, hf, b, tok):
            k = keep_sq(t, hf, b, tok)
            yk.append(k)
            return k

        def row_y(t):
            T_h2.append(rms_row(t, x, rms_add_row(t, *g0, yk), *gf))

        out_proj((yTr, hTr), T_y, keep_y, row_y)

        mem_kv(1, 0)
        T_z, T_h2 = T_h2, turn_row(0, z, (hTr, yTr), T_h2[0])
        mem_kv(1, 1)
        T_h2 += turn_row(1, z, (hTr, yTr), T_z[1])
        refill()
        g1 = gain(1, ins["g_ffn_post"][0])
        ar_at[0] = 0
        ar_at[0] = 2 * NJ * T
        pT = ar(2 * T).rearrange("p (c t) -> p c t", c=2)
        ar_at[0] = 0
        sgm, pl = (ar(2 * D).rearrange("p (t d) -> p t d", t=2) for _ in range(2))
        zf = z[:, :, :].rearrange("p t d -> p (t d)")
        cbs = Ring([Place(zf[:, i * T:i * T + T]) for i in range(3)])
        gbs = Ring([Place(zf[:, (3 + i) * T:(3 + i) * T + T]) for i in range(3)])
        pin = zf[:, 6 * T:8 * T].rearrange("p (t d) -> p t d", t=2)
        s_p = sem("s_p")
        SP.dma(lambda e: e.dma_start(pin, ins["p"][0, 0].rearrange("(t p) d -> p t d", p=128)), s_p, T_h2)
        T_f = []
        def conv(u, two):
            at = []
            for q, (b, d, free) in enumerate(two):
                j = 2 * u + q
                w = [colv[:, CW + i * NJ + j:CW + i * NJ + j + 1] for i in range(3)]
                at.append((j, b, d, free, cbs.take(), gbs.take(), w, colv[:, CB + j:CB + j + 1]))
            k = [S.do(lambda e, b=b, c=cb.ap, w=w, bias=bias: e.activation(
                c, b[:, 0:256], ACT.Identity, bias=bias, scale=w[2]), d, cb.free, T_col)
                for j, b, d, free, cb, gb, w, bias in at]
            for sh in (1, 2):
                k = [V.do(lambda e, b=b, c=cb.ap, w=w, sh=sh: e.scalar_tensor_tensor(
                    c[:, sh:T], b[:, 0:T - sh], w[2 - sh], c[:, sh:T], ALU.mult, ALU.add), k[q])
                    for q, (j, b, d, free, cb, gb, w, bias) in enumerate(at)]
            k = [S.do(lambda e, c=cb.ap, g=gb.ap: e.activation(g, c, ACT.Gelu_apprx_tanh), k[q], gb.free)
                 for q, (j, b, d, free, cb, gb, w, bias) in enumerate(at)]
            for q, (j, b, d, free, cb, gb, w, bias) in enumerate(at):
                cb.free = [k[q]]
                k[q] = V.do(lambda e, b=b, g=gb.ap: e.tensor_tensor(g, g, b[:, 256:512], ALU.mult), k[q])
                free.append(k[q])
            for q, (j, b, d, free, cb, gb, w, bias) in enumerate(at):
                a = S.do(lambda e, j=j, g=gb.ap: e.copy(h2h[:, j, :], g), k[q])
                a = G.do(lambda e, j=j, g=gb.ap: e.tensor_tensor(
                    h2l[:, j, :], g, h2h[:, j, :].bitcast(F32), ALU.subtract), a)
                gb.free = [a]
                T_f.append(a)

        for u in range(NJ // 2):
            two = []

            def take(c, b, d, u=u, two=two):
                two.append((b, d, []))
                if c == 1:
                    conv(u, two)
                return two[c][2]

            feat3((hTr, yTr), T_h2, 512, lambda c, h: h * 256 + c * 128, take)

        bk = work.take()
        PE.wait((s_p, 16), bk.free)
        for q in range(4):
            d = PE.do(lambda e, b=bk.ap, q=q: e.transpose(
                b[:, q * 128:q * 128 + 128], pin[:, q % 2, (q // 2) * 128:(q // 2) * 128 + 128], ident), inc=(q == 3))
        T_pT = evac(pT, bk.ap[:, :].rearrange("p (c t) -> p c t", c=2), d)
        bk.free = [T_pT]

        PE.wait(*[b.free for b in acc])

        def down_rows(j, pc, k, outs):
            PE.wait(k, T_f[j])
            for o in outs:
                t, hf = o // 2, o % 2
                d = three(acc[o].ap[:, :], [a[:, j, t * 128:t * 128 + 128] for a in (h2h, h2l)],
                          [a[:, hf * 512:hf * 512 + 512] for a in pc.ap], j == 0, j == NJ - 1, inc=o == outs[-1])
            return d

        for j in range(NJ - 4):
            pc, k = cutq.pop(0)
            pc.free = [down_rows(j, pc, k, range(4))]
            split()
        pcs = [cutq.pop(0) for _ in range(4)]
        fk, T_x2 = [], []
        for t in range(2):
            for q, (pc, k) in enumerate(pcs):
                d = down_rows(NJ - 4 + q, pc, k, (2 * t, 2 * t + 1))
            for hf in range(2):
                fk.append(keep_sq(t, hf, acc[2 * t + hf].ap, d))
                acc[2 * t + hf].free = [fk[-1]]
            T_x2.append(rms_add_row(t, *g1, fk))
        for pc, _ in pcs:
            pc.free = [d]
        ln_load(0, 0)

        sl, wt = stream((lambda a: a[:, 0:2048].rearrange("p (c n) -> p c n", c=2),
                         ins["w_ple"][0].rearrange("(c p) n -> p c n", p=128)))
        wv = wview(sl, 2, 1024)
        for o in range(4):
            t, hf = o // 2, o % 2
            bk = work.take()
            PE.wait(bk.free, wt, T_pT)
            for k in range(2):
                d = PE.do(lambda e, b=bk.ap, k=k, t=t, hf=hf, wv=wv: e.matmul(
                    b[:, :], pT[:, k, t * 128:t * 128 + 128], wv[:, k, hf * 512:hf * 512 + 512],
                    start=(k == 0), stop=(k == 1)), inc=(k == 1))
            T_pl = S.do(lambda e, b=bk.ap, t=t, hf=hf: e.copy(pl[:, t, hf * 512:hf * 512 + 512], b[:, :]), d)
            bk.free = [T_pl]
        sl.free = [d]
        split()
        split()
        T_x2T = turn(x, (hTr, yTr), T_x2)
        refill()

        def keep_sg(t, hf, b, tok):
            k = S.do(lambda e: e.activation(sgm[:, t, hf * 512:hf * 512 + 512], b[:, :], ACT.Sigmoid), tok)
            return k

        out_proj((hTr, yTr), T_x2T, keep_sg, lambda t: None)
        refill()
        T_sg = (S.sem, S.count)
        T_x3 = []
        for o in range(4):
            t, hf = o // 2, o % 2
            hs = slice(hf * 512, hf * 512 + 512)
            a = V.do(lambda e, t=t, hs=hs: e.tensor_tensor(sgm[:, t, hs], sgm[:, t, hs], pl[:, t, hs], ALU.mult),
                     T_pl, T_sg)
            T_x3.append((V if t else G).do(lambda e, t=t, hs=hs: e.tensor_tensor(x[:, t, hs], x[:, t, hs], sgm[:, t, hs], ALU.add),
                             a, T_x2T))

        def cross(i, xqT, tok):
            def make(h, t):
                r, c = 64 * (h % 2), h // 2
                return dict(S=[(xqT[r:r + 64, c, t * 128:t * 128 + 128], mkT[r:r + 64, i, c, :], 256, None, None)],
                            v=[[mv[:, i, s, h * 64:h * 64 + 64] for s in range(2)]])

            def fin(p, b, tok2):
                k = evac2([yTr[:, 6 + p, :], hTr[:, 6 + p, :]], b[:, 0:256], tok2)
                T_y.append(k)
                return k

            attention(pair_jobs(4, make), [*tok, *T_mk], fin)

        def turn_cols(src, c0, chunks, dst, tok, scale=None, step=128, eng=None):
            res = []
            for c in range(0, chunks, 2):
                bk = work.take()
                PE.wait(bk.free, tok)
                m = min(2, chunks - c)
                for q in range(2 * m):
                    cc, t = c + q // 2, q % 2
                    a = src[:, t, c0 + cc * step:c0 + cc * step + 128]
                    d = PE.do(lambda e, b=bk.ap, q=q, a=a: e.transpose(b[:, q * 128:q * 128 + 128], a, ident),
                              inc=(q == 2 * m - 1))
                k = evac(dst[:, c:c + m, :], bk.ap[:, 0:m * 256].rearrange("p (c t) -> p c t", c=m), d, scale, eng)
                bk.free = [k]
                res.append(k)
            return res

        lg = sm(40).rearrange("p (t n) -> p t n", t=2)
        eg = sm(8).rearrange("p (t n) -> p t n", t=2)
        ohg = sm(8).rearrange("p (t n) -> p t n", t=2)
        oh1 = sm(8).rearrange("p (t n) -> p t n", t=2)
        oh2 = sm(8).rearrange("p (t n) -> p t n", t=2)
        le = sm(8).rearrange("p (t n) -> p t n", t=2)
        le2 = sm(8).rearrange("p (t n) -> p t n", t=2)
        w4 = sm(8).rearrange("p (t n) -> p t n", t=2)
        c4 = sm(8).rearrange("p (t n) -> p t n", t=2)
        r2 = [sm(2) for _ in range(5)]
        pick = sm(32).rearrange("p (t g j) -> p t g j", t=2, g=4)
        gate = sm(32).rearrange("p (t n) -> p t n", t=2)
        rank = cst[:, C_RANK:C_RANK + 4].unsqueeze(1).broadcast_to([128, 2, 4])

        def bc(a, n=4):
            return a.unsqueeze(2).broadcast_to([128, 2, n])

        def first_max(dst, src, mx, tok):
            a = V.do(lambda e: e.tensor_reduce(mx, src, AX.X, ALU.max), tok)
            a = V.do(lambda e: e.tensor_tensor(c4, src, bc(mx), ALU.is_equal), a)
            a = V.do(lambda e: e.tensor_tensor(c4, c4, rank, ALU.mult), a)
            a = V.do(lambda e: e.tensor_reduce(r2[4], c4, AX.X, ALU.max), a)
            return V.do(lambda e: e.tensor_tensor(dst, c4, bc(r2[4]), ALU.is_equal), a)

        most = sm(1)[0:1, :]
        most_i = sm(1).bitcast(I32)[0:1, :]
        pos = sm(32)

        def moe(i, tok, after):
            order = [("g", 0), ("u", 0)]
            for ex in range(1, 16):
                order += [("g", ex), ("d", ex - 1), ("u", ex)]
            order.append(("d", 15))

            def unit(kind, ex):
                w = ins[{"g": "moe_w_gate_2", "u": "moe_w_up_2", "d": "moe_w_down_2"}[kind]][i, ex]
                n = w.shape[1]
                return [(lambda a, h=h: a[:, h * 2048:h * 2048 + 2048].rearrange("p (c n) -> p c n", n=n),
                         w[h * (w.shape[0] // 2):(h + 1) * (w.shape[0] // 2), :].rearrange("(c p) n -> p c n", p=128))
                        for h in range(2)]

            assert not plan and not cutq
            for sl in slots[NSLOT - 2:]:
                sl.free = [c.free for c in cuts.places]
            mring.at = 0
            fetch([(unit(*u), True) for u in order[:NSLOT]])
            todo = list(order)

            def weights(kind, ex):
                assert todo.pop(0) == (kind, ex)
                sl, wt = stream(*unit(kind, ex), halves=True)
                return sl, wt, wview(sl, 4, 1024) if kind == "d" else wview(sl, KC, 512)

            parts, dn, cut = [], {}, [0]

            def split(eng=V):
                ex, r = divmod(cut[0], 8)
                if ex == 16:
                    return
                kind, j = "gu"[r // 4], r % 4
                cut[0] += 1
                if j == 0:
                    if kind == "u" and ex:
                        dn[ex - 1] = weights("d", ex - 1)
                    now[:] = weights(kind, ex)
                sl, wt, wv = now
                wt = wt[j // 2]
                pc = pieces.take()
                hi, lo = pc.ap
                src = wv[:, 2 * j:2 * j + 2, :]
                a = S.do(lambda e: e.copy(hi[:, :, :], src), wt, pc.free)
                k = eng.do(lambda e: e.tensor_tensor(lo[:, :, :], src, hi[:, :, :].bitcast(F32), ALU.subtract), a, wt)
                if j % 2:
                    sl.halves[j // 2].free = [k]
                parts.append((pc, k))

            now = []

            lgT = Lb.take()
            for t in range(2):
                T_xT = turn_row(t, x, hT, tok[t], "SV"[t])
                bk = work.take()
                PE.wait(bk.free, T_xT, T_small)
                for k in range(KC):
                    d = PE.do(lambda e, b=bk.ap, t=t, k=k: e.matmul(
                        b[0:20, 0:128], wge[:, i, k, :], hT[:, k, t * 128:t * 128 + 128],
                        start=(k == 0), stop=(k == KC - 1)), inc=(k == KC - 1))
                kl = S.do(lambda e, b=bk.ap, t=t: e.copy(lgT.ap[0:20, t * 128:t * 128 + 128], b[0:20, 0:128]), d, lgT.free)
                bk.free = [kl]
            for _ in range(4):
                split(G)
            gate0, cut0 = tuple(now), [k for _, k in parts]
            bk = work.take()
            PE.wait(bk.free, kl)
            for t in range(2):
                d = PE.do(lambda e, b=bk.ap, t=t: e.transpose(
                    b[:, t * 20:t * 20 + 20], lgT.ap[0:20, t * 128:t * 128 + 128], ident[0:20, 0:20]), inc=(t == 1))
            lgT.free = [d]
            a = V.do(lambda e, b=bk.ap: e.tensor_tensor(
                lg, b[:, 0:40].rearrange("p (t n) -> p t n", t=2),
                bge[:, i, :].unsqueeze(1).broadcast_to([128, 2, 20]), ALU.add), d)
            bk.free = [a]
            gmax, gs, m1, m2 = r2[0], r2[1], r2[2], r2[3]
            a = first_max(ohg, lg[:, :, 0:4], gmax, a)
            a = V.do(lambda e: e.tensor_tensor(
                pick, lg[:, :, 4:20].rearrange("p t (g j) -> p t g j", g=4),
                ohg.unsqueeze(3).broadcast_to([128, 2, 4, 4]), ALU.mult), a)
            a = V.do(lambda e: e.tensor_reduce(le, pick.rearrange("p t g j -> p t j g"), AX.X, ALU.add), a)
            a = first_max(oh1, le, m1, a)
            a = V.do(lambda e: e.scalar_tensor_tensor(le2, oh1, -BIG, le, ALU.mult, ALU.add), a)
            a = first_max(oh2, le2, m2, a)
            a = V.do(lambda e: e.tensor_tensor(oh1, oh1, oh2, ALU.add), a)
            sel = V.do(lambda e: e.tensor_tensor(
                pick, ohg.unsqueeze(3).broadcast_to([128, 2, 4, 4]), oh1.unsqueeze(2).broadcast_to([128, 2, 4, 4]),
                ALU.mult), a)

            def gates():
                V.do(lambda e: e.tensor_tensor(eg, lg[:, :, 0:4], bc(gmax), ALU.subtract))
                b1 = V.do(lambda e: e.tensor_tensor(w4, le, bc(m1), ALU.subtract))
                S.do(lambda e: e.activation(eg, eg, ACT.Exp), b1)
                e2 = S.do(lambda e: e.activation(w4, w4, ACT.Exp))
                V.do(lambda e: e.tensor_tensor(w4, w4, oh1, ALU.mult), e2)
                V.do(lambda e: e.tensor_reduce(gs, eg, AX.X, ALU.add))
                V.do(lambda e: e.tensor_reduce(m1, w4, AX.X, ALU.add))
                V.do(lambda e: e.tensor_tensor(m1, m1, gs, ALU.mult))
                V.do(lambda e: e.reciprocal(m2, m1))
                V.do(lambda e: e.tensor_tensor(w4, w4, bc(m2), ALU.mult))
                return V.do(lambda e: e.tensor_tensor(
                    gate.rearrange("p t (g j) -> p t g j", g=4), ohg.unsqueeze(3).broadcast_to([128, 2, 4, 4]),
                    w4.unsqueeze(2).broadcast_to([128, 2, 4, 4]), ALU.mult))

            bk = work.take()
            up, one = cst[:, C_UP:C_UP + 128], cst[:, C_ONE:C_ONE + 128]
            PE.wait(bk.free, sel)
            for col, rows_, l, t, first, last in ((0, 128, up, 0, True, True), (16, 128, one, 0, True, False),
                                                  (16, 128, up, 1, False, True), (32, 1, one[:, 0:1], 0, True, False),
                                                  (32, 1, one[:, 0:1], 1, False, True)):
                d = PE.do(lambda e, b=bk.ap, c=col, r=rows_, l=l, t=t, f=first, z_=last: e.matmul(
                    b[0:r, c:c + 16], l, pick[:, t, :, :].rearrange("p g j -> p (g j)"), start=f, stop=z_), inc=last)
            T_gates = gates()
            a = V.do(lambda e, b=bk.ap: e.tensor_reduce(most, b[0:1, 32:48], AX.X, ALU.max), d)
            T_most = V.do(lambda e: e.tensor_copy(most_i, most), a)
            T_pos = V.do(lambda e, b=bk.ap: e.scalar_tensor_tensor(
                pos, pick.rearrange("p t g j -> p (t g j)"), -1000.0, b[:, 0:32], ALU.mult, ALU.add), d)
            bk.free = [T_pos]

            def short():
                todo[:] = order[1:]
                ur, yb = Ring(banks[0:2]), banks[2:4]
                P4 = hT[:, :, :].rearrange("p c t -> p (c t)").rearrange("p (t e s) -> p t e s", t=2, e=16)
                Pg4 = z[:, :, :].rearrange("p t (e s) -> p t e s", e=16)
                kP = []

                def places(e0, e1):
                    n = e1 - e0
                    for t in range(2):
                        io = cst[:, C_IOTA:C_IOTA + CAP].unsqueeze(1).broadcast_to([128, n, CAP])
                        pt = pos[:, t * 16 + e0:t * 16 + e1].unsqueeze(2).broadcast_to([128, n, CAP])
                        k = V.do(lambda e, t=t, io=io, pt=pt: e.tensor_tensor(P4[:, t, e0:e1, :], io, pt, ALU.is_equal), T_pos)
                    kP.append(k)

                places(0, 2)
                got, bts_of = {}, {}

                def gather(p, hf):
                    if hf == 0:
                        got[p] = (xgs.take(), [])
                    xg, ks = got[p]
                    bk = ur.take()
                    PE.wait(bk.free, kP[0 if p == 0 else 1])
                    for c in range(4):
                        for t in range(2):
                            d = PE.do(lambda e, b=bk.ap, c=c, t=t, kc=4 * hf + c: e.matmul(
                                b[:, c * 128:c * 128 + 128], x[:, t, kc * 128:kc * 128 + 128],
                                P4[:, t, 2 * p:2 * p + 2, :].rearrange("p e s -> p (e s)"),
                                start=(t == 0), stop=(t == 1)), inc=(c == 3 and t == 1))

                    def keep():
                        v = xg.ap.rearrange("p (e k h s) -> p h k e s", e=2, k=KC, h=2)
                        b4 = bk.ap[:, :].rearrange("p (c e s) -> p c e s", c=4, e=2)
                        part = [[v[:, h, 4 * hf:4 * hf + 4, ee, :] for h in range(2)] for ee in range(2)]
                        for ee, (hi, lo) in enumerate(part):
                            k = S.do(lambda e, hi=hi, ee=ee: e.copy(hi, b4[:, :, ee, :]), d, xg.free)
                        V.wait(k)
                        for ee, (hi, lo) in enumerate(part):
                            k = V.do(lambda e, hi=hi, lo=lo, ee=ee: e.tensor_tensor(
                                lo, b4[:, :, ee, :], hi.bitcast(F32), ALU.subtract))
                        bk.free = [k]
                        ks.append(k)

                    return keep

                def way_back(p):
                    bk, bt = ur.take(), bts.take()
                    PE.wait(bk.free, kG)
                    for t in range(2):
                        d = PE.do(lambda e, b=bk.ap, t=t: e.transpose(
                            b[:, t * 128:t * 128 + 128], Pg4[:, t, 2 * p:2 * p + 2, :].rearrange("p e s -> p (e s)"),
                            ident), inc=(t == 1))
                    kb = evac(bt.ap, bk.ap[:, 0:256], [d, *bt.free], eng="S")
                    bk.free = [kb]
                    bts_of[p] = (bt, kb)

                def down(ex, hd, kh):
                    sl, wt, wv = dn.pop(ex) if ex in dn else weights("d", ex)
                    r = 64 * (ex % 2)
                    PE.wait(kh)
                    if ex % 2 == 0:
                        PE.wait(yb[0].free, yb[1].free)
                    for f in range(4):
                        PE.wait(wt[f // 2])
                        for hf in range(2):
                            d = PE.do(lambda e, hf=hf, f=f: e.matmul(
                                yb[hf].ap[r:r + 64, :], hd.ap[:, f * CAP:f * CAP + CAP], wv[:, f, hf * 512:hf * 512 + 512],
                                start=(f == 0), stop=(f == 3)), inc=(f % 2 == 1 and hf == 1))
                            if f < 3 or hf == 0:
                                yield
                        if f % 2:
                            sl.halves[f // 2].free = [d]
                    hd.free = [d]
                    if ex % 2:
                        ye = yes.take()
                        ks = []
                        for hf in range(2):
                            k = evac(ye.ap[:, hf * 512:hf * 512 + 512], yb[hf].ap[:, :], [d, *ye.free])
                            yb[hf].free = [k]
                            ks.append(k)
                        ready[ex // 2] = (ye, ks)
                    yield

                ready = {}

                def scatter(p, ye, ky, bt, kb):
                    PE.wait(ky, kb)
                    if p == 0:
                        PE.wait(*[b.free for b in acc])
                    for o in range(4):
                        t, hf = o // 2, o % 2
                        d = PE.do(lambda e, o=o, t=t, hf=hf: e.matmul(
                            acc[o].ap[:, :], bt.ap[:, t * 128:t * 128 + 128], ye.ap[:, hf * 512:hf * 512 + 512],
                            start=(p == 0), stop=(p == 7)), inc=(o == 3))
                    ye.free, bt.free = [d], [d]

                prev = None
                keep = gather(0, 0)
                keep2 = gather(0, 1)
                keep()
                keep2()
                places(2, 16)
                for t in range(2):
                    gt = gate[:, t, :].unsqueeze(2).broadcast_to([128, 16, CAP])
                    kG = G.do(lambda e, t=t, gt=gt: e.tensor_tensor(Pg4[:, t], P4[:, t], gt, ALU.mult), kP, T_gates)
                for ex in range(16):
                    p = ex // 2
                    xg, kx = got[p]
                    raw = []
                    for gv in range(2):
                        bk = ur.take()
                        PE.wait(bk.free)
                        for j in range(4):
                            pc, kp = parts.pop(0)
                            PE.wait(kp, kx[j // 2])
                            for q in range(2):
                                c0 = (ex % 2) * 1024 + (2 * j + q) * 128
                                for w in pc.ap:
                                    d = PE.do(lambda e, b=bk.ap, xg=xg.ap, c0=c0, w=w, q=q, f=(j == 0 and q == 0
                                              and w is pc.ap[0]), z_=(j == 3 and q == 1 and w is pc.ap[1]): e.matmul(
                                        b[:, :], xg[:, c0:c0 + 128], w[:, q, :], start=f, stop=z_),
                                        inc=(q == 1 and w is pc.ap[1]))
                            pc.free = [d]
                            if gv == 0 or j < (3 if ex % 2 else 1):
                                split()
                            if prev is not None:
                                for _ in range((0, 1, 1, 2, 2, 1, 1, 0)[4 * gv + j]):
                                    next(prev)
                        r = (Lb, Pb)[gv].take()
                        k = evac(r.ap[:, :], bk.ap[:, :], [d, *r.free], eng="S")
                        bk.free = [k]
                        raw.append((r, k))
                    if ex % 2:
                        xg.free = [d]
                    more = ex % 2 and p + 1 < 8
                    if more:
                        keep = gather(p + 1, 0)
                        keep()
                    elif ex % 2 == 0:
                        way_back(p)
                        if p:
                            scatter(p - 1, *ready[p - 1], *bts_of[p - 1])
                        split()
                        split()
                    split()
                    bk, hd, tm = ur.take(), hds1.take(), tms1.take()
                    PE.wait(bk.free)
                    for gv, (r, k) in enumerate(raw):
                        PE.wait(k)
                        for f in range(4):
                            d = PE.do(lambda e, b=bk.ap, o=(gv * 4 + f) * CAP, r=r.ap, f=f: e.matmul(
                                b[:, o:o + CAP], r[:, f * 128:f * 128 + 128], cst[:, C_TWO:C_TWO + CAP],
                                start=True, stop=True), inc=(f == 3))
                        r.free = [d]
                    if more:
                        keep = gather(p + 1, 1)
                    a = S.do(lambda e, b=bk.ap, t=tm.ap: e.activation(t, b[:, 0:4 * CAP], ACT.Silu), d, tm.free)
                    a = V.do(lambda e, b=bk.ap, t=tm.ap, h=hd.ap: e.tensor_tensor(
                        h, t, b[:, 4 * CAP:8 * CAP], ALU.mult), a, hd.free)
                    tm.free, bk.free = [a], [a]
                    if more:
                        keep()
                    prev = down(ex, hd, a)
                for _ in prev:
                    pass
                scatter(7, *ready[7], *bts_of[7])
                fetch([(u, False) for u in after])

            def long():
                todo[:] = order[1:]
                bk = work.take()
                PE.wait(bk.free, T_gates)
                for t in range(2):
                    d = PE.do(lambda e, b=bk.ap, t=t: e.transpose(
                        b[0:16, t * 128:t * 128 + 128], gate[:, t, :], ident), inc=(t == 1))
                T_gT = V.do(lambda e, b=bk.ap: e.tensor_copy(gT[0:16, :], b[0:16, 0:256]), d)
                bk.free = [T_gT]

                def down(ex, hd, toks_h, sl, wt, wv):
                    PE.wait(wt, *toks_h)
                    if ex == 0:
                        PE.wait(*[b.free for b in acc])
                    for f in range(4):
                        for o in range(4):
                            t, hf = o // 2, o % 2
                            d = PE.do(lambda e, o=o, t=t, hf=hf, f=f, wv=wv, hd=hd.ap: e.matmul(
                                acc[o].ap[:, :], hd[:, f * 256 + t * 128:f * 256 + t * 128 + 128],
                                wv[:, f, hf * 512:hf * 512 + 512], start=(ex == 0 and f == 0),
                                stop=(ex == 15 and f == 3)), inc=(f == 3 and o == 3))
                    sl.free = [d]
                    hd.free = [d]

                prev = None
                for ex in range(16):
                    hd = hds.take()
                    sg, gt_, wg = weights("g", ex) if ex else gate0
                    dw = weights("d", ex - 1) if ex else None
                    su, ut_, wu = weights("u", ex)
                    bk = work.take()
                    d = PE.do(lambda e, b=bk.ap, ex=ex: e.matmul(
                        b[:, 0:256], ident[0:16, ex:ex + 1].broadcast_to([16, 128]), gT[0:16, :],
                        start=True, stop=True), bk.free, T_gT)
                    gbc = gbcs.take()
                    kb = S.do(lambda e, b=bk.ap, g=gbc.ap: e.copy(g, b[:, 0:256]), d, gbc.free)
                    bk.free = [kb]
                    toks_h = []
                    for f in range(4):
                        bk = work.take()
                        PE.wait(bk.free, gt_, ut_)
                        for gv, wv in ((0, wg), (1, wu)):
                            for k in range(KC):
                                d = PE.do(lambda e, b=bk.ap, gv=gv, wv=wv, k=k, f=f: e.matmul(
                                    b[:, gv * 256:gv * 256 + 256], wv[:, k, f * 128:f * 128 + 128], hT[:, k, :],
                                    start=(k == 0), stop=(k == KC - 1)), inc=(gv == 1 and k == KC - 1))
                        tm = tms.take()
                        a = S.do(lambda e, b=bk.ap, t=tm.ap: e.activation(t, b[:, 0:256], ACT.Silu), d, tm.free)
                        a = V.do(lambda e, b=bk.ap, t=tm.ap: e.tensor_tensor(t, t, b[:, 256:512], ALU.mult), a)
                        bk.free = [a]
                        k = G.do(lambda e, t=tm.ap, g=gbc.ap, h=hd.ap, f=f: e.tensor_tensor(
                            h[:, f * 256:f * 256 + 256], t, g, ALU.mult), a, kb, hd.free)
                        tm.free = [k]
                        toks_h.append(k)
                    gbc.free = [k]
                    sg.free = su.free = [d] if ex else [d, *cut0]
                    if prev is not None:
                        down(*prev, *dw)
                    prev = (ex, hd, toks_h)
                down(*prev, *weights("d", 15))
                fetch([(u, False) for u in after])

            ends = fork(most_i, T_most, short, long)
            res = []
            for t in range(2):
                for hf in range(2):
                    acc[2 * t + hf].free = [add_stats(t, hf, acc[2 * t + hf].ap, ends)]
                res.append(ln_row(t, i, 1))
            if i == 0:
                ln_load(1, 0)
            return res

        T_y.clear()
        T_xT = turn(x, (hTr, yTr), [T_x3[0:2], T_x3[2:4]])
        ar_at[0] = 0
        NP = 2600
        pj = ar(2 * NP).rearrange("p (t n) -> p t n", t=2)
        qT2 = ar(6 * T).rearrange("p (c t) -> p c t", c=6)
        xqT = ar(2 * T).rearrange("p (c t) -> p c t", c=2)
        ksT = ar(5 * T).rearrange("p (c t) -> p c t", c=5)
        kwT = ar(5 * T).rearrange("p (c t) -> p c t", c=5)
        kvf = ar(4 * T)
        kvX = [a[:, 0:5, :] for a in (hT, yT)]
        PcT = [z[:, h // 4, (h % 4) * T:(h % 4) * T + T] if h < 8 else kvf[:, (h - 8) * T:(h - 7) * T] for h in range(12)]
        PcT2 = [z[:, c // 2, (c % 2) * 512:(c % 2) * 512 + 512].rearrange("p (h t) -> p h t", h=2) if c < 4
                else kvf[:, (c - 4) * 512:(c - 3) * 512].rearrange("p (h t) -> p h t", h=2) for c in range(6)]
        tmp4 = [sm(96) for _ in range(4)]
        pv = []

        T_ar = T_x3
        for c in range(6):
            n = 512 if c < 5 else 36

            def keep_pj(t, b, tok, c=c, n=n):
                k = evac(pj[:, t, c * 512:c * 512 + n], b[:, 0:n], [tok, *T_ar])
                pv.append(k)
                return k

            tok3((hTr, yTr), T_xT, n, keep_pj)
        T_kc = []
        for kv in range(2):
            X, done = kvX[kv], []
            done.append(G.do(lambda e, X=X: e.memset(X[:, 4, :], 0.0), pv))
            done.append(G.do(lambda e, X=X, kv=kv: e.tensor_copy(X[:, 4, 0:32:2], peT[:, kv * 16:kv * 16 + 16]), T_peT))
            for c in range(0, 5, 2):
                bk = work.take()
                PE.wait(bk.free, pv)
                m = min(2, 5 - c)
                for q in range(2 * m):
                    c0 = 704 + kv * 256 + (c + q // 2) * 64
                    d = PE.do(lambda e, b=bk.ap, q=q, c0=c0: e.transpose(
                        b[:, q * 128:q * 128 + 128], pj[:, q % 2, c0:c0 + 128], ident), inc=(q == 2 * m - 1))
                w = bk.ap[:, 0:m * 256].rearrange("p (c t) -> p c t", c=m)
                lo = 1 if c == 0 else 0
                k = S.do(lambda e, X=X, c=c, m=m, w=w, lo=lo: e.copy(X[0:64, c + lo - 1:c + m - 1, :], w[0:64, lo:m, :]), d)
                if c < 4:
                    k = S.do(lambda e, X=X, c=c, w=w: e.copy(X[64:128, c:c + 2, 0:T - 1], w[64:128, :, 1:T]))
                bk.free = [k]
                done.append(k)
            done.append(G.do(lambda e, X=X: e.memset(X[64:128, 0:4, T - 1:T], 0.0)))
            T_kc.append(done)
        for t in range(2):
            h12 = pj[:, t, 0:768].rearrange("p (h d) -> p h d", h=12)
            tq = [a.rearrange("p (h d) -> p h d", h=12) for a in tmp4]
            k = rope(h12[:, :, 0:8], h12[:, :, 8:16], t, 0, 8, [12], tq, [*pv, d])
            for b0 in (1280, 1792):
                h4 = pj[:, t, b0:b0 + 256].rearrange("p (h d) -> p h d", h=4)
                tk = [a[:, 0:32].rearrange("p (h d) -> p h d", h=4) for a in tmp4]
                k = rope(h4[:, :, 0:8], h4[:, :, 8:16], t, 0, 8, [4], tk, None)
        sgt = sm(72).rearrange("p (t n) -> p t n", t=2)
        T_gate = S.do(lambda e: e.activation(sgt, pj[:, :, 2304:2340], ACT.Sigmoid), pv)
        hs = sm(2)
        hid = sm(120).rearrange("p (k n) -> p k n", k=2)
        kcp = ar(384)
        kcm = [kcp[:, 64:320].rearrange("p (h d) -> p h d", h=4), ar(256).rearrange("p (h d) -> p h d", h=4)]
        kcB = sm(180).rearrange("p (a c q n) -> p a c q n", a=2, c=3, q=2)
        T_zero = G.do(lambda e: e.memset(kcB, 0.0), T_ar)
        T_pad = [G.do(lambda e, a=a: e.memset(kcp[:, a:a + 64], 0.0), T_ar) for a in (0, 320)]
        T_cm = []
        sl, wt = stream(*[(lambda a, kv=kv: a[:, kv * 2048:kv * 2048 + 2048].rearrange("p (c h) -> p c h", c=16),
                           ins["nsa_cmp_w1_2"][0, kv].rearrange("(c p) h -> p c h", p=128)) for kv in range(2)])
        for kv in range(2):
            wv = sl.ap[:, kv * 2048:kv * 2048 + 2048].rearrange("p (c h) -> p c h", c=16)
            bk = work.take()
            PE.wait(wt, T_kc[kv], bk.free)
            for c in range(16):
                d = PE.do(lambda e, b=bk.ap, c=c, kv=kv, wv=wv: e.matmul(
                    b[:, 0:75].rearrange("p (h n) -> p h n", h=5), wv[:, c, :], kvX[kv][:, :, 2 * c:2 * c + 225:16],
                    start=(c == 0), stop=(c == 15)), inc=(c == 15))
            if kv == 1:
                sl.free = [d]
            S.do(lambda e, b=bk.ap, kv=kv: e.copy(hs[:, kv:kv + 1], b[:, 60:61]), d)
            a = S.do(lambda e, b=bk.ap, kv=kv: e.activation(hid[:, kv, :], b[:, 0:60], ACT.Silu, bias=hs[:, kv:kv + 1]))
            bk.free = [a]
            bk = work.take()
            PE.wait(a, bk.free, T_small)
            for h in range(4):
                d = PE.do(lambda e, b=bk.ap, h=h, kv=kv: e.matmul(
                    b[0:NCMP, h * 64:h * 64 + 64], hid[:, kv, h * 15:h * 15 + 15], w2c[:, kv, :],
                    start=True, stop=True), inc=(h == 3))
            a = S.do(lambda e, b=bk.ap, kv=kv: e.copy(
                kcm[kv][0:NCMP, :, :], b[0:NCMP, 0:256].rearrange("p (h d) -> p h d", h=4)), d)
            bk.free = [a]
            T_cm.append(a)
        T_q = turn_cols(pj, 0, 6, qT2, k, -0.125)
        tk = [a[0:NCMP, 0:32].rearrange("p (h d) -> p h d", h=4) for a in tmp4]
        a = rope(kcm[0][0:NCMP, :, 0:8], kcm[0][0:NCMP, :, 8:16], 2, 0, 8, [4], tk, T_cm, NCMP)
        bk = work.take()
        PE.wait(bk.free, a, T_pad)
        for h in range(5):
            d = PE.do(lambda e, b=bk.ap, h=h: e.transpose(
                b[:, h * 15:h * 15 + 15], kcp[0:NCMP, h * 64:h * 64 + 128], ident[0:NCMP, 0:NCMP]), inc=(h == 4))
        T_kcT = []
        for q in range(2):
            w4_ = bk.ap[64 * q:64 * q + 64, 0:75].rearrange("p (h n) -> p h n", h=5)
            for c in range(3):
                h = (2 * c + q) // 3 + 1 - q
                T_kcT.append(V.do(lambda e, q=q, c=c, h=h, w=w4_: e.tensor_copy(
                    kcB[64 * q:64 * q + 64, :, c, q, :], w[:, h:h + 3:2, :]), d, T_zero))
        T_kcT = T_kcT[-1]
        bk.free = [T_kcT]

        pc = [ar(180).rearrange("p (h n) -> p h n", h=12) for _ in range(2)]
        T_pc, T_ex, cms = [], [], [sm(48).rearrange("p (q h) -> p q h", q=4)] * 2
        for t in range(2):
            bk = work.take()
            PE.wait(bk.free, T_q, T_kcT)
            for c in range(6):
                d = PE.do(lambda e, b=bk.ap, c=c, t=t: e.matmul(
                    b[:, c * 30:c * 30 + 30], qT2[:, c, t * 128:t * 128 + 128],
                    kcB[:, c // 3, c % 3, :, :].rearrange("p q n -> p (q n)"), start=True, stop=True), inc=(c == 5))
            p3, cm = pc[t], cms[t]
            a = V.do(lambda e, b=bk.ap, p3=p3, t=t: e.scalar_tensor_tensor(
                p3, b[:, 0:180].rearrange("p (h n) -> p h n", h=12), -1.0,
                cbias[:, t, :].unsqueeze(1).broadcast_to([128, 12, NCMP]), ALU.mult, ALU.add), d, T_cb)
            bk.free = [a]
            a = V.do(lambda e, cm=cm, p3=p3: e.tensor_reduce(cm[:, 0, :], p3, AX.X, ALU.max), a)
            a = V.do(lambda e, cm=cm, p3=p3: e.tensor_tensor(
                p3, p3, cm[:, 0, :].unsqueeze(2).broadcast_to([128, 12, NCMP]), ALU.subtract), a)
            a = S.do(lambda e, cm=cm, p3=p3: e.activation(p3, p3, ACT.Exp), a)
            T_ex.append(a)
        T_ks = turn_cols(pj, 1280 - 64, 5, ksT, k, None, 64, "S")
        T_kw = turn_cols(pj, 1792 - 64, 5, kwT, k, None, 64, "S")
        T_xq = turn_cols(pj, 2340, 2, xqT, pv, -0.125, eng="S")
        for t in range(2):
            p3, cm = pc[t], cms[t]
            okb = cok[:, t, :].unsqueeze(1).broadcast_to([128, 12, NCMP])
            a = V.do(lambda e, cm=cm, p3=p3, okb=okb: e.tensor_tensor(p3, p3, okb, ALU.mult), T_ex[t])
            a = V.do(lambda e, cm=cm, p3=p3: e.tensor_reduce(cm[:, 1, :], p3, AX.X, ALU.add), a)
            a = V.do(lambda e, cm=cm: e.tensor_scalar(cm[:, 1, :], cm[:, 1, :], 1e-30, None, ALU.max), a)
            a = V.do(lambda e, cm=cm: e.reciprocal(cm[:, 2, :], cm[:, 1, :]), a)
            g3 = sgt[:, t, :].rearrange("p (h b) -> p h b", b=3)
            a = V.do(lambda e, cm=cm, g3=g3: e.tensor_tensor(cm[:, 3, :], cm[:, 2, :], g3[:, :, 0], ALU.mult), a, T_gate)
            a = V.do(lambda e, cm=cm, p3=p3: e.tensor_tensor(
                p3, p3, cm[:, 3, :].unsqueeze(2).broadcast_to([128, 12, NCMP]), ALU.mult), a)
            T_pc.append(a)
        for c in range(6):
            bk = work.take()
            PE.wait(bk.free, T_pc)
            for q in range(4):
                h, t = 2 * c + q // 2, q % 2
                d = PE.do(lambda e, b=bk.ap, q=q, h=h, t=t: e.transpose(
                    b[0:NCMP, q * 128:q * 128 + 128], pc[t][:, h, :], ident), inc=(q == 3))
            T_PcT = evac(PcT2[c][0:NCMP, :, :],
                         bk.ap[0:NCMP, :].rearrange("p (h t) -> p h t", h=2), d)
            bk.free = [T_PcT]
            pv.append(T_PcT)

        def nsa(h, t):
            mk, w = msk(t)
            r, c, kv = 64 * (h % 2), h // 2, h // 3
            q = qT2[r:r + 64, c, t * 128:t * 128 + 128]
            return dict(
                S=[(q, ksT[r:r + 64, kv + 1 - h % 2, 0:w], w, mk, sgt[:, t, 3 * h + 1:3 * h + 2]),
                   (q, kwT[r:r + 64, kv + 1 - h % 2, 0:w], w, mk, sgt[:, t, 3 * h + 2:3 * h + 3])],
                v=[[pj[:, s, 1536 + kv * 64:1536 + kv * 64 + 64] for s in range(2)],
                   [pj[:, s, 2048 + kv * 64:2048 + kv * 64 + 64] for s in range(2)]],
                extra=[(kcm[1][0:NCMP, kv, :], PcT[h][0:NCMP, t * 128:t * 128 + 128])])

        def mix_out(p, b, tok):
            k = evac2([yTr[:, p, :], hTr[:, p, :]], b[:, 0:256], tok)
            T_y.append(k)
            return k

        V.wait(T_gate)
        attention(pair_jobs(12, nsa), [*T_q, *T_ks, *T_kw, *pv, *T_cm, *T_kc], mix_out)
        cross(0, xqT, T_xq)

        def join(i):
            def use(t, hf, b, tok):
                return add_stats(t, hf, b, tok)
            res = []
            out_proj((yTr, hTr), list(T_y), use, lambda t: res.append(ln_row(t, i, 0)))
            ln_load(i, 1)
            return res

        T_xa = join(0)
        T_mixed = list(T_xa)

        ar_at[0] = 0
        hds = Ring([Place(ar(1024)) for _ in range(2)])
        gbcs = Ring([Place(ar(256)) for _ in range(2)])
        tms = Ring([Place(ar(256)) for _ in range(3)])
        gT = ar(256)
        xgs = Ring([Place(a[:, :]) for a in xgr])
        pieces = Ring([Place(a) for a in zip(whr, wlr)])
        yes = Ring([Place(yT[:, 4 * i:4 * i + 4, :].rearrange("p c t -> p (c t)")) for i in range(2)])
        six = [Place(t.ap[:, h:h + 256]) for t in Tb.places for h in (0, 256)]
        bts, hds1, tms1 = Ring(six[0:3]), Ring(six[3:5]), Ring(six[5:6])
        w_m = ins["mla_w_in_2"][0]
        u_uq = (lambda a: a[:, 0:2304].rearrange("p (c n) -> p c n", c=2),
                ins["mla_w_uq_2"][0].rearrange("(c p) n -> p c n", p=128))
        u_ukv = (lambda a: a[:, 0:1536], ins["mla_w_ukv_2"][0])
        T_xb = moe(0, T_xa, [[cols(w_m, KC, 0, 512)], [cols(w_m, KC, 512, 160)], [cols(ins["w_out_2"][1], KC, 0, 512)]])

        T_y.clear()
        start([by_cols(w_m, 0, 512), by_cols(w_m, 512, 160)] + [by_cols(ins["w_out_2"][1], n0, 512) for n0 in (0, 512)], 2)
        T_xT = turn(x, (hTr, yTr), T_xb)
        refill()
        ar_at[0] = 0
        pm = ar(2 * 672).rearrange("p (t n) -> p t n", t=2)
        cqT = ar(2 * T).rearrange("p (c t) -> p c t", c=2)
        ckT = ar(T).rearrange("p (c t) -> p c t", c=1)
        xqT2 = ar(2 * T).rearrange("p (c t) -> p c t", c=2)
        hf_ = hT[:, :, :].rearrange("p c t -> p (c t)")
        qks = [Ring([Place(a.rearrange("p (t h d) -> p t h d", t=2, h=4)) for a in (ar(768), hf_[:, k * 768:k * 768 + 768])])
               for k in range(2)]
        trq = [ar(64).rearrange("p (h d) -> p h d", h=4) for _ in range(4)]
        vm = ar(2 * 768).rearrange("p (t h d) -> p t h d", t=2, h=12)
        qT3 = ar(12 * T).rearrange("p (h t) -> p h t", h=12)
        kT3 = ar(12 * T).rearrange("p (h t) -> p h t", h=12)
        assert ar_at[0] <= 12360
        pv2 = []
        for n0, n in ((0, 512), (512, 160)):
            def keep_pm(t, b, tok, n0=n0, n=n):
                k = evac(pm[:, t, n0:n0 + n], b[:, 0:n], [tok, *T_xb])
                pv2.append(k)
                return k
            tok3((hTr, yTr), T_xT, n, keep_pm)
        sqm = sm(4).rearrange("p (n t) -> p n t", n=2)
        rsm = sm(4).rearrange("p (n t) -> p n t", n=2)
        jk = Lb.take()
        S.wait(jk.free)
        for t in range(2):
            for n, (c0, w) in enumerate(((0, 256), (256, 128))):
                a = S.do(lambda e, t=t, n=n, c0=c0, w=w: e.activation(
                    jk.ap[:, 0:w], pm[:, t, c0:c0 + w], ACT.Square, accum_out=sqm[:, n, t:t + 1]), pv2)
        jk.free = [a]
        r0 = rsqrt(rsm[:, 0, :], sqm[:, 0, :], 1e-6, 1.0 / 256, a)
        r1 = rsqrt(rsm[:, 1, :], sqm[:, 1, :], 1e-6, 1.0 / 128, a)
        for t in range(2):
            V.do(lambda e, t=t: e.tensor_scalar(pm[:, t, 0:256], pm[:, t, 0:256], rsm[:, 0, t:t + 1], None, ALU.mult), r0)
            kn = V.do(lambda e, t=t: e.tensor_scalar(pm[:, t, 256:384], pm[:, t, 256:384], rsm[:, 1, t:t + 1], None,
                                                     ALU.mult), r1)
        tr = [tmp4[i][:, 0:16] for i in range(4)]
        for t in range(2):
            kr = rope(pm[:, t, 384:400], pm[:, t, 400:416], t, 8, 24, [], tr, pv2)
        T_xq2 = turn_cols(pm, 416, 2, xqT2, pv2, -0.125)
        T_cq = []
        bk = work.take()
        PE.wait(bk.free, kn)
        for q in range(4):
            d = PE.do(lambda e, b=bk.ap, q=q: e.transpose(
                b[:, q * 128:q * 128 + 128], pm[:, q % 2, (q // 2) * 128:(q // 2) * 128 + 128], ident), inc=(q == 3))
        for c in range(2):
            k = V.do(lambda e, b=bk.ap, c=c: e.tensor_scalar(
                cqT[:, c, :], b[:, c * 256:c * 256 + 256], colv[:, QN + c:QN + c + 1], None, ALU.mult), d)
        bk.free = [k]
        T_cq.append(k)
        bk = work.take()
        PE.wait(bk.free)
        for q in range(2):
            d = PE.do(lambda e, b=bk.ap, q=q: e.transpose(
                b[:, q * 128:q * 128 + 128], pm[:, q, 256:384], ident), inc=(q == 1))
        k = V.do(lambda e, b=bk.ap: e.tensor_scalar(
            ckT[:, 0, :], b[:, 0:256], colv[:, KN:KN + 1], None, ALU.mult), d)
        bk.free = [k]
        T_ck = [k]

        slq, qt_ = stream(u_uq)
        slk, kt_ = stream(u_ukv)
        wq_, wk_ = wview(slq, 2, 1152), slk.ap[:, 0:1536]
        T_q3 = []
        def mla_project(piece, kind):
            qk = qks[kind].take()
            kt2 = []
            for t in range(2):
                bk = work.take()
                if kind == 0:
                    PE.wait(bk.free, qt_, T_cq)
                    for k in range(2):
                        d = PE.do(lambda e, b=bk.ap, k=k, t=t, p=piece: e.matmul(
                            b[:, 0:384], cqT[:, k, t * 128:t * 128 + 128], wq_[:, k, p * 384:p * 384 + 384],
                            start=(k == 0), stop=(k == 1)), inc=(k == 1))
                    slq.free = [d]
                    a = evac(qk.ap[:, t, :, :], bk.ap[:, 0:384].rearrange("p (h d) -> p h d", h=4), [d, *qk.free])
                    bk.free = [a]
                    a = rope(qk.ap[:, t, :, 64:80], qk.ap[:, t, :, 80:96], t, 8, 24, [4],
                             trq, a)
                    kt2.append(a)
                else:
                    d = PE.do(lambda e, b=bk.ap, t=t, p=piece: e.matmul(
                        b[:, :], ckT[:, 0, t * 128:t * 128 + 128], wk_[:, p * 512:p * 512 + 512],
                        start=True, stop=True), bk.free, kt_, T_ck)
                    slk.free = [d]
                    b4 = bk.ap[:, :].rearrange("p (h d) -> p h d", h=4)
                    a1 = S.do(lambda e, b4=b4, t=t, qk=qk: e.copy(qk.ap[:, t, :, 0:64], b4[:, :, 0:64]), d, qk.free)
                    a2 = S.do(lambda e, b4=b4, t=t, p=piece: e.copy(vm[:, t, 4 * p:4 * p + 4, :], b4[:, :, 64:128]))
                    bk.free = [a2]
                    a3 = G.do(lambda e, t=t, qk=qk: e.tensor_copy(
                        qk.ap[:, t, :, 64:96], pm[:, t, 384:416].unsqueeze(1).broadcast_to([128, 4, 32])),
                        kr, qk.free)
                    kt2 += [a2, a3]
                    T_q3.append(a2)
            return qk, kt2

        def mla_turn(piece, kind, qk, kt2):
            dst = qT3 if kind == 0 else kT3
            for hh in range(2):
                bk = work.take()
                PE.wait(bk.free, kt2)
                for q in range(4):
                    h, t = 2 * hh + q // 2, q % 2
                    d = PE.do(lambda e, b=bk.ap, q=q, h=h, t=t, qk=qk: e.transpose(
                        b[0:96, q * 128:q * 128 + 128], qk.ap[:, t, h, :], ident), inc=(q == 3))
                h0 = 4 * piece + 2 * hh
                a = evac(dst[0:96, h0:h0 + 2, :], bk.ap[0:96, :].rearrange("p (h t) -> p h t", h=2), d,
                         -float(96.0 ** -0.5) if kind == 0 else None)
                bk.free = [a]
                T_q3.append(a)
            qk.free = [d]

        waiting = []
        for piece in range(3):
            for kind in range(2):
                waiting.append((piece, kind, *mla_project(piece, kind)))
                if len(waiting) > 2:
                    mla_turn(*waiting.pop(0))
        for w in waiting:
            mla_turn(*w)

        def mla(h, t):
            mk, w = msk(t)
            return dict(S=[(qT3[0:96, h, t * 128:t * 128 + 128], kT3[0:96, h, 0:w], w, mk, None)],
                        v=[[vm[:, s, h, :] for s in range(2)]])

        attention(pair_jobs(12, mla), T_q3, mix_out)
        cross(1, xqT2, T_xq2)
        T_xa = join(1)
        T_mixed = list(T_xa)
        T_fin = moe(1, T_xa, [])

        for t in range(2):
            SP.dma(lambda e, t=t: e.dma_start(out[0, t * 128:t * 128 + 128, :], x[:, t, :]), s_out, T_fin[t])
        SP.wait((s_out, 32))

        block = ctx.enter_context(nc.Block())

        @block.sync
        def _(e):
            SP.emit(e)

        @block.tensor
        def _(e):
            PE.emit(e)

        @block.vector
        def _(e):
            V.emit(e)

        @block.scalar
        def _(e):
            S.emit(e)

        @block.gpsimd
        def _(e):
            G.emit(e)


_INS = ["x", "p", "rel_bias", "g_mix_pre", "g_mix_post", "g_ffn_pre", "g_ffn_post", "w_in", "w_pool", "pool_scale",
        "w_out", "w_up", "conv_w", "conv_b", "w_down", "w_ple", "w_ple_gate", "mem_2", "positions_2", "nsa_w_in_2",
        "nsa_cmp_pe_2", "nsa_cmp_w1_2", "nsa_cmp_w2_2", "mla_w_in_2", "mla_q_norm_2", "mla_w_uq_2",
        "mla_kv_norm_2", "mla_w_ukv_2", "mem_w_kv_2", "w_out_2", "ln_g_2", "ln_b_2", "moe_w_grp_2", "moe_b_grp_2",
        "moe_w_exp_2", "moe_b_exp_2", "moe_w_gate_2", "moe_w_up_2", "moe_w_down_2"]


def kernel(**inputs):
    import numpy as _np
    import concourse.bacc as _bacc
    from concourse import mybir as _mybir
    from concourse.bass_utils import run_bass_kernel_spmd as _run

    nc = _bacc.Bacc("TRN2", target_bir_lowering=False, num_devices=1)
    arrays, args = {}, {}

    def give(name, a):
        arrays[name] = a
        return nc.dram_tensor(name, a.shape, _mybir.dt.from_np(a.dtype), kind="ExternalInput").ap()

    for name in _INS:
        args[name] = give(f"in_{name}", _np.ascontiguousarray(inputs[name]))
    cst, onehot = constants()
    cst_d, oh_d = give("const_rows", cst), give("const_onehot", onehot)
    scratch = nc.dram_tensor("bias_rows", (8, 384), F32, kind="Internal").ap()
    out = nc.dram_tensor("out", (1, T, D), F32, kind="ExternalOutput").ap()
    build(nc, args, out, cst_d, oh_d, scratch)
    r = _run(nc, [arrays], core_ids=[0])
    return r.results[0]["out"]
```
